# Optimizing a Trainium2 kernel written in Bass

```python
import math
import jax, jax.numpy as jnp
from jax import lax
import numpy as np

D_MODEL = 1024
BATCH = 1
SEQ = 2048
DEPTH = 1

CHUNK = 64
MIX_WIDTH = D_MODEL
SSM_WIDTH = MIX_WIDTH // 2
POOL_WIDTH = MIX_WIDTH - SSM_WIDTH
SSM_GROUP = 16
SSM_GROUPS = SSM_WIDTH // SSM_GROUP
SSM_STATE = 64
POOL_WINDOWS = (2, 4, 8, 16)
POOL_GROUPS = len(POOL_WINDOWS)
POOL_GROUP_WIDTH = POOL_WIDTH // POOL_GROUPS
D_FF = ((8 * D_MODEL // 3 + 255) // 256) * 256
CONV_WIDTH = 3
N_MOD = 6
EPS = 1e-6
DT_MIN = 1e-3
DT_MAX = 1e-1

kernel_name = "hymba_s5_pool_convffn_block"

def rms_norm(x, g):
    xf = x.astype(jnp.float32)
    y = xf * lax.rsqrt(jnp.mean(xf * xf, axis=-1, keepdims=True) + EPS)
    return (y * g.astype(jnp.float32)).astype(x.dtype)

def modulate(h, shift, scale):
    return h * (1 + scale[:, None, :]) + shift[:, None, :]

def s5_mixer(u, lam_re, lam_im, log_dt, b_re, b_im, c_re, c_im, d_skip):
    f32 = jnp.float32
    bsz, seq, _ = u.shape
    n_chunks = seq // CHUNK
    lam = lax.complex(lam_re.astype(f32), lam_im.astype(f32))
    dt = jnp.exp(log_dt.astype(f32))[:, None]
    lam_bar = jnp.exp(lam * dt)
    b_mat = lax.complex(b_re.astype(f32), b_im.astype(f32))
    b_bar = ((lam_bar - 1) / lam)[..., None] * b_mat
    c_mat = lax.complex(c_re.astype(f32), c_im.astype(f32))
    d = d_skip.astype(f32).reshape(SSM_GROUPS, SSM_GROUP)
    u_chunks = u.astype(f32).reshape(bsz, n_chunks, CHUNK, SSM_GROUPS, SSM_GROUP)
    u_chunks = u_chunks.transpose(1, 0, 2, 3, 4)

    def combine(e1, e2):
        a1, b1 = e1
        a2, b2 = e2
        return a1 * a2, a2 * b1 + b2

    def chunk_step(state, u_c):
        bu = jnp.einsum('bcgh,gph->bcgp', u_c.astype(jnp.complex64), b_bar)
        bu = bu.at[:, 0].add(lam_bar * state)
        a = jnp.broadcast_to(lam_bar, bu.shape)
        _, xs = lax.associative_scan(combine, (a, bu), axis=1)
        y = jnp.einsum('bcgp,ghp->bcgh', xs, c_mat).real + d * u_c
        return xs[:, -1], y

    state0 = jnp.zeros((bsz, SSM_GROUPS, SSM_STATE), jnp.complex64)
    _, ys = lax.scan(chunk_step, state0, u_chunks)
    return ys.transpose(1, 0, 2, 3, 4).reshape(bsz, seq, SSM_WIDTH)

def multiscale_pool(p, w_pool, b_pool, pool_scale):
    f32 = jnp.float32
    bsz, seq, _ = p.shape
    pf = p.astype(f32)
    cs = jnp.concatenate([jnp.zeros((bsz, 1, POOL_WIDTH), f32), jnp.cumsum(pf, axis=1)], axis=1)
    pos = jnp.arange(1, seq + 1, dtype=f32)[None, :, None]
    pooled = []
    for gi, w in enumerate(POOL_WINDOWS):
        sl = slice(gi * POOL_GROUP_WIDTH, (gi + 1) * POOL_GROUP_WIDTH)
        cs_g = cs[:, :, sl]
        lagged = jnp.concatenate(
            [jnp.zeros((bsz, w - 1, POOL_GROUP_WIDTH), f32), cs_g[:, :seq + 1 - w]], axis=1)
        mean = (cs_g[:, 1:] - lagged) / jnp.minimum(pos, float(w))
        pooled.append(mean - pf[:, :, sl])
    z = jnp.stack(pooled, axis=2)
    z = jnp.einsum('blgc,gcd->blgd', z, w_pool) + b_pool
    return z.reshape(bsz, seq, POOL_WIDTH) * pool_scale

def causal_dwconv(h, w, b):
    ch = h.shape[-1]
    y = lax.conv_general_dilated(
        h, w[:, None, :].astype(h.dtype), window_strides=(1,),
        padding=[(CONV_WIDTH - 1, 0)], dimension_numbers=('NWC', 'WIO', 'NWC'),
        feature_group_count=ch)
    return y + b

def hybrid_layer(x, c, w_ada, b_ada, g_norm_mix, w_in, ssm_lam_re, ssm_lam_im, ssm_log_dt,
                 ssm_b_re, ssm_b_im, ssm_c_re, ssm_c_im, ssm_d, w_glu, b_glu, w_pool, b_pool,
                 pool_scale, w_out, g_norm_ffn, w_up, w_conv, b_conv, w_down):
    mod = jax.nn.silu(c) @ w_ada + b_ada
    sh1, sc1, gt1, sh2, sc2, gt2 = jnp.split(mod, N_MOD, axis=-1)

    h = modulate(rms_norm(x, g_norm_mix), sh1, sc1)
    z_in = h @ w_in
    u, p = z_in[..., :SSM_WIDTH], z_in[..., SSM_WIDTH:]
    y = jax.nn.gelu(s5_mixer(u, ssm_lam_re, ssm_lam_im, ssm_log_dt, ssm_b_re, ssm_b_im,
                             ssm_c_re, ssm_c_im, ssm_d))
    val, gate = jnp.split(y @ w_glu + b_glu, 2, axis=-1)
    y_ssm = val * jax.nn.sigmoid(gate)
    y_pool = multiscale_pool(p, w_pool, b_pool, pool_scale)
    mixed = jnp.concatenate([y_ssm, y_pool], axis=-1) @ w_out
    x = x + gt1[:, None, :] * mixed

    h = modulate(rms_norm(x, g_norm_ffn), sh2, sc2)
    v, g = jnp.split(h @ w_up, 2, axis=-1)
    g = causal_dwconv(g, w_conv, b_conv)
    x = x + gt2[:, None, :] * ((jax.nn.silu(g) * v) @ w_down)
    return x

def setup_inputs(seed: int = 0) -> dict:
    key = jax.random.key(seed)
    ks = jax.random.split(key, 32)

    def nrm(k, shape, scale):
        return jax.random.normal(k, shape, jnp.float32) * scale

    L = DEPTH
    G, P, H = SSM_GROUPS, SSM_STATE, SSM_GROUP
    n_idx = jnp.arange(P, dtype=jnp.float32)
    return {
        "x": nrm(ks[0], (BATCH, SEQ, D_MODEL), 1.0),
        "c": nrm(ks[1], (BATCH, D_MODEL), 1.0),
        "w_ada": nrm(ks[2], (L, D_MODEL, N_MOD * D_MODEL), D_MODEL ** -0.5),
        "b_ada": nrm(ks[3], (L, N_MOD * D_MODEL), 0.02),
        "g_norm_mix": 1.0 + nrm(ks[4], (L, D_MODEL), 0.02),
        "w_in": nrm(ks[5], (L, D_MODEL, MIX_WIDTH), D_MODEL ** -0.5),
        "ssm_lam_re": -0.5 + nrm(ks[6], (L, G, P), 0.01),
        "ssm_lam_im": math.pi * n_idx + nrm(ks[7], (L, G, P), 0.01),
        "ssm_log_dt": jax.random.uniform(ks[8], (L, G), jnp.float32,
                                         math.log(DT_MIN), math.log(DT_MAX)),
        "ssm_b_re": nrm(ks[9], (L, G, P, H), (2 * H) ** -0.5),
        "ssm_b_im": nrm(ks[10], (L, G, P, H), (2 * H) ** -0.5),
        "ssm_c_re": nrm(ks[11], (L, G, H, P), (2 * P) ** -0.5 * 4.0),
        "ssm_c_im": nrm(ks[12], (L, G, H, P), (2 * P) ** -0.5 * 4.0),
        "ssm_d": nrm(ks[13], (L, SSM_WIDTH), 1.0),
        "w_glu": nrm(ks[14], (L, SSM_WIDTH, 2 * SSM_WIDTH), SSM_WIDTH ** -0.5),
        "b_glu": nrm(ks[15], (L, 2 * SSM_WIDTH), 0.02),
        "w_pool": nrm(ks[16], (L, POOL_GROUPS, POOL_GROUP_WIDTH, POOL_GROUP_WIDTH),
                      POOL_GROUP_WIDTH ** -0.5),
        "b_pool": nrm(ks[17], (L, POOL_GROUPS, POOL_GROUP_WIDTH), 0.02),
        "pool_scale": 1.0 + nrm(ks[18], (L, POOL_WIDTH), 0.1),
        "w_out": nrm(ks[19], (L, MIX_WIDTH, D_MODEL), MIX_WIDTH ** -0.5),
        "g_norm_ffn": 1.0 + nrm(ks[20], (L, D_MODEL), 0.02),
        "w_up": nrm(ks[21], (L, D_MODEL, 2 * D_FF), D_MODEL ** -0.5),
        "w_conv": nrm(ks[22], (L, CONV_WIDTH, D_FF), CONV_WIDTH ** -0.5),
        "b_conv": nrm(ks[23], (L, D_FF), 0.02),
        "w_down": nrm(ks[24], (L, D_FF, D_MODEL), D_FF ** -0.5),
        "g_norm_final": 1.0 + nrm(ks[25], (D_MODEL,), 0.02),
    }

def reference(x, c, w_ada, b_ada, g_norm_mix, w_in, ssm_lam_re, ssm_lam_im, ssm_log_dt,
              ssm_b_re, ssm_b_im, ssm_c_re, ssm_c_im, ssm_d, w_glu, b_glu, w_pool, b_pool,
              pool_scale, w_out, g_norm_ffn, w_up, w_conv, b_conv, w_down, g_norm_final):
    for l in range(DEPTH):
        x = hybrid_layer(x, c, w_ada[l], b_ada[l], g_norm_mix[l], w_in[l], ssm_lam_re[l],
                         ssm_lam_im[l], ssm_log_dt[l], ssm_b_re[l], ssm_b_im[l], ssm_c_re[l],
                         ssm_c_im[l], ssm_d[l], w_glu[l], b_glu[l], w_pool[l], b_pool[l],
                         pool_scale[l], w_out[l], g_norm_ffn[l], w_up[l], w_conv[l],
                         b_conv[l], w_down[l])
    return rms_norm(x, g_norm_final)


_drawn_inputs = setup_inputs


def setup_inputs(seed=0):
    import zlib

    import numpy as np

    out = dict(_drawn_inputs(seed))
    spreads = {}
    factors = {'g_norm_mix': 6.071,
     'ssm_lam_re': 8.0,
     'b_glu': 8.0,
     'b_pool': 7.339,
     'g_norm_ffn': 4.52,
     'b_conv': 7.508,
     'g_norm_final': 2.798}
    for name, (base, spread) in spreads.items():
        noise = np.random.default_rng([zlib.crc32(name.encode()), seed]).standard_normal(out[name].shape)
        drawn = base * np.exp(spread * noise) if base else spread * noise
        out[name] = __import__('jax').numpy.asarray(drawn.astype(out[name].dtype))
    for name, factor in factors.items():
        out[name] = (out[name] * factor).astype(out[name].dtype)
    return out
```

```python
import math
from contextlib import ExitStack

import numpy as np

import concourse.bass as bass
from concourse import mybir

F32 = mybir.dt.float32
F32R = mybir.dt.float32r
BF16 = mybir.dt.bfloat16
I32 = mybir.dt.int32
ALU = mybir.AluOpType
ACT = mybir.ActivationFunctionType

P = 128
D = 1024
SEQ = 2048
KD = D // P
SSM_W = 512
POOL_W = 512
G, H, NS = 32, 16, 64
CH = 8
HALF = SEQ // 2
NCH = HALF // CH
QG = 4
NQ = G // QG
WINDOWS = (2, 4, 8, 16)
HALO = 16
D_FF = 2816
NF = D_FF // P
TB = 512
NB = SEQ // TB
TF = 1024
NP = SEQ // TF
EPS = 1e-6
MULT = [1, 2, 3, 4, 5, 6, 7, 8, 16, 32, 64, 128, 256, 512]
NM = len(MULT)

TWO_PI_PARTS = (6.28125, 0.0019350051879882812, 3.0198272e-07)
LN2_PARTS = (0.693359375, -2.12194440e-4)
ROUND = 12582912.0


class Chain:

    def __init__(self, eng, sem):
        self.eng, self.sem, self.n = eng, sem, 0

    def link(self, ins):
        self.n += 1
        ins.then_inc(self.sem, 1)
        self.eng.wait_ge(self.sem, self.n)

    def done(self, ins, sem, n):
        ins.then_inc(sem, 1)
        self.eng.wait_ge(sem, n)


class Place:

    def __init__(self, nc, base):
        self.nc, self.base = nc, base

    def at(self, name, kib, shape, dtype=F32):
        size = int(np.prod(shape[1:])) * (2 if dtype == BF16 else 4)
        assert kib * 1024 + size <= SBUF_BYTES, name
        return self.nc.alloc_sbuf_tensor_at(name, list(shape), dtype, offset=self.base + int(kib * 1024))


SBUF_BYTES = 212000


def three(nc, out, wh, wl, xh, xl, first, last):
    nc.tensor.matmul(out, wh, xh, start=first, stop=False)
    nc.tensor.matmul(out, wh, xl, start=False, stop=False)
    return nc.tensor.matmul(out, wl, xh, start=False, stop=last)


def prepare(nc, S, I):
    m = S.map
    ps = S.ps
    sem = S.sem
    ctx = ExitStack()
    wt = [m.at(f"ada_w{i}", 6 + 8 * i, [P, 2048]) for i in range(2)]
    acc = m.at("ada_acc", 22, [P, 2048])
    brow = m.at("ada_brow", 32, [P, 2 * D])
    bcol = m.at("ada_bcol", 40, [P, 6 * KD])
    gcol = m.at("norm_g", 40.25, [P, 2 * KD])
    csb = m.at("c_in", 40.5, [P, KD])
    csl = m.at("c_silu", 40.75, [P, KD])
    lam_rows = m.at("lam_rows", 41, [G, 2, 2 * NS])
    lam = m.at("lam", 43, [P, 2, G])
    dt = m.at("dt", 43.5, [P, G])
    ex = [m.at(f"exp_t{i}", 44 + 1.0 * i, [P, 8 * G]) for i in range(4)]
    exi = m.at("exp_i", 48, [P, 8 * G], I32)
    mag = m.at("mag", 49, [P, 8, G])
    magin = m.at("magin", 50, [P, 8, G])
    ang = m.at("ang", 51, [P, NM, G])
    angn = m.at("angn", 53, [P, NM, G])
    sn = m.at("sn", 55, [P, NM, G])
    cs = m.at("cs", 57, [P, NM, G])
    lc = m.at("lc", 59, [P, 8, G])
    ls = m.at("ls", 60, [P, 8, G])
    x9 = m.at("x9", 61, [P, 9, G])
    y9 = m.at("y9", 62.25, [P, 9, G])
    wre = m.at("wre", 64, [P, 8, G])
    wim = m.at("wim", 65, [P, 8, G])
    x8 = m.at("x8", 66, [P, 8, G])
    y8 = m.at("y8", 67, [P, 8, G])
    sm = [m.at(f"sm{i}", 68 + 0.25 * i, [P, G]) for i in range(8)]
    tw = [m.at(f"tw{i}", 70 + 1.0 * i, [P, 8, G]) for i in range(2)]
    b_in = [m.at(f"b_in{i}", 72 + 2 * i, [P, G, H]) for i in range(2)]
    c_rows = m.at("c_rows", 76, [P, 2, 4, 2 * NS])
    c_t = m.at("c_t", 80, [P, 2, G, H])
    t5 = [m.at(f"t5_{i}", 84 + 2 * i, [P, G, H]) for i in range(2)]
    cl = m.at("cl", 88, [P, G, 9, H])
    it = m.at("it", 106, [P, G, CH, H])
    isb = m.at("isb", 122, [P, G, P])
    kern = m.at("kern", 138, [H, G, P])
    d_t = m.at("d_t", 154, [H, G])
    ekern = m.at("ekern", 154.25, [H, G, H])
    zpad = m.at("zpad", 157, [H, G, 112])
    ec = m.at("e_cos", 171, [P, G, NCH])
    es = m.at("e_sin", 187, [P, G, NCH])
    et = m.at("e_tmp", 6, [P, G, NCH // 2])

    ld_c, ld_small, ld_w, ld_g = sem("p_ld_c"), sem("p_ld_small"), [sem("p_ld_w0"), sem("p_ld_w1")], sem("p_ld_g")
    c_ready, w_used, acc_used = sem("p_c_ready"), sem("p_w_used"), sem("p_acc_used")
    dch, pch, ach = sem("p_dch"), sem("p_pch"), sem("p_ach")
    id_ready, lamt, ct_ready, ang_ready, sin_ready = sem("p_id"), sem("p_lamt"), sem("p_ct"), sem("p_ang"), sem("p_sin")
    ct_copied, it_ready, itt, it_copied = sem("p_ctc"), sem("p_it"), sem("p_itt"), sem("p_itc")
    kr, kr_copied, kr_done, stored, cl_ready, tab_ready = sem("p_kr"), sem("p_krc"), sem("p_krd"), sem("p_st"), sem("p_cl"), sem("p_tab")
    row_out, row_st, zp_ready = sem("p_row"), sem("p_rowst"), sem("p_zp")
    S.saved = stored

    w_ada = I["w_ada"][0].rearrange("(p k) n -> p k n", k=KD)
    nloads = 3 * KD

    block = ctx.enter_context(nc.Block())

    @block.sync
    def _(sp):
        sp.dma_start(csb[:], I["c"][0].rearrange("(p k) -> p k", k=KD)).then_inc(ld_c, 16)
        n = 0
        for sec in range(3):
            for k in range(KD):
                if n >= 2:
                    sp.wait_ge(w_used, n - 1)
                sp.dma_start(wt[n % 2][:], w_ada[:, k, sec * 2048:(sec + 1) * 2048]).then_inc(ld_w[n % 2], 16)
                n += 1
        sp.wait_ge(row_out, 4)
        sp.dma_start(S.gates[:].rearrange("(a s) d -> a (s d)", a=1), brow[0:1, :]).then_inc(row_st, 16)
        sp.wait_ge(row_st, 16)

    @block.scalar
    def _(act):
        d = act.dma_start
        for i, name in enumerate(("ssm_lam_re", "ssm_lam_im")):
            for dup in range(2):
                d(lam_rows[:, i, dup * NS:(dup + 1) * NS], I[name][0]).then_inc(ld_small, 16)
        d(dt[:], I["ssm_log_dt"][0:1, :].to_broadcast([P, G])).then_inc(ld_small, 16)
        for i, name in enumerate(("ssm_b_re", "ssm_b_im")):
            for dup in range(2):
                d(b_in[i][dup * NS:(dup + 1) * NS], I[name][0].rearrange("g p h -> p g h")).then_inc(ld_small, 16)
        for i, name in enumerate(("ssm_c_re", "ssm_c_im")):
            for dup in range(2):
                d(c_rows[:, i, :, dup * NS:(dup + 1) * NS],
                  I[name][0].rearrange("(a g) h p -> (g h) a p", a=4)).then_inc(ld_small, 16)
        d(d_t[:], I["ssm_d"][0].rearrange("(g h) -> h g", h=H), allow_slow_non_contiguous=True).then_inc(ld_small, 16)
        d(bcol[:].rearrange("p (s k) -> p s k", s=6), I["b_ada"][0].rearrange("(s p k) -> p s k", s=6, k=KD)).then_inc(ld_g, 16)
        d(gcol[:, 0:KD], I["g_norm_mix"][0].rearrange("(p k) -> p k", k=KD)).then_inc(ld_g, 16)
        d(gcol[:, KD:2 * KD], I["g_norm_ffn"][0].rearrange("(p k) -> p k", k=KD)).then_inc(ld_g, 16)
        for i, s in enumerate((2, 5)):
            d(brow[:, i * D:(i + 1) * D], I["b_ada"][0:1, s * D:(s + 1) * D].to_broadcast([P, D])).then_inc(ld_g, 16)
        act.wait_ge(ld_c, 16)
        nc.scalar.activation(csl[:], csb[:], ACT.Silu).then_inc(c_ready, 1)
        act.wait_ge(ang_ready, 1)
        nc.scalar.activation(sn[:], ang[:], ACT.Sin).then_inc(sin_ready, 1)
        nc.scalar.activation(cs[:], ang[:], ACT.Sin, scale=0.5).then_inc(sin_ready, 1)
        for i in range(2):
            act.wait_ge(ct_ready, 4 * (i + 1))
            nc.scalar.copy(c_t[:, i].rearrange("p g h -> p (g h)"), ps[1 + i][:]).then_inc(ct_copied, 1)
        for q in range(NQ):
            act.wait_ge(itt, 4 * (q + 1))
            nc.scalar.copy(isb[:, 4 * q:4 * q + 4, :].rearrange("p g n -> p (g n)"), ps[q % 2][:]).then_inc(it_copied, 1)
            act.wait_ge(kr, 4 * (q + 1))
            nc.scalar.copy(kern[:, 4 * q:4 * q + 4, :].rearrange("p g n -> p (g n)"), ps[2 + q % 2][0:H, :]).then_inc(kr_copied, 1)
        act.wait_ge(it_copied, NQ)
        d(S.mats[:, 1, :], isb[:].rearrange("p g n -> p (g n)")).then_inc(stored, 16)
        d(S.mats[:, 2, :].rearrange("p (g n) -> p g n", g=G), cl[:, :, 1:9, :].rearrange("p g t h -> p g (t h)")).then_inc(stored, 16)
        act.wait_ge(zp_ready, 1)
        d(S.kpad[:, :, 0:112].rearrange("g h n -> h g n"), zpad[:]).then_inc(stored, 16)
        act.wait_ge(kr_done, 1)
        d(S.kpad[:, :, 112:240].rearrange("g h n -> h g n"), kern[:]).then_inc(stored, 16)
        act.wait_ge(tab_ready, 7)
        d(S.tabs[:, 0, :], ec[:].rearrange("p g n -> p (g n)")).then_inc(stored, 16)
        d(S.tabs[:, 1, :], es[:].rearrange("p g n -> p (g n)")).then_inc(stored, 16)
        act.wait_ge(stored, 96)

    @block.gpsimd
    def _(pool):
        ch = Chain(pool, pch)
        nc.gpsimd.memset(S.ones[:], 1.0).then_inc(id_ready, 1)
        nc.gpsimd.memset(zpad[:], 0.0).then_inc(zp_ready, 1)
        ch.link(nc.gpsimd.memset(S.ident[:], 0.0))
        ch.link(nc.gpsimd.memset(S.swap[:], 0.0))
        nc.gpsimd.affine_select(out=S.ident[:], in_=S.ident[:], compare_op=ALU.not_equal, fill=1.0, base=0,
                                pattern=[[-1, P]], channel_multiplier=1).then_inc(id_ready, 1)
        ch.link(nc.gpsimd.affine_select(out=S.swap[:], in_=S.swap[:], compare_op=ALU.not_equal, fill=1.0, base=-NS,
                                        pattern=[[-1, P]], channel_multiplier=1))
        nc.gpsimd.affine_select(out=S.swap[:], in_=S.swap[:], compare_op=ALU.not_equal, fill=-1.0, base=NS,
                                pattern=[[-1, P]], channel_multiplier=1).then_inc(id_ready, 1)

    @block.vector
    def _(dve):
        ch = Chain(dve, dch)
        L = ch.link
        V = nc.vector
        TT, TS, STT = V.tensor_tensor, V.tensor_scalar, V.scalar_tensor_tensor

        def expf(out, x, n):
            t, k, r, p = (e[:, 0:n] for e in ex)
            L(TS(x, x, 88.0, -87.0, ALU.min, ALU.max))
            L(TS(t, x, 1.0 / math.log(2.0), ROUND, ALU.mult, ALU.add))
            L(TS(k, t, -ROUND, None, ALU.add))
            L(STT(r, k, -LN2_PARTS[0], x, ALU.mult, ALU.add))
            L(STT(r, k, -LN2_PARTS[1], r, ALU.mult, ALU.add))
            L(TS(p, r, 1.0 / 5040, None, ALU.mult))
            for c in (720, 120, 24, 6, 2, 1):
                L(STT(p, p, 1.0 / c, r, ALU.add, ALU.mult))
            L(TS(t, k, 127.0, 8388608.0, ALU.add, ALU.mult))
            L(V.tensor_copy(exi[:, 0:n], t))
            L(STT(out, p, 1.0, exi[:, 0:n].bitcast(F32), ALU.add, ALU.mult))

        dve.wait_ge(ld_small, 16 * 14)
        dve.wait_ge(lamt, 2)
        L(V.tensor_copy(lam[:].rearrange("p i g -> p (i g)"), ps[0][:, 0:2 * G]))
        L(V.tensor_copy(sm[7][:], dt[:]))
        expf(dt[:], sm[7][:], G)
        L(TT(sm[0][:], lam[:, 0], dt[:], ALU.mult))
        L(TT(sm[1][:], lam[:, 1], dt[:], ALU.mult))
        for tau in range(8):
            TS(magin[:, tau], sm[0][:], float(tau + 1), None, ALU.mult)
        for i, mu in enumerate(MULT):
            last = TS(ang[:, i], sm[1][:], float(mu), None, ALU.mult)
        L(last)
        L(TS(angn[:], ang[:], 1.0 / (2 * math.pi), ROUND, ALU.mult, ALU.add))
        L(TS(angn[:], angn[:], -ROUND, None, ALU.add))
        for c in TWO_PI_PARTS:
            L(STT(ang[:], angn[:], -c, ang[:], ALU.mult, ALU.add))
        ch.done(TS(ang[:], ang[:], 3.1415925, -3.1415925, ALU.min, ALU.max), ang_ready, 1)
        expf(mag[:].rearrange("p t g -> p (t g)"), magin[:].rearrange("p t g -> p (t g)"), 8 * G)
        dve.wait_ge(sin_ready, 2)
        L(TT(cs[:], cs[:], cs[:], ALU.mult))
        L(TS(cs[:], cs[:], -2.0, 1.0, ALU.mult, ALU.add))
        L(V.tensor_copy(S.rad8[:], mag[:, 7]))
        L(TT(lc[:], mag[:], cs[:, 0:8], ALU.mult))
        L(TT(ls[:], mag[:], sn[:, 0:8], ALU.mult))
        lre, lim = lam[:, 0], lam[:, 1]
        L(TT(sm[0][:], lre, lre, ALU.mult))
        L(TT(sm[1][:], lim, lim, ALU.mult))
        L(TT(sm[0][:], sm[0][:], sm[1][:], ALU.add))
        L(V.reciprocal(sm[1][:], sm[0][:]))
        L(TS(sm[2][:], lc[:, 0], -1.0, None, ALU.add))
        L(TT(sm[3][:], sm[2][:], lre, ALU.mult))
        L(TT(sm[4][:], ls[:, 0], lim, ALU.mult))
        L(TT(sm[3][:], sm[3][:], sm[4][:], ALU.add))
        L(TT(wre[:, 0], sm[3][:], sm[1][:], ALU.mult))
        L(TT(sm[3][:], ls[:, 0], lre, ALU.mult))
        L(TT(sm[4][:], sm[2][:], lim, ALU.mult))
        L(TT(sm[3][:], sm[3][:], sm[4][:], ALU.subtract))
        L(TT(wim[:, 0], sm[3][:], sm[1][:], ALU.mult))
        wr0 = wre[:, 0:1, :].to_broadcast([P, 7, G])
        wi0 = wim[:, 0:1, :].to_broadcast([P, 7, G])
        a, b = tw[0][:, 0:7], tw[1][:, 0:7]
        L(TT(a, lc[:, 0:7], wr0, ALU.mult))
        L(TT(b, ls[:, 0:7], wi0, ALU.mult))
        L(TT(wre[:, 1:8], a, b, ALU.subtract))
        L(TT(a, lc[:, 0:7], wi0, ALU.mult))
        L(TT(b, ls[:, 0:7], wr0, ALU.mult))
        L(TT(wim[:, 1:8], a, b, ALU.add))
        re, im = slice(0, NS), slice(NS, P)
        V.tensor_copy(x8[re], wre[re])
        V.tensor_copy(x8[im], wim[im])
        TS(y8[re], wim[re], -1.0, None, ALU.mult)
        V.tensor_copy(y8[im], wre[im])
        V.tensor_copy(x9[re, 1:9], lc[re])
        TS(x9[im, 1:9], ls[im], -1.0, None, ALU.mult)
        TS(y9[re, 1:9], ls[re], -1.0, None, ALU.mult)
        TS(y9[im, 1:9], lc[im], -1.0, None, ALU.mult)
        V.memset(x9[re, 0], 1.0)
        V.memset(x9[im, 0], 0.0)
        V.memset(y9[re, 0], 0.0)
        L(V.memset(y9[im, 0], -1.0))
        for s in range(CH):
            k = CH - 1 - s
            L(TT(t5[0][:], b_in[0][:], x8[:, k, :].unsqueeze(2).to_broadcast([P, G, H]), ALU.mult))
            L(TT(t5[1][:], b_in[1][:], y8[:, k, :].unsqueeze(2).to_broadcast([P, G, H]), ALU.mult))
            ch.done(TT(it[:, :, s, :], t5[0][:], t5[1][:], ALU.add), it_ready, s + 1)
        dve.wait_ge(ct_copied, 2)
        for tau in range(9):
            L(TT(t5[0][:], c_t[:, 0], x9[:, tau, :].unsqueeze(2).to_broadcast([P, G, H]), ALU.mult))
            L(TT(t5[1][:], c_t[:, 1], y9[:, tau, :].unsqueeze(2).to_broadcast([P, G, H]), ALU.mult))
            ch.done(TT(cl[:, :, tau, :], t5[0][:], t5[1][:], ALU.add), cl_ready, tau + 1)

        dve.wait_ge(c_ready, 1)
        dve.wait_ge(ld_g, 16 * 5)
        n = 0
        for sec in range(3):
            for k in range(KD):
                dve.wait_ge(ld_w[n % 2], 16 * (n // 2 + 1))
                ins = (TS(acc[:], wt[n % 2][:], csl[:, 0:1], None, ALU.mult) if k == 0 else
                       STT(acc[:], wt[n % 2][:], csl[:, k:k + 1], acc[:], ALU.mult, ALU.add))
                ins.then_inc(w_used, 1)
                n += 1
                dve.wait_ge(w_used, n)
            dve.wait_ge(acc_used, sec + 1)
            if sec == 0:
                L(TT(S.b1[:], ps[4][:, 0:KD], bcol[:, 0:KD], ALU.add))
                L(TT(sm[5][:, 0:KD], ps[4][:, KD:2 * KD], bcol[:, KD:2 * KD], ALU.add))
                L(STT(S.a1[:], sm[5][:, 0:KD], 1.0, gcol[:, 0:KD], ALU.add, ALU.mult))
            elif sec == 1:
                L(TT(S.b2[:], ps[4][:, KD:2 * KD], bcol[:, 3 * KD:4 * KD], ALU.add))
            else:
                L(TT(sm[5][:, 0:KD], ps[4][:, 0:KD], bcol[:, 4 * KD:5 * KD], ALU.add))
                L(STT(S.a2[:], sm[5][:, 0:KD], 1.0, gcol[:, KD:2 * KD], ALU.add, ALU.mult))
            if sec:
                for hf in range(2):
                    i = 2 * (sec - 1) + hf
                    o = (sec - 1) * D + hf * 512
                    ch.done(TT(brow[0:1, o:o + 512], ps[5 + hf][0:1, :], brow[0:1, o:o + 512], ALU.add), row_out, i + 1)

        dve.wait_ge(kr_copied, NQ)
        L(TT(ekern[:], S.ident[0:H, 0:H].unsqueeze(1).to_broadcast([H, G, H]),
             d_t[:].unsqueeze(2).to_broadcast([H, G, H]), ALU.mult))
        TT(kern[:, :, 0:H], kern[:, :, 0:H], ekern[:], ALU.add).then_inc(kr_done, 1)

        V.tensor_copy(ec[:, :, 0], cs[:, 7])
        L(V.tensor_copy(es[:, :, 0], sn[:, 7]))
        w = 1
        for lev in range(7):
            cw = cs[:, 7 + lev, :].unsqueeze(2).to_broadcast([P, G, w])
            sw = sn[:, 7 + lev, :].unsqueeze(2).to_broadcast([P, G, w])
            L(TT(ec[:, :, w:2 * w], ec[:, :, 0:w], cw, ALU.mult))
            L(TT(et[:, :, 0:w], es[:, :, 0:w], sw, ALU.mult))
            L(TT(ec[:, :, w:2 * w], ec[:, :, w:2 * w], et[:, :, 0:w], ALU.subtract))
            L(TT(es[:, :, w:2 * w], es[:, :, 0:w], cw, ALU.mult))
            L(TT(et[:, :, 0:w], ec[:, :, 0:w], sw, ALU.mult))
            ch.done(TT(es[:, :, w:2 * w], es[:, :, w:2 * w], et[:, :, 0:w], ALU.add), tab_ready, lev + 1)
            w *= 2

    @block.tensor
    def _(pe):
        T = nc.tensor
        pe.wait_ge(id_ready, 3)
        pe.wait_ge(ld_small, 16 * 14)
        for i in range(2):
            T.transpose(ps[0][:, i * G:(i + 1) * G], lam_rows[:, i, :], S.ident[0:G, 0:G]).then_inc(lamt, 1)
        for i in range(2):
            for a in range(4):
                T.transpose(ps[1 + i][:, a * P:(a + 1) * P], c_rows[:, i, a, :], S.ident[:]).then_inc(ct_ready, 1)
        pe.wait_ge(it_ready, CH)
        pe.wait_ge(cl_ready, 9)
        for q in range(NQ):
            if q == 0:
                pe.wait_ge(ct_copied, 2)
            if q >= 2:
                pe.wait_ge(it_copied, q - 1)
                pe.wait_ge(kr_copied, q - 1)
            for g in range(4 * q, 4 * q + 4):
                T.transpose(ps[q % 2][:, (g % 4) * P:(g % 4 + 1) * P], it[:, g].rearrange("p s h -> p (s h)"),
                            S.ident[:]).then_inc(itt, 1)
            for g in range(4 * q, 4 * q + 4):
                T.matmul(ps[2 + q % 2][0:H, (g % 4) * P:(g % 4 + 1) * P], it[:, g, CH - 1, :],
                         cl[:, g, 0:8, :].rearrange("p t h -> p (t h)"), start=True, stop=True).then_inc(kr, 1)
        for sec in range(3):
            pe.wait_ge(w_used, KD * (sec + 1))
            if sec == 2:
                pe.wait_ge(row_out, 2)
            cols = {0: (0, 1), 1: (1,), 2: (0,)}[sec]
            for v in cols:
                for k in range(KD):
                    last = T.matmul(ps[4][:, v * KD + k:v * KD + k + 1], acc[:, bass.ds(v * D + k, P, step=KD)],
                                    S.ones[:, 0:1], start=True, stop=True)
            if sec:
                o = {1: 0, 2: D}[sec]
                for hf in range(2):
                    last = T.matmul(ps[5 + hf][0:1, :], S.ones[:, 0:1], acc[:, o + hf * 512:o + hf * 512 + 512], start=True, stop=True)
            last.then_inc(acc_used, 1)

    ctx.close()


def rstd_steps(nc, link, out, ss, tmp, half_root):
    V = nc.vector
    m, r = tmp
    link(V.tensor_scalar(m, ss, 1.0 / D, EPS, ALU.mult, ALU.add))
    link(V.reciprocal(r, m))
    half_root(out, r)
    link(V.tensor_tensor(r, out, out, ALU.mult))
    link(V.tensor_tensor(r, r, m, ALU.mult))
    link(V.tensor_scalar(r, r, -0.5, 1.5, ALU.mult, ALU.add))
    link(V.tensor_tensor(out, out, r, ALU.mult))


def project(nc, S, I):
    m, ps, sem = S.map, S.ps, S.sem
    ctx = ExitStack()
    NJ = TB // P
    xb = m.at("a_x", 39, [P, NJ, D])
    hh = [m.at(f"a_hh{i}", 55 + 32 * i, [P, KD, TB], F32R) for i in range(2)]
    hl = [m.at(f"a_hl{i}", 71 + 32 * i, [P, KD, TB], F32R) for i in range(2)]
    wh = m.at("a_wh", 119, [P, KD, D], F32R)
    wl = m.at("a_wl", 151, [P, KD, D], F32R)
    usb = [m.at(f"a_u{i}", 183 + 2 * i, [P, SSM_W]) for i in range(2)]
    full = [m.at(f"a_full{i}", 187 + 2 * i, [P, TB]) for i in range(2)]
    wraw = [m.at(f"a_wraw{i}", 191 + 4 * i, [P, D]) for i in range(2)]
    junk = m.at("a_junk", 199, [P, D], BF16)
    st = m.at("a_stat", 201, [P, 8, NJ])

    w_in = I["w_in"][0].rearrange("(p k) n -> p k n", k=KD)
    x_v = I["x"][0].rearrange("(b j p) d -> b p j d", p=P, j=NJ)
    ld_x, ld_w = sem("a_ld_x"), [sem("a_ld_w0"), sem("a_ld_w1")]
    whi, wlo = sem("a_whi"), sem("a_wlo")
    sq, root_in, root = sem("a_sq"), sem("a_root_in"), sem("a_root")
    xn, tr, hi, fu, lo, mm, ev_u, ev_p = (sem("a_" + n) for n in ("xn", "tr", "hi", "full", "lo", "mm", "ev_u", "ev_p"))
    u_st = [sem("a_ust0"), sem("a_ust1")]
    dch = sem("a_dch")
    block = ctx.enter_context(nc.Block())

    @block.sync
    def _(sp):
        sp.dma_start(xb[:], x_v[0]).then_inc(ld_x, 16)
        for k in range(KD):
            if k >= 2:
                sp.wait_ge(whi, k - 1)
                sp.wait_ge(wlo, k - 1)
            sp.dma_start(wraw[k % 2][:], w_in[:, k, :]).then_inc(ld_w[k % 2], 16)
        for b in range(NB):
            if b + 1 < NB:
                sp.wait_ge(tr, KD * (b + 1))
                sp.dma_start(xb[:], x_v[b + 1]).then_inc(ld_x, 16)
            for j in range(NJ):
                n = NJ * b + j
                sp.wait_ge(ev_u, n + 1)
                sp.dma_start(S.u[b * TB + j * P:b * TB + (j + 1) * P, :], usb[n % 2][:]).then_inc(u_st[n % 2], 16)
        for i in range(2):
            sp.wait_ge(u_st[i], 16 * NB * NJ // 2)

    @block.scalar
    def _(act):
        def squares(b):
            act.wait_ge(ld_x, 16 * (b + 1))
            for j in range(NJ):
                nc.scalar.activation(junk[:], xb[:, j], ACT.Square, accum_out=st[:, 0, j:j + 1]).then_inc(sq, 1)
                act.wait_ge(sq, NJ * b + j + 1)
            act.wait_ge(root_in, b + 1)
            nc.scalar.activation(st[:, 1], st[:, 3], ACT.Sqrt).then_inc(root, 1)

        def weights(k):
            act.wait_ge(ld_w[k % 2], 16 * (k // 2 + 1))
            nc.scalar.copy(wh[:, k], wraw[k % 2][:]).then_inc(whi, 1)

        def highs(b):
            for k in range(KD):
                n = KD * b + k
                act.wait_ge(tr, n + 1)
                if n >= 2:
                    act.wait_ge(lo, n - 1)
                nc.scalar.activation(full[k % 2][:], ps[k % 2][:], ACT.Identity, bias=S.b1[:, k:k + 1],
                                     scale=S.a1[:, k:k + 1]).then_inc(fu, 1)

        def evac(b):
            for j in range(NJ):
                n = NJ * b + j
                act.wait_ge(mm, 8 * b + j + 1)
                if n >= 2:
                    act.wait_ge(u_st[n % 2], 16 * (n // 2))
                nc.scalar.copy(usb[n % 2][:], ps[2 + (8 * b + j) % 6][:]).then_inc(ev_u, 1)

        squares(0)
        weights(0)
        weights(1)
        highs(0)
        for k in range(2, KD):
            weights(k)
        for b in range(NB):
            if b + 1 < NB:
                squares(b + 1)
            evac(b)
            if b + 1 < NB:
                highs(b + 1)

    @block.vector
    def _(dve):
        V = nc.vector
        ch = Chain(dve, dch)

        def half_root(n):
            def f(out, r):
                V.tensor_copy(st[:, 3], r).then_inc(root_in, 1)
                dve.wait_ge(root, n + 1)
            return f

        def normalise(b):
            dve.wait_ge(sq, NJ * (b + 1))
            rstd_steps(nc, ch.link, st[:, 1], st[:, 0], (st[:, 2], st[:, 4]), half_root(b))
            for j in range(NJ):
                V.tensor_scalar(xb[:, j], xb[:, j], st[:, 1, j:j + 1], None, ALU.mult).then_inc(xn, 1)

        def lows(b):
            for k in range(KD):
                n = KD * b + k
                dve.wait_ge(fu, n + 1)
                if b >= 2:
                    dve.wait_ge(mm, 8 * (b - 1))
                V.tensor_copy(hh[b % 2][:, k], full[k % 2][:]).then_inc(hi, 1)
                dve.wait_ge(hi, n + 1)
                V.tensor_tensor(hl[b % 2][:, k], full[k % 2][:], hh[b % 2][:, k].bitcast(F32), ALU.subtract).then_inc(lo, 1)

        def wlows(k):
            dve.wait_ge(whi, k + 1)
            V.tensor_tensor(wl[:, k], wraw[k % 2][:], wh[:, k].bitcast(F32), ALU.subtract).then_inc(wlo, 1)

        def evac(b):
            for j in range(4):
                dve.wait_ge(mm, 8 * b + 5 + j)
                V.tensor_copy(S.pt[:, j, HALO + b * TB:HALO + (b + 1) * TB], ps[2 + (8 * b + 4 + j) % 6][:]).then_inc(ev_p, 1)

        V.memset(S.pt[:, :, 0:HALO], 0.0)
        normalise(0)
        wlows(0)
        wlows(1)
        lows(0)
        for k in range(2, KD):
            wlows(k)
        for b in range(NB):
            if b + 1 < NB:
                normalise(b + 1)
            if b + 1 < NB:
                lows(b + 1)
            evac(b)

    @block.tensor
    def _(pe):
        T = nc.tensor

        def transposes(b):
            pe.wait_ge(xn, NJ * (b + 1))
            for k in range(KD):
                n = KD * b + k
                if n >= 2:
                    pe.wait_ge(fu, n - 1)
                for j in range(NJ):
                    last = T.transpose(ps[k % 2][:, j * P:(j + 1) * P], xb[:, j, bass.ds(k, P, step=KD)], S.ident[:])
                last.then_inc(tr, 1)

        def output(b, o):
            n = 8 * b + o
            if n >= 6:
                q = n - 6
                if q % 8 < 4:
                    pe.wait_ge(ev_u, 4 * (q // 8) + q % 8 + 1)
                else:
                    pe.wait_ge(ev_p, 4 * (q // 8) + q % 8 - 3)
            out = ps[2 + n % 6][:]
            h, l = hh[b % 2], hl[b % 2]
            for k in range(KD):
                if b == 0 and o == 0:
                    pe.wait_ge(whi, k + 1)
                    pe.wait_ge(wlo, k + 1)
                if o < 4:
                    js = slice(o * P, (o + 1) * P)
                    last = three(nc, out, h[:, k, js], l[:, k, js], wh[:, k, 0:SSM_W], wl[:, k, 0:SSM_W], k == 0, k == KD - 1)
                else:
                    cs = slice(SSM_W + (o - 4) * P, SSM_W + (o - 3) * P)
                    last = three(nc, out, wh[:, k, cs], wl[:, k, cs], h[:, k, :], l[:, k, :], k == 0, k == KD - 1)
            last.then_inc(mm, 1)

        transposes(0)
        for b in range(NB):
            pe.wait_ge(lo, KD * (b + 1))
            for o in range(4):
                output(b, o)
            if b + 1 < NB:
                transposes(b + 1)
            for o in range(4, 8):
                output(b, o)

    ctx.close()


def scan(nc, S, I):
    m, ps, sem = S.map, S.ps, S.sem
    ctx = ExitStack()
    NQ2 = 2 * NQ
    W = QG * NCH
    tm = m.at("s_t", 71, [P, G, P])
    im = m.at("s_i", 87, [P, G, P])
    om = m.at("s_o", 103, [P, G, P])
    ec = m.at("s_cos", 119, [P, G, NCH])
    es = m.at("s_sin", 135, [P, G, NCH])
    us = m.at("s_u", 151, [P, CH, SSM_W])
    yh = [m.at(f"s_y{i}", 167 + 4 * i, [P, CH, P]) for i in range(2)]
    ut = [m.at(f"s_ut{i}", 175 + 2 * i, [P, W]) for i in range(4)]
    ss = m.at("s_s", 183, [P, W])
    bb = m.at("s_b", 185, [P, QG, NCH])
    zz = [m.at(f"s_z{i}", 187 + 2 * i, [P, QG, NCH]) for i in range(2)]
    xx = [m.at(f"s_x{i}", 191 + 2.0625 * i, [P, QG, NCH + 1]) for i in range(2)]
    uq = m.at("s_uq", 195.125, [P, QG, CH, H])
    pl = [m.at(f"s_pl{i}", 197.125 + 4.0625 * i, [P, HALO + HALF]) for i in range(2)]
    carry = m.at("s_carry", 205.25, [P, G])
    rc = m.at("s_rc", 205.5, [P, 4, HALO])
    ri = m.at("s_ri", 205.75, [P, HALO], I32)
    rt = m.at("s_rt", 205.875, [P, HALO])

    ld_m, ld_u, u_q, tr_u, ut_c, s_mm, s_c, s_j, m_used, z_ready, j2, x_ready, y_mm, y_act, y_tr, y_c = (
        sem("s_" + n) for n in ("ld_m", "ld_u", "u_q", "tr_u", "ut_c", "smm", "sc", "sj", "m_used", "z_ready", "j2",
                                "x_ready", "y_mm", "y_act", "y_tr", "y_c"))
    dch, pch, count, inv_count = sem("s_dch"), sem("s_pch"), sem("s_count"), sem("s_inv")
    u_v = S.u.rearrange("(h c t) n -> h c t n", h=2, t=CH)
    block = ctx.enter_context(nc.Block())

    @block.sync
    def _(sp):
        sp.dma_start(us[:], u_v[0]).then_inc(ld_u, 16)
        sp.dma_start(im[:].rearrange("p g n -> p (g n)"), S.mats[:, 1, :]).then_inc(ld_m, 16)
        sp.dma_start(om[:].rearrange("p g n -> p (g n)"), S.mats[:, 2, :]).then_inc(ld_m, 16)
        sp.dma_start(ec[:].rearrange("p g n -> p (g n)"), S.tabs[:, 0, :]).then_inc(ld_m, 16)
        sp.dma_start(es[:].rearrange("p g n -> p (g n)"), S.tabs[:, 1, :]).then_inc(ld_m, 16)
        for s in range(CH):
            o = (CH - 1 - s) * H
            sp.dma_start(tm[s * H:(s + 1) * H], S.kpad[:, :, o:o + P].rearrange("g h n -> h g n")).then_inc(ld_m, 16)
        sp.wait_ge(tr_u, NQ)
        sp.dma_start(us[:], u_v[1]).then_inc(ld_u, 16)

    def turns(flip, swap, swap_back, enter, leave, back):
        def do(step, i):
            if 0 <= i < NQ2:
                step(i)
        for i in range(-2, NQ2 + 2):
            do(flip, i + 2)
            do(swap, i + 1)
            do(swap_back, i)
            do(enter, i + 2)
            do(leave, i - 1)
            do(back, i - 2)

    @block.tensor
    def _(pe):
        T = nc.tensor

        def flip(i):
            pe.wait_ge(u_q, i + 1)
            if i:
                pe.wait_ge(ut_c, i)
            for g in range(QG):
                last = T.transpose(ps[0][:, g * P:(g + 1) * P], uq[:, g].rearrange("p t h -> p (t h)"), S.ident[:])
            last.then_inc(tr_u, 1)

        def enter(i):
            pe.wait_ge(ut_c, i + 1)
            if i:
                pe.wait_ge(m_used, i)
            for g in range(QG):
                last = T.matmul(ps[1][:, g * P:(g + 1) * P], im[:, i % NQ * QG + g, :], ut[i % 4][:, g * P:(g + 1) * P],
                                start=True, stop=True)
            last.then_inc(s_mm, 1)

        def swap(i):
            pe.wait_ge(s_c, i + 1)
            if i:
                pe.wait_ge(m_used, i)
            T.matmul(ps[2][:], S.swap[:], ss[:], start=True, stop=True).then_inc(s_j, 1)

        def swap_back(i):
            pe.wait_ge(z_ready, i + 1)
            if i:
                pe.wait_ge(x_ready, i)
            T.matmul(ps[3][:], S.swap[:], zz[i % 2][:].rearrange("p g n -> p (g n)"), start=True, stop=True).then_inc(j2, 1)

        def leave(i):
            pe.wait_ge(x_ready, i + 1)
            if i >= 2:
                pe.wait_ge(y_act, i - 1)
            for g in range(QG):
                gg = i % NQ * QG + g
                o = ps[4 + i % 2][:, g * P:(g + 1) * P]
                T.matmul(o, ut[i % 4][:, g * P:(g + 1) * P], tm[:, gg, :], start=True, stop=False)
                last = T.matmul(o, xx[i % 2][:, g, 0:NCH], om[:, gg, :], start=False, stop=True)
            last.then_inc(y_mm, 1)

        def back(i):
            if i % 2 == 0:
                return
            pe.wait_ge(y_act, i + 1)
            for r in range(2):
                if i > 1:
                    pe.wait_ge(y_c, i - 1 + r - 1)
                for t in range(4):
                    last = T.transpose(ps[6 + r][:, t * P:(t + 1) * P], yh[(i // 2) % 2][:, 4 * r + t, :], S.ident[:])
                last.then_inc(y_tr, 1)

        pe.wait_ge(ld_m, 16 * 12)
        turns(flip, swap, swap_back, enter, leave, back)

    @block.scalar
    def _(act):
        def gather(i):
            half, q = divmod(i, NQ)
            if q == 0:
                act.wait_ge(ld_u, 16 * (half + 1))
            if i:
                act.wait_ge(tr_u, i)
            c = q * QG * H
            nc.scalar.copy(uq[:], us[:, :, c:c + QG * H].rearrange("p t (g h) -> p g t h", g=QG)).then_inc(u_q, 1)

        def flipped(i):
            act.wait_ge(tr_u, i + 1)
            if i >= 4:
                act.wait_ge(y_mm, i - 3)
            nc.scalar.copy(ut[i % 4][:], ps[0][:]).then_inc(ut_c, 1)
            if i + 1 < NQ2:
                gather(i + 1)

        def entered(i):
            act.wait_ge(s_mm, i + 1)
            if i:
                act.wait_ge(s_j, i)
            nc.scalar.copy(ss[:], ps[1][:]).then_inc(s_c, 1)

        def gelu(i):
            act.wait_ge(y_mm, i + 1)
            if i >= 4:
                act.wait_ge(y_tr, 2 * (i // 2 - 1))
            f = (i % 2) * QG * H
            for g in range(QG):
                last = nc.scalar.activation(yh[(i // 2) % 2][:, :, f + g * H:f + (g + 1) * H],
                                            ps[4 + i % 2][:, g * P:(g + 1) * P].rearrange("p (t h) -> p t h", t=CH),
                                            ACT.Gelu_apprx_tanh)
            last.then_inc(y_act, 1)

        def back(i):
            if i % 2 == 0:
                return
            half, q = divmod(i, NQ)
            for r in range(2):
                act.wait_ge(y_tr, i - 1 + r + 1)
                dst = S.yt[:, q // 2, half * HALF:(half + 1) * HALF].rearrange("p (c t) -> p t c", t=CH)
                nc.scalar.copy(dst[:, 4 * r:4 * r + 4, :], ps[6 + r][:].rearrange("p (t c) -> p t c", t=4)).then_inc(y_c, 1)

        gather(0)
        turns(flipped, lambda i: None, lambda i: None, entered, gelu, back)

    @block.vector
    def _(dve):
        V = nc.vector
        ch = Chain(dve, dch)
        L = ch.link
        TT = V.tensor_tensor
        f = "p g n -> p (g n)"

        def trig(i):
            gs = slice(i % NQ * QG, (i % NQ + 1) * QG)
            return gs, ec[:, gs, :].rearrange(f), es[:, gs, :].rearrange(f)

        def scan_item(i):
            gs, cosq, sinq = trig(i)
            zf, bf = zz[i % 2][:].rearrange(f), bb[:].rearrange(f)
            dve.wait_ge(s_c, i + 1)
            if i >= 2:
                dve.wait_ge(j2, i - 1)
            TT(zf, ps[1][:], cosq, ALU.mult)
            dve.wait_ge(s_j, i + 1)
            L(TT(bf, ps[2][:], sinq, ALU.mult))
            V.tensor_tensor(zf, zf, bf, ALU.add).then_inc(m_used, 1)
            dve.wait_ge(m_used, i + 1)
            for g in range(QG):
                gg = i % NQ * QG + g
                last = V.tensor_tensor_scan(zz[i % 2][:, g, :], S.rad8[:, gg:gg + 1].to_broadcast([P, NCH]),
                                            zz[i % 2][:, g, :], carry[:, gg:gg + 1], ALU.mult, ALU.add)
            last.then_inc(z_ready, 1)

        def turn_on(i):
            gs, cosq, sinq = trig(i)
            x = xx[i % 2]
            if i >= 2:
                dve.wait_ge(y_mm, i - 1)
            V.tensor_copy(x[:, :, 0:1], carry[:, gs].unsqueeze(2))
            dve.wait_ge(z_ready, i + 1)
            TT(x[:, :, 1:NCH + 1], zz[i % 2][:], ec[:, gs, :], ALU.mult)
            dve.wait_ge(j2, i + 1)
            L(TT(bb[:].rearrange(f), ps[3][:], sinq, ALU.mult))
            L(TT(x[:, :, 1:NCH + 1], x[:, :, 1:NCH + 1], bb[:], ALU.subtract))
            V.tensor_copy(carry[:, gs].unsqueeze(2), x[:, :, NCH:NCH + 1]).then_inc(x_ready, 1)
            if i + 1 == NQ:
                dve.wait_ge(x_ready, NQ)

        L(V.memset(carry[:], 0.0))
        dve.wait_ge(count, 4)
        V.reciprocal(rc[:], rc[:]).then_inc(inv_count, 1)
        dve.wait_ge(ld_m, 16 * 12)
        turns(lambda i: None, scan_item, turn_on, lambda i: None, lambda i: None, lambda i: None)

    @block.gpsimd
    def _(pool):
        ch = Chain(pool, pch)
        L = ch.link
        Q = nc.gpsimd
        L(Q.iota(ri[:], [[1, HALO]], base=1, channel_multiplier=0))
        L(Q.tensor_copy(rt[:], ri[:]))
        for w in range(4):
            Q.tensor_scalar(rc[:, w], rt[:], float(WINDOWS[w]), None, ALU.min).then_inc(count, 1)
        pool.wait_ge(inv_count, 1)
        for w, win in enumerate(WINDOWS):
            for half in (1, 0):
                o = half * HALF
                cur, sh, n = S.pt[:, w, o:o + HALO + HALF], 1, 0
                while sh < win:
                    nxt, lo = pl[n % 2], 2 * sh - 1
                    L(Q.tensor_tensor(nxt[:, lo:], cur[:, lo:], cur[:, lo - sh:HALO + HALF - sh], ALU.add))
                    cur, sh, n = nxt[:], sh * 2, n + 1
                if half == 0:
                    L(Q.tensor_tensor(rt[:], cur[:, HALO:2 * HALO], rc[:, w], ALU.mult))
                L(Q.tensor_scalar(cur[:, HALO:], cur[:, HALO:], 1.0 / win, None, ALU.mult))
                if half == 0:
                    L(Q.tensor_copy(cur[:, HALO:2 * HALO], rt[:]))
                L(Q.tensor_tensor(S.pt[:, w, o + HALO:o + HALO + HALF], cur[:, HALO:],
                                  S.pt[:, w, o + HALO:o + HALO + HALF], ALU.subtract))

    ctx.close()


def mix(nc, S, I):
    m, ps, sem = S.map, S.ps, S.sem
    ctx = ExitStack()
    KG = SSM_W // P
    KM = KD
    gh = m.at("m_gh", 71, [P, KG, 2 * SSM_W], F32R)
    gl = m.at("m_gl", 87, [P, KG, 2 * SSM_W], F32R)
    oh = m.at("m_oh", 103, [P, KM, D], F32R)
    ol = m.at("m_ol", 135, [P, KM, D], F32R)
    yhh = m.at("m_yh", 167, [P, KG, TB], F32R)
    yhl = m.at("m_yl", 175, [P, KG, TB], F32R)
    raw = [m.at(f"m_raw{i}", 183 + 4 * i, [P, D]) for i in range(2)]
    sig = [m.at(f"m_sig{i}", 191 + 2 * i, [P, TB]) for i in range(2)]
    wp = m.at("m_wp", 195, [P, 4, P])
    col = m.at("m_col", 197, [P, 16])
    mh = m.at("m_mh", 71, [P, KM, TB], F32R)
    ml = m.at("m_ml", 87, [P, KM, TB], F32R)
    xt = [m.at(f"m_x{i}", 167 + 4 * i, [P, D]) for i in range(2)]
    x1 = [m.at(f"m_x1{i}", 175 + 4 * i, [P, D]) for i in range(2)]
    gb = m.at("m_gate", 183, [P, D])

    ld_g, ld_s = [sem("m_ld0"), sem("m_ld1")], sem("m_lds")
    whi, wlo, yhi, ylo, mm, sg, ys, pmm, pev = (sem("m_" + n) for n in ("whi", "wlo", "yhi", "ylo", "mm", "sg", "ys", "pmm", "pev"))
    NW = KG + KM
    ctxb = ExitStack()
    block = ctxb.enter_context(nc.Block())

    def wraw(n):
        return (gh, gl, n) if n < KG else (oh, ol, n - KG)

    @block.sync
    def _(sp):
        wg = I["w_glu"][0].rearrange("(k p) n -> p k n", p=P)
        wo = I["w_out"][0].rearrange("(k p) n -> p k n", p=P)
        for n in range(NW):
            if n >= 2:
                sp.wait_ge(whi, n - 1)
                sp.wait_ge(wlo, n - 1)
            sp.dma_start(raw[n % 2][:], wg[:, n] if n < KG else wo[:, n - KG]).then_inc(ld_g[n % 2], 16)
            if n == 1:
                sp.dma_start(wp[:], I["w_pool"][0].rearrange("g c d -> c g d")).then_inc(ld_s, 16)
                sp.dma_start(col[:, 0:8], I["b_glu"][0].rearrange("(k p) -> p k", p=P), allow_slow_non_contiguous=True).then_inc(ld_s, 16)
                sp.dma_start(col[:, 8:12], I["b_pool"][0].rearrange("g d -> d g"), allow_slow_non_contiguous=True).then_inc(ld_s, 16)
                sp.dma_start(col[:, 12:16], I["pool_scale"][0].rearrange("(g d) -> d g", g=4), allow_slow_non_contiguous=True).then_inc(ld_s, 16)

    @block.scalar
    def _(act):
        act.wait_ge(ld_s, 64)
        n = 0

        def weight(n):
            h, _, k = wraw(n)
            act.wait_ge(ld_g[n % 2], 16 * (n // 2 + 1))
            nc.scalar.copy(h[:, k], raw[n % 2][:]).then_inc(whi, 1)

        for n in range(KG):
            weight(n)
        for b in range(NB):
            if b:
                act.wait_ge(mm, 8 * b)
            nc.scalar.copy(yhh[:], S.yt[:, :, b * TB:(b + 1) * TB]).then_inc(yhi, 1)
            for t in range(4):
                i = 4 * b + t
                act.wait_ge(mm, 8 * b + 2 * t + 2)
                if i >= 2:
                    act.wait_ge(ys, i - 1)
                nc.scalar.activation(sig[i % 2][:], ps[2 * (i % 2) + 1][:], ACT.Sigmoid, bias=col[:, 4 + t:5 + t]).then_inc(sg, 1)
            for n in range(KG + 2 * b, KG + 2 * b + 2):
                weight(n)

    @block.vector
    def _(dve):
        V = nc.vector
        dve.wait_ge(ld_s, 64)

        def weight(n):
            h, l, k = wraw(n)
            dve.wait_ge(whi, n + 1)
            V.tensor_tensor(l[:, k], raw[n % 2][:], h[:, k].bitcast(F32), ALU.subtract).then_inc(wlo, 1)

        for n in range(KG):
            weight(n)
        for b in range(NB):
            bs = slice(b * TB, (b + 1) * TB)
            dve.wait_ge(yhi, b + 1)
            V.tensor_tensor(yhl[:], S.yt[:, :, bs], yhh[:].bitcast(F32), ALU.subtract).then_inc(ylo, 1)
            dve.wait_ge(ylo, b + 1)
            for w in range(4):
                i = 4 * b + w
                dve.wait_ge(pmm, i + 1)
                V.tensor_scalar(S.pt[:, w, HALO + b * TB:HALO + (b + 1) * TB], ps[4 + i % 2][:], col[:, 8 + w:9 + w],
                                col[:, 12 + w:13 + w], ALU.add, ALU.mult).then_inc(pev, 1)
            for t in range(4):
                i = 4 * b + t
                dve.wait_ge(sg, i + 1)
                V.scalar_tensor_tensor(S.yt[:, t, bs], ps[2 * (i % 2)][:], col[:, t:t + 1], sig[i % 2][:], ALU.add,
                                       ALU.mult).then_inc(ys, 1)
            for n in range(KG + 2 * b, KG + 2 * b + 2):
                weight(n)

    @block.tensor
    def _(pe):
        T = nc.tensor
        pe.wait_ge(ld_s, 64)
        for b in range(NB):
            for w in range(4):
                i = 4 * b + w
                if i >= 2:
                    pe.wait_ge(pev, i - 1)
                T.matmul(ps[4 + i % 2][:], wp[:, w], S.pt[:, w, HALO + b * TB:HALO + (b + 1) * TB], start=True,
                         stop=True).then_inc(pmm, 1)
            pe.wait_ge(wlo, KG)
            pe.wait_ge(ylo, b + 1)
            for t in range(4):
                i = 4 * b + t
                if i >= 2:
                    pe.wait_ge(ys, i - 1)
                for part in range(2):
                    for k in range(KG):
                        c = slice(part * SSM_W + t * P, part * SSM_W + (t + 1) * P)
                        last = three(nc, ps[2 * (i % 2) + part][:], gh[:, k, c], gl[:, k, c], yhh[:, k], yhl[:, k], k == 0, k == KG - 1)
                    last.then_inc(mm, 1)

    ctxb.close()

    NJ = TB // P
    ld_x, ld_b, mhi, mlo, om, t1, x1r, xst = [sem("o_ldx0"), sem("o_ldx1")], sem("o_ldb"), sem("o_mhi"), sem("o_mlo"), sem("o_mm"), sem("o_t1"), sem("o_x1"), [sem("o_st0"), sem("o_st1")]
    block = ctx.enter_context(nc.Block())

    @block.sync
    def _(sp):
        sp.dma_start(gb[:], S.gates[0:1, :].to_broadcast([P, D])).then_inc(ld_b, 16)
        for n in range(SEQ // P):
            if n >= 2:
                sp.wait_ge(x1r, 2 * (n - 1))
            sp.dma_start(xt[n % 2][:], I["x"][0, n * P:(n + 1) * P, :]).then_inc(ld_x[n % 2], 16)
            if n >= 1:
                sp.wait_ge(x1r, 2 * n)
                sp.dma_start(S.x1[(n - 1) * P:n * P, :], x1[(n - 1) % 2][:]).then_inc(xst[(n - 1) % 2], 16)
        n = SEQ // P
        sp.wait_ge(x1r, 2 * n)
        sp.dma_start(S.x1[(n - 1) * P:n * P, :], x1[(n - 1) % 2][:]).then_inc(xst[(n - 1) % 2], 16)
        sp.wait_ge(xst[0], 16 * n // 2)
        sp.wait_ge(xst[1], 16 * n // 2)

    @block.scalar
    def _(act):
        for b in range(NB):
            bs = slice(b * TB, (b + 1) * TB)
            for k in range(KM):
                if b:
                    act.wait_ge(om, 8 * b)
                src = S.yt[:, k, bs] if k < 4 else S.pt[:, k - 4, HALO + b * TB:HALO + (b + 1) * TB]
                nc.scalar.copy(mh[:, k], src).then_inc(mhi, 1)

    @block.gpsimd
    def _(pool):
        for b in range(NB):
            bs = slice(b * TB, (b + 1) * TB)
            for k in range(KM):
                src = S.yt[:, k, bs] if k < 4 else S.pt[:, k - 4, HALO + b * TB:HALO + (b + 1) * TB]
                pool.wait_ge(mhi, KM * b + k + 1)
                nc.gpsimd.tensor_tensor(ml[:, k], src, mh[:, k].bitcast(F32), ALU.subtract).then_inc(mlo, 1)

    @block.vector
    def _(dve):
        V = nc.vector
        dve.wait_ge(ld_b, 16)
        for n in range(SEQ // P):
            dve.wait_ge(ld_x[n % 2], 16 * (n // 2 + 1))
            if n >= 2:
                dve.wait_ge(xst[n % 2], 16 * (n // 2))
            for r in range(2):
                i = 2 * n + r
                rs = slice(r * 512, (r + 1) * 512)
                dve.wait_ge(om, i + 1)
                V.tensor_tensor(x1[n % 2][:, rs], ps[i % 8][:], gb[:, rs], ALU.mult).then_inc(t1, 1)
                dve.wait_ge(t1, i + 1)
                V.tensor_tensor(x1[n % 2][:, rs], x1[n % 2][:, rs], xt[n % 2][:, rs], ALU.add).then_inc(x1r, 1)

    @block.tensor
    def _(pe):
        for b in range(NB):
            pe.wait_ge(mlo, KM * (b + 1))
            for j in range(NJ):
                for r in range(2):
                    i = 8 * b + 2 * j + r
                    if i >= 8:
                        pe.wait_ge(t1, i - 7)
                    for k in range(KM):
                        js, rs = slice(j * P, (j + 1) * P), slice(r * 512, (r + 1) * 512)
                        last = three(nc, ps[i % 8][:], mh[:, k, js], ml[:, k, js], oh[:, k, rs], ol[:, k, rs], k == 0, k == KM - 1)
                    last.then_inc(om, 1)

    ctx.close()


def ffn(nc, S, I):
    m, ps, sem = S.map, S.ps, S.sem
    ctx = ExitStack()
    NT = TF // P
    h2h = m.at("f_h2h", 6, [P, KD, TF], F32R)
    h2l = m.at("f_h2l", 38, [P, KD, TF], F32R)
    acc = m.at("f_acc", 70, [P, NT, D])
    uraw = [m.at(f"f_uraw{i}", 102 + 8 * i, [P, KD, 2, P]) for i in range(2)]
    uh = [m.at(f"f_uh{i}", 118 + 16 * i, [P, KD, 2, P], F32R) for i in range(2)]
    ul = [m.at(f"f_ul{i}", 126 + 16 * i, [P, KD, 2, P], F32R) for i in range(2)]
    draw = [m.at(f"f_draw{i}", 150 + 4 * i, [P, D]) for i in range(2)]
    dh = [m.at(f"f_dh{i}", 158 + 8 * i, [P, D], F32R) for i in range(2)]
    dl = [m.at(f"f_dl{i}", 162 + 8 * i, [P, D], F32R) for i in range(2)]
    ah = [m.at(f"f_ah{i}", 174 + 8 * i, [P, TF], F32R) for i in range(2)]
    al = [m.at(f"f_al{i}", 178 + 8 * i, [P, TF], F32R) for i in range(2)]
    gs = m.at("f_gs", 190, [P, 2 + TF])
    cv = [m.at(f"f_cv{i}", 194.5 + 2 * i, [P, 512]) for i in range(2)]
    full = [m.at(f"f_full{i}", 198.5 + 2 * i, [P, 512]) for i in range(2)]
    halo = m.at("f_halo", 202.5, [P, NF, 2])
    cw = m.at("f_cw", 202.75, [P, 4 * NF])
    st = m.at("f_stat", 203.25, [P, 8, NT])
    cj = [m.at(f"f_cj{i}", 203.5 + 0.0625 * i, [P, 4]) for i in range(2)]
    crow = m.at("f_crow", 118, [4 * NF, P])
    junk = m.at("f_junk", 110, [P, D], BF16)
    gt = m.at("f_gt", 6, [P, D])
    gf = m.at("f_gf", 10, [P, D])
    xr = [m.at(f"f_xr{i}", 14 + 4 * i, [P, D]) for i in range(2)]
    oo = [m.at(f"f_oo{i}", 22 + 4 * i, [P, D]) for i in range(2)]
    junk2 = m.at("f_junk2", 30, [P, D], BF16)

    w_up = I["w_up"][0].rearrange("(p k) n -> p k n", k=KD)
    w_dn = I["w_down"][0]
    ld_cw, cwt, cw_ok = sem("f_ld_cw"), sem("f_cwt"), sem("f_cw_ok")

    ctxb = ExitStack()
    block = ctxb.enter_context(nc.Block())

    @block.sync
    def _(sp):
        for i in range(3):
            sp.dma_start(crow[i * NF:(i + 1) * NF, :], I["w_conv"][0, i].rearrange("(j p) -> j p", p=P)).then_inc(ld_cw, 16)
        sp.dma_start(crow[3 * NF:4 * NF, :], I["b_conv"][0].rearrange("(j p) -> j p", p=P)).then_inc(ld_cw, 16)

    @block.tensor
    def _(pe):
        pe.wait_ge(ld_cw, 64)
        nc.tensor.transpose(ps[0][:, 0:4 * NF], crow[:], S.ident[0:4 * NF, 0:4 * NF]).then_inc(cwt, 1)

    @block.vector
    def _(dve):
        nc.vector.memset(halo[:], 0.0)
        dve.wait_ge(cwt, 1)
        nc.vector.tensor_copy(cw[:], ps[0][:, 0:4 * NF]).then_inc(cw_ok, 1)
        dve.wait_ge(cw_ok, 1)

    ctxb.close()

    ld_x, sq, root_in, root, xn, tr, hi, fu, lo, dch = (sem("f_" + s) for s in ("ldx", "sq", "ri", "ro", "xn", "tr", "hi", "fu", "lo", "dch"))
    ld_b, ld_r, t1, sq2, root_in2, root2, oo_r, o_st = (sem("z_" + s) for s in ("ldb", "ldr", "t1", "sq", "ri", "ro", "oo", "ost"))
    names = ("ldu0", "ldu1", "ldd0", "ldd1", "uhi", "ulo", "dhi", "dlo", "upg", "upv", "gev", "cvd", "sil", "prod",
             "vhi", "vlo", "dmm", "dad", "chn", "hal")
    q = {s: sem("b_" + s) for s in names}
    links = [0]
    for half in range(NP):
        t0, n0 = half * TF, half * 2 * KD
        ctxb = ExitStack()
        block = ctxb.enter_context(nc.Block())

        @block.sync
        def _(sp):
            for j in range(NT):
                sp.dma_start(acc[:, j], S.x1[t0 + j * P:t0 + (j + 1) * P, :]).then_inc(ld_x, 16)

        @block.scalar
        def _(act):
            act.wait_ge(ld_x, 16 * NT * (half + 1))
            for j in range(NT):
                nc.scalar.activation(junk[:], acc[:, j], ACT.Square, accum_out=st[:, 0, j:j + 1]).then_inc(sq, 1)
                act.wait_ge(sq, half * NT + j + 1)
            act.wait_ge(root_in, half + 1)
            nc.scalar.activation(st[:, 1], st[:, 3], ACT.Sqrt).then_inc(root, 1)
            for k in range(KD):
                for g in range(2):
                    n = 2 * k + g
                    act.wait_ge(tr, n0 + n + 1)
                    if n >= 2:
                        act.wait_ge(lo, n0 + n - 1)
                    nc.scalar.activation(full[n % 2][:], ps[n % 4][:], ACT.Identity,
                                         bias=S.b2[:, k:k + 1], scale=S.a2[:, k:k + 1]).then_inc(fu, 1)

        @block.vector
        def _(dve):
            V = nc.vector
            ch = Chain(dve, dch)
            ch.n = links[-1]
            dve.wait_ge(sq, NT * (half + 1))

            def half_root(out, r):
                V.tensor_copy(st[:, 3], r).then_inc(root_in, 1)
                dve.wait_ge(root, half + 1)

            rstd_steps(nc, ch.link, st[:, 1], st[:, 0], (st[:, 2], st[:, 4]), half_root)
            for j in range(NT):
                V.tensor_scalar(acc[:, j], acc[:, j], st[:, 1, j:j + 1], None, ALU.mult).then_inc(xn, 1)
            for n in range(2 * KD):
                k, g = divmod(n, 2)
                c = slice(g * 512, (g + 1) * 512)
                dve.wait_ge(fu, n0 + n + 1)
                V.tensor_copy(h2h[:, k, c], full[n % 2][:]).then_inc(hi, 1)
                dve.wait_ge(hi, n0 + n + 1)
                V.tensor_tensor(h2l[:, k, c], full[n % 2][:], h2h[:, k, c].bitcast(F32), ALU.subtract).then_inc(lo, 1)
            dve.wait_ge(tr, n0 + 2 * KD)
            V.memset(acc[:], 0.0)
            links.append(ch.n)

        @block.tensor
        def _(pe):
            for n in range(2 * KD):
                k, g = divmod(n, 2)
                pe.wait_ge(xn, half * NT + 4 * g + 4)
                if n >= 4:
                    pe.wait_ge(fu, n0 + n - 3)
                for j in range(4):
                    last = nc.tensor.transpose(ps[n % 4][:, j * P:(j + 1) * P], acc[:, 4 * g + j, bass.ds(k, P, step=KD)], S.ident[:])
                last.then_inc(tr, 1)

        ctxb.close()
        ffn_blocks(nc, S, q, half, w_up, w_dn, uraw, uh, ul, draw, dh, dl, h2h, h2l, ah, al, gs, cv, full, halo, cw, cj, acc)

        ctxb = ExitStack()
        block = ctxb.enter_context(nc.Block())

        @block.sync
        def _(sp):
            sp.dma_start(gt[:], S.gates[1:2, :].to_broadcast([P, D])).then_inc(ld_b, 16)
            sp.dma_start(gf[:], I["g_norm_final"].rearrange("(a d) -> a d", a=1).to_broadcast([P, D])).then_inc(ld_b, 16)
            for j in range(NT):
                if j >= 2:
                    sp.wait_ge(t1, half * NT + j - 1)
                if j >= 1:
                    sp.wait_ge(ld_r, 16 * (half * NT + j))
                sp.dma_start(xr[j % 2][:], S.x1[t0 + j * P:t0 + (j + 1) * P, :]).then_inc(ld_r, 16)
            for j in range(NT):
                sp.wait_ge(oo_r, half * NT + j + 1)
                sp.dma_start(I["out"][0, t0 + j * P:t0 + (j + 1) * P, :], acc[:, j]).then_inc(o_st, 16)
            sp.wait_ge(o_st, 16 * NT * (half + 1))

        @block.scalar
        def _(act):
            for j in range(NT):
                act.wait_ge(t1, half * NT + j + 1)
                nc.scalar.activation(junk2[:], acc[:, j], ACT.Square, accum_out=st[:, 0, j:j + 1]).then_inc(sq2, 1)
                act.wait_ge(sq2, half * NT + j + 1)
            act.wait_ge(root_in2, half + 1)
            nc.scalar.activation(st[:, 1], st[:, 3], ACT.Sqrt).then_inc(root2, 1)

        @block.vector
        def _(dve):
            V = nc.vector
            ch = Chain(dve, dch)
            ch.n = links[-1]
            dve.wait_ge(ld_b, 32 * (half + 1))
            for j in range(NT):
                ch.link(V.tensor_tensor(acc[:, j], acc[:, j], gt[:], ALU.mult))
                dve.wait_ge(ld_r, 16 * (half * NT + j + 1))
                V.tensor_tensor(acc[:, j], acc[:, j], xr[j % 2][:], ALU.add).then_inc(t1, 1)
            dve.wait_ge(sq2, NT * (half + 1))

            def half_root(out, r):
                V.tensor_copy(st[:, 3], r).then_inc(root_in2, 1)
                dve.wait_ge(root2, half + 1)

            rstd_steps(nc, ch.link, st[:, 1], st[:, 0], (st[:, 2], st[:, 4]), half_root)
            for j in range(NT):
                V.scalar_tensor_tensor(acc[:, j], acc[:, j], st[:, 1, j:j + 1], gf[:], ALU.mult, ALU.mult).then_inc(oo_r, 1)
            links.append(ch.n)

        ctxb.close()
    ctx.close()


def ffn_blocks(nc, S, q, half, w_up, w_dn, uraw, uh, ul, draw, dh, dl, h2h, h2l, ah, al, gs, cv, full, halo, cw, cj, acc):
    ps = S.ps
    NT = TF // P
    j0 = half * NF
    V, A, T, Q = nc.vector, nc.scalar, nc.tensor, nc.gpsimd
    ctx = ExitStack()
    block = ctx.enter_context(nc.Block())
    NO = 2 * NT

    @block.sync
    def _(sp):
        def load(j, b, first):
            if not first:
                sp.wait_ge(q["uhi"], j0 + j - 1)
                sp.wait_ge(q["ulo"], j0 + j - 1)
            c = j * P
            for part in range(2):
                sp.dma_start(uraw[b][:, :, part, :], w_up[:, :, bass.ds(part * D_FF + c, P)]).then_inc(q[f"ldu{b}"], 16)
            if not first:
                sp.wait_ge(q["dhi"], j0 + j - 1)
                sp.wait_ge(q["dlo"], j0 + j - 1)
            sp.dma_start(draw[b][:], w_dn[bass.ds(c, P), :]).then_inc(q[f"ldd{b}"], 16)

        load(0, 0, True)
        load(1, 1, True)
        with sp.Fori(1, NF // 2) as it:
            load(2 * it, 0, False)
            load(2 * it + 1, 1, False)

    @block.scalar
    def _(act):
        def uhi(j, b, it, guard):
            act.wait_ge(q[f"ldu{b}"], 32 * (it + 1 + j0 // 2))
            if guard:
                act.wait_ge(q["upv"], 2 * (j0 + j - 1))
            A.copy(uh[b][:], uraw[b][:]).then_inc(q["uhi"], 1)

        def dhi(j, b, it, guard):
            act.wait_ge(q[f"ldd{b}"], 16 * (it + 1 + j0 // 2))
            if guard:
                act.wait_ge(q["dmm"], NO * (j0 + j - 1))
            A.copy(dh[b][:], draw[b][:]).then_inc(q["dhi"], 1)

        def hidden(j, b, guard):
            for t in range(2):
                ts = slice(t * 512, (t + 1) * 512)
                act.wait_ge(q["upg"], 2 * (j0 + j) + t + 1)
                if t == 0 and (guard or b):
                    act.wait_ge(q["cvd"], 2 * (j0 + j))
                    act.wait_ge(q["hal"], j0 + j)
                A.copy(gs[:, 2 + t * 512:2 + (t + 1) * 512], ps[t][:]).then_inc(q["gev"], 1)
            for t in range(2):
                act.wait_ge(q["cvd"], 2 * (j0 + j) + t + 1)
                A.activation(cv[t][:], cv[t][:], ACT.Silu, bias=cj[b][:, 3:4]).then_inc(q["sil"], 1)
            for t in range(2):
                ts = slice(t * 512, (t + 1) * 512)
                act.wait_ge(q["prod"], 2 * (j0 + j) + t + 1)
                if guard:
                    act.wait_ge(q["dmm"], NO * (j0 + j - 1))
                A.copy(ah[b][:, ts], full[t][:]).then_inc(q["vhi"], 1)

        uhi(0, 0, 0, False)
        uhi(1, 1, 0, False)
        dhi(0, 0, 0, False)
        dhi(1, 1, 0, False)
        hidden(0, 0, False)
        with act.Fori(1, NF // 2) as it:
            uhi(2 * it, 0, it, True)
            hidden(2 * it - 1, 1, True)
            uhi(2 * it + 1, 1, it, True)
            dhi(2 * it, 0, it, True)
            hidden(2 * it, 0, True)
            dhi(2 * it + 1, 1, it, True)
        hidden(NF - 1, 1, True)

    @block.gpsimd
    def _(pool):
        def lows(j, b):
            pool.wait_ge(q["uhi"], j0 + j + 1)
            Q.tensor_tensor(ul[b][:], uraw[b][:], uh[b][:].bitcast(F32), ALU.subtract).then_inc(q["ulo"], 1)
            pool.wait_ge(q["dhi"], j0 + j + 1)
            Q.tensor_tensor(dl[b][:], draw[b][:], dh[b][:].bitcast(F32), ALU.subtract).then_inc(q["dlo"], 1)

        lows(0, 0)
        lows(1, 1)
        with pool.Fori(1, NF // 2) as it:
            lows(2 * it, 0)
            lows(2 * it + 1, 1)

    @block.vector
    def _(dve):
        def adds(j):
            for i in range(NO):
                t, r = divmod(i, 2)
                dve.wait_ge(q["dmm"], NO * (j0 + j) + i + 1)
                c = acc[:, t, r * 512:(r + 1) * 512]
                V.tensor_tensor(c, ps[4 + i % 4][:], c, ALU.add).then_inc(q["dad"], 1)

        def hidden(j, b, guard):
            V.tensor_copy(cj[b][:].unsqueeze(2), cw[:].rearrange("p (i j) -> p i j", j=NF)[:, :, bass.ds(j, 1)])
            V.tensor_copy(gs[:, 0:2], halo[:, bass.ds(j, 1), :]).then_inc(q["chn"], 1)
            dve.wait_ge(q["chn"], 5 * (j0 + j) + 1)
            for t in range(2):
                o = t * 512
                dve.wait_ge(q["gev"], 2 * (j0 + j) + t + 1)
                V.tensor_scalar(cv[t][:], gs[:, o:o + 512], cj[b][:, 0:1], None, ALU.mult).then_inc(q["chn"], 1)
                dve.wait_ge(q["chn"], 5 * (j0 + j) + 2 + 2 * t)
                V.scalar_tensor_tensor(cv[t][:], gs[:, o + 1:o + 513], cj[b][:, 1:2], cv[t][:], ALU.mult, ALU.add).then_inc(q["chn"], 1)
                dve.wait_ge(q["chn"], 5 * (j0 + j) + 3 + 2 * t)
                V.scalar_tensor_tensor(cv[t][:], gs[:, o + 2:o + 514], cj[b][:, 2:3], cv[t][:], ALU.mult, ALU.add).then_inc(q["cvd"], 1)
            V.tensor_copy(halo[:, bass.ds(j, 1), :], gs[:, TF:TF + 2]).then_inc(q["hal"], 1)
            for t in range(2):
                dve.wait_ge(q["sil"], 2 * (j0 + j) + t + 1)
                dve.wait_ge(q["upv"], 2 * (j0 + j) + t + 1)
                V.tensor_tensor(full[t][:], ps[2 + t][:], cv[t][:], ALU.mult).then_inc(q["prod"], 1)
            for t in range(2):
                ts = slice(t * 512, (t + 1) * 512)
                dve.wait_ge(q["vhi"], 2 * (j0 + j) + t + 1)
                V.tensor_tensor(al[b][:, ts], full[t][:], ah[b][:, ts].bitcast(F32), ALU.subtract).then_inc(q["vlo"], 1)

        hidden(0, 0, False)
        with dve.Fori(1, NF // 2) as it:
            adds(2 * it - 2)
            hidden(2 * it - 1, 1, True)
            adds(2 * it - 1)
            hidden(2 * it, 0, True)
        adds(NF - 2)
        hidden(NF - 1, 1, True)
        adds(NF - 1)

    @block.tensor
    def _(pe):
        def up(j, b, first):
            pe.wait_ge(q["ulo"], j0 + j + 1)
            for part, name, free in ((1, "upg", "gev"), (0, "upv", "prod")):
                for t in range(2):
                    if not first:
                        pe.wait_ge(q[free], 2 * (j0 + j) - 1 + t)
                    for k in range(KD):
                        ts = slice(t * 512, (t + 1) * 512)
                        last = three(nc, ps[(2 if part == 0 else 0) + t][:], uh[b][:, k, part, :], ul[b][:, k, part, :],
                                     h2h[:, k, ts], h2l[:, k, ts], k == 0, k == KD - 1)
                    last.then_inc(q[name], 1)

        def down(j, b, first):
            pe.wait_ge(q["vlo"], 2 * (j0 + j) + 2)
            pe.wait_ge(q["dlo"], j0 + j + 1)
            for i in range(NO):
                t, r = divmod(i, 2)
                if not (first and i < 4):
                    pe.wait_ge(q["dad"], NO * (j0 + j) + i - 3)
                ts, rs = slice(t * P, (t + 1) * P), slice(r * 512, (r + 1) * 512)
                three(nc, ps[4 + i % 4][:], ah[b][:, ts], al[b][:, ts], dh[b][:, rs], dl[b][:, rs], True, True).then_inc(q["dmm"], 1)

        up(0, 0, True)
        up(1, 1, False)
        down(0, 0, True)
        with pe.Fori(1, NF // 2) as it:
            up(2 * it, 0, False)
            down(2 * it - 1, 1, False)
            up(2 * it + 1, 1, False)
            down(2 * it, 0, False)
        down(NF - 1, 1, False)

    ctx.close()


class Shared:
    pass


def build(nc, I, debug=None):
    S = Shared()
    base = (nc.sbuf_base + 63) // 64 * 64
    slab = nc.alloc_sbuf_tensor("slab", [P, (SBUF_BYTES + 64) // 4], F32)
    S.map = Place(nc, base)
    ctx = ExitStack()
    S.sem = lambda name: ctx.enter_context(nc.semaphore(name))
    S.ps = [nc.alloc_psum_tensor(f"bank{i}", [P, 512], F32) for i in range(8)]
    at = S.map.at
    S.ident = at("ident", 0, [P, P])
    S.swap = at("swap", 0.5, [P, P])
    S.ones = at("ones", 1, [P, P])
    S.a1, S.b1, S.a2, S.b2 = (at(n, 1.5 + 0.0625 * i, [P, KD]) for i, n in enumerate(("a1", "b1", "a2", "b2")))
    S.rad8 = at("rad8", 2, [P, G])
    S.pt = at("pt", 6, [P, 4, HALO + SEQ])
    S.yt = at("yt", 39, [P, 4, SEQ])
    kind = "ExternalOutput" if debug else None

    def dram(name, shape):
        if debug is not None and name in debug:
            return debug[name]
        return nc.dram_tensor(name, list(shape), F32).ap()

    S.u = dram("u_scratch", (SEQ, SSM_W))
    S.x1 = dram("x1_scratch", (SEQ, D))
    S.kpad = dram("kpad", (G, H, 240))
    S.mats = dram("mats", (P, 3, G * P))
    S.tabs = dram("tabs", (P, 2, G * NCH))
    S.gates = dram("gates", (2, D))
    prepare(nc, S, I)
    project(nc, S, I)
    scan(nc, S, I)
    mix(nc, S, I)
    ffn(nc, S, I)
    ctx.close()


_INS = ["x", "c", "w_ada", "b_ada", "g_norm_mix", "w_in", "ssm_lam_re", "ssm_lam_im", "ssm_log_dt", "ssm_b_re",
        "ssm_b_im", "ssm_c_re", "ssm_c_im", "ssm_d", "w_glu", "b_glu", "w_pool", "b_pool", "pool_scale", "w_out",
        "g_norm_ffn", "w_up", "w_conv", "b_conv", "w_down", "g_norm_final"]


def kernel(**inputs):
    import numpy as _np
    import concourse.bacc as _bacc
    from concourse import mybir as _mybir
    from concourse.bass_utils import run_bass_kernel_spmd as _run

    nc = _bacc.Bacc("TRN2", target_bir_lowering=False, num_devices=1)
    arrays, handles = {}, {}
    for name in _INS:
        a = _np.ascontiguousarray(inputs[name])
        arrays[f"in_{name}"] = a
        handles[name] = nc.dram_tensor(f"in_{name}", a.shape, _mybir.dt.from_np(a.dtype), kind="ExternalInput").ap()
    handles["out"] = nc.dram_tensor("out_0", (1, SEQ, D), _mybir.dt.float32, kind="ExternalOutput").ap()
    build(nc, handles)
    r = _run(nc, [arrays], core_ids=[0])
    return r.results[0]["out_0"]
```

```python
import math
from contextlib import ExitStack

import numpy as np

import concourse.bass as bass
from concourse import mybir

F32 = mybir.dt.float32
F32R = mybir.dt.float32r
BF16 = mybir.dt.bfloat16
I32 = mybir.dt.int32
ALU = mybir.AluOpType
ACT = mybir.ActivationFunctionType

P = 128
D = 1024
SEQ = 2048
KD = D // P
SSM_W = 512
POOL_W = 512
G, H, NS = 32, 16, 64
CH = 8
HALF = SEQ // 2
NCH = HALF // CH
QG = 4
NQ = G // QG
WINDOWS = (2, 4, 8, 16)
HALO = 16
D_FF = 2816
NF = D_FF // P
TM = 256
TA = 256
TF = 1024
NP = SEQ // TF
EPS = 1e-6
MULT = [1, 2, 3, 4, 5, 6, 7, 8, 16, 32, 64, 128, 256, 512]
NM = len(MULT)

TWO_PI_PARTS = (6.28125, 0.0019350051879882812, 3.0198272e-07)
LN2_PARTS = (0.693359375, -2.12194440e-4)
ROUND = 12582912.0


class Chain:

    def __init__(self, eng, sem):
        self.eng, self.sem, self.n = eng, sem, 0

    def link(self, ins):
        self.n += 1
        ins.then_inc(self.sem, 1)
        self.eng.wait_ge(self.sem, self.n)

    def done(self, ins, sem, n):
        ins.then_inc(sem, 1)
        self.eng.wait_ge(sem, n)


class Place:

    def __init__(self, nc, base):
        self.nc, self.base = nc, base

    def at(self, name, kib, shape, dtype=F32):
        size = int(np.prod(shape[1:])) * (2 if dtype == BF16 else 4)
        assert kib * 1024 + size <= SBUF_BYTES, name
        return self.nc.alloc_sbuf_tensor_at(name, list(shape), dtype, offset=self.base + int(kib * 1024))


SBUF_BYTES = 212000


def three(nc, out, wh, wl, xh, xl, first, last):
    nc.tensor.matmul(out, wh, xh, start=first, stop=False)
    nc.tensor.matmul(out, wh, xl, start=False, stop=False)
    return nc.tensor.matmul(out, wl, xh, start=False, stop=last)


def prepare(nc, S, I):
    m = S.map
    ps = S.ps
    sem = S.sem
    ctx = ExitStack()
    kern = m.at("kern", 3, [H, G, P])
    zpad = m.at("zpad", 19, [H, G, 112])
    b_in = [m.at(f"b_in{i}", 59.25 + 2 * i, [P, G, H]) for i in range(2)]
    c_rows = m.at("c_rows", 63.25, [P, 2, 4, 2 * NS])
    c_t = m.at("c_t", 67.25, [P, 2, G, H])
    t5 = [m.at(f"t5_{i}", 71.25 + 2 * i, [P, G, H]) for i in range(2)]
    lam_rows = m.at("lam_rows", 75.25, [G, 2, 2 * NS])
    x9 = m.at("x9", 77.25, [P, 9, G])
    y9 = m.at("y9", 78.5, [P, 9, G])
    x8 = m.at("x8", 79.75, [P, 8, G])
    y8 = m.at("y8", 80.75, [P, 8, G])
    gcol = m.at("norm_g", 81.75, [P, KD])
    csb = m.at("c_in", 82, [P, KD])
    d_t = m.at("d_t", 82.75, [H, G])
    sn, cs = S.sn, S.cs
    lam = m.at("lam", 87, [P, 2, G])
    dt = m.at("dt", 87.5, [P, G])
    ex = [m.at(f"exp_t{i}", 88 + 1.0 * i, [P, 8 * G]) for i in range(4)]
    exi = m.at("exp_i", 92, [P, 8 * G], I32)
    mag = m.at("mag", 93, [P, 8, G])
    magin = m.at("magin", 94, [P, 8, G])
    ang = m.at("ang", 95, [P, NM, G])
    angn = m.at("angn", 97, [P, NM, G])
    lc = m.at("lc", 99, [P, 8, G])
    ls = m.at("ls", 100, [P, 8, G])
    wre = m.at("wre", 101, [P, 8, G])
    wim = m.at("wim", 102, [P, 8, G])
    sm = [m.at(f"sm{i}", 103 + 0.25 * i, [P, G]) for i in range(8)]
    tw = [m.at(f"tw{i}", 105 + 1.0 * i, [P, 8, G]) for i in range(2)]
    ekern = m.at("ekern", 107, [H, G, H])
    t5p = [m.at(f"t5p_{i}", 109 + 2 * i, [P, G, H]) for i in range(2)]
    isb = m.at("isb", 119, [P, G, P])
    cl = m.at("cl", 135, [P, G, 9, H])
    wt = [m.at(f"ada_w{i}", 153 + 8 * i, [P, 2048]) for i in range(2)]
    brow = m.at("ada_brow", 169, [1, 2048])
    arow = m.at("ada_row", 177, [1, 2048])
    it = m.at("it", 185, [P, G, CH, H])
    csl = S.csl

    ld_c, ld_small, ld_w, ld_g = sem("p_ld_c"), sem("p_ld_small"), [sem("p_ld_w0"), sem("p_ld_w1")], sem("p_ld_g")
    c_ready, w_used = sem("p_c_ready"), sem("p_w_used")
    dch, pch, ach = sem("p_dch"), sem("p_pch"), sem("p_ach")
    id_ready, lamt, ct_ready, ang_ready, sin_ready = sem("p_id"), sem("p_lamt"), sem("p_ct"), sem("p_ang"), sem("p_sin")
    ct_copied, it_ready, itt, it_copied = sem("p_ctc"), sem("p_it"), sem("p_itt"), sem("p_itc")
    kr, kr_copied, kr_done, cl_ready = sem("p_kr"), sem("p_krc"), sem("p_krd"), sem("p_cl")
    row_out, col_mm, zp_ready, xy_ready = (sem("p_" + n) for n in ("row", "colmm", "zp", "xy"))
    ld_b = sem("p_ldb")

    it_ready_d = sem("p_itd")
    w_ada = I["w_ada"][0].rearrange("(p k) n -> p k n", k=KD)
    SP_TOK = 3
    junk = m.at("p_junk", 113, [P, D], BF16)

    block = ctx.enter_context(nc.Block())

    @block.sync
    def _(sp):
        sp.dma_start(csb[:], I["c"][0].rearrange("(p k) -> p k", k=KD)).then_inc(ld_c, 16)
        sp.dma_start(brow[:], I["b_ada"][0:1, 0:2048]).then_inc(ld_b, 16)
        for k in range(KD):
            if k >= 2:
                sp.wait_ge(w_used, k - 1)
            sp.dma_start(wt[k % 2][:], w_ada[:, k, 0:2048]).then_inc(ld_w[k % 2], 16)
        for b in range(2):
            sp.dma_start(S.xb[b][:], S.x_v[b]).then_inc(S.ld_x[b], 16)
        for k in range(2):
            sp.dma_start(S.wraw[k][:], S.w_in[:, k, :]).then_inc(S.ld_w[k], 16)

    @block.scalar
    def _(act):
        d = act.dma_start
        for i, name in enumerate(("ssm_lam_re", "ssm_lam_im")):
            for dup in range(2):
                d(lam_rows[:, i, dup * NS:(dup + 1) * NS], I[name][0]).then_inc(ld_small, 16)
        d(dt[:], I["ssm_log_dt"][0:1, :].to_broadcast([P, G])).then_inc(ld_small, 16)
        for i, name in enumerate(("ssm_b_re", "ssm_b_im")):
            for dup in range(2):
                d(b_in[i][dup * NS:(dup + 1) * NS], I[name][0].rearrange("g p h -> p g h")).then_inc(ld_small, 16)
        for i, name in enumerate(("ssm_c_re", "ssm_c_im")):
            for dup in range(2):
                d(c_rows[:, i, :, dup * NS:(dup + 1) * NS],
                  I[name][0].rearrange("(a g) h p -> (g h) a p", a=4)).then_inc(ld_small, 16)
        d(d_t[:], I["ssm_d"][0].rearrange("(g h) -> h g", h=H), allow_slow_non_contiguous=True).then_inc(ld_small, 16)
        d(gcol[:], I["g_norm_mix"][0].rearrange("(p k) -> p k", k=KD)).then_inc(ld_g, 16)
        d(S.g_ffn[:], I["g_norm_ffn"][0].rearrange("(p k) -> p k", k=KD)).then_inc(ld_g, 16)
        act.wait_ge(ld_c, 16)
        nc.scalar.activation(csl[:], csb[:], ACT.Silu).then_inc(c_ready, 1)
        act.wait_ge(ang_ready, 1)
        nc.scalar.activation(sn[:], ang[:], ACT.Sin).then_inc(sin_ready, 1)
        nc.scalar.activation(cs[:], ang[:], ACT.Sin, scale=0.5).then_inc(sin_ready, 1)
        for i in range(2):
            act.wait_ge(ct_ready, 4 * (i + 1))
            nc.scalar.copy(c_t[:, i].rearrange("p g h -> p (g h)"), ps[1 + i][:]).then_inc(ct_copied, 1)
        act.wait_ge(zp_ready, 1)
        d(S.kpad[:, :, 0:112].rearrange("g h n -> h g n"), zpad[:]).then_inc(S.kpad_st, 16)

        act.wait_ge(w_used, KD)
        for i in range(4):
            last = nc.scalar.copy(arow[0:1, i * 512:(i + 1) * 512], ps[4 + i][0:1, :])
        last.then_inc(row_out, 1)
        for q in range(NQ):
            act.wait_ge(itt, 4 * (q + 1))
            nc.scalar.copy(isb[:, 4 * q:4 * q + 4, :].rearrange("p g n -> p (g n)"), ps[q % 2][:]).then_inc(it_copied, 1)
        act.wait_ge(it_copied, NQ)
        d(S.mats[:, 0, :], isb[:].rearrange("p g n -> p (g n)")).then_inc(S.mats_st, 16)
        act.wait_ge(cl_ready, 9)
        d(S.mats[:, 1, :].rearrange("p (g n) -> p g n", g=G), cl[:, :, 1:9, :].rearrange("p g t h -> p g (t h)")).then_inc(S.mats_st, 16)
        squares(nc, S, act, 0, junk)
        for q in range(NQ):
            act.wait_ge(kr, 4 * (q + 1))
            nc.scalar.copy(kern[:, 4 * q:4 * q + 4, :].rearrange("p g n -> p (g n)"), ps[2 + q % 2][0:H, :]).then_inc(kr_copied, 1)
        act.wait_ge(kr_done, 1)
        d(S.kpad[:, :, 112:240].rearrange("g h n -> h g n"), kern[:]).then_inc(S.kpad_st, 16)

    @block.gpsimd
    def _(pool):
        ch = Chain(pool, pch)
        nc.gpsimd.memset(S.ones[:], 1.0).then_inc(id_ready, 1)
        nc.gpsimd.memset(zpad[:], 0.0).then_inc(zp_ready, 1)
        ch.link(nc.gpsimd.memset(S.ident[:], 0.0))
        ch.link(nc.gpsimd.memset(S.swap[:], 0.0))
        nc.gpsimd.affine_select(out=S.ident[:], in_=S.ident[:], compare_op=ALU.not_equal, fill=1.0, base=0,
                                pattern=[[-1, P]], channel_multiplier=1).then_inc(id_ready, 1)
        ch.link(nc.gpsimd.affine_select(out=S.swap[:], in_=S.swap[:], compare_op=ALU.not_equal, fill=1.0, base=-NS,
                                        pattern=[[-1, P]], channel_multiplier=1))
        nc.gpsimd.affine_select(out=S.swap[:], in_=S.swap[:], compare_op=ALU.not_equal, fill=-1.0, base=NS,
                                pattern=[[-1, P]], channel_multiplier=1).then_inc(id_ready, 1)
        TT = nc.gpsimd.tensor_tensor
        pool.wait_ge(ld_small, 16 * 14)
        pool.wait_ge(xy_ready, 1)
        for s in range(SP_TOK, CH):
            k = CH - 1 - s
            ch.link(TT(t5p[0][:], b_in[0][:], x8[:, k, :].unsqueeze(2).to_broadcast([P, G, H]), ALU.mult))
            ch.link(TT(t5p[1][:], b_in[1][:], y8[:, k, :].unsqueeze(2).to_broadcast([P, G, H]), ALU.mult))
            ch.done(TT(it[:, :, s, :], t5p[0][:], t5p[1][:], ALU.add), it_ready, s - SP_TOK + 1)

    @block.vector
    def _(dve):
        ch = Chain(dve, dch)
        L = ch.link
        V = nc.vector
        TT, TS, STT = V.tensor_tensor, V.tensor_scalar, V.scalar_tensor_tensor

        def expf(out, x, n):
            t, k, r, p = (e[:, 0:n] for e in ex)
            L(TS(x, x, 88.0, -87.0, ALU.min, ALU.max))
            L(TS(t, x, 1.0 / math.log(2.0), ROUND, ALU.mult, ALU.add))
            L(TS(k, t, -ROUND, None, ALU.add))
            L(STT(r, k, -LN2_PARTS[0], x, ALU.mult, ALU.add))
            L(STT(r, k, -LN2_PARTS[1], r, ALU.mult, ALU.add))
            L(TS(p, r, 1.0 / 5040, None, ALU.mult))
            for c in (720, 120, 24, 6, 2, 1):
                L(STT(p, p, 1.0 / c, r, ALU.add, ALU.mult))
            L(TS(t, k, 127.0, 8388608.0, ALU.add, ALU.mult))
            L(V.tensor_copy(exi[:, 0:n], t))
            L(STT(out, p, 1.0, exi[:, 0:n].bitcast(F32), ALU.add, ALU.mult))

        dve.wait_ge(ld_small, 16 * 14)
        dve.wait_ge(lamt, 2)
        L(V.tensor_copy(lam[:].rearrange("p i g -> p (i g)"), ps[0][:, 0:2 * G]))
        L(V.tensor_copy(sm[7][:], dt[:]))
        expf(dt[:], sm[7][:], G)
        L(TT(sm[0][:], lam[:, 0], dt[:], ALU.mult))
        L(TT(sm[1][:], lam[:, 1], dt[:], ALU.mult))
        for tau in range(8):
            TS(magin[:, tau], sm[0][:], float(tau + 1), None, ALU.mult)
        for i, mu in enumerate(MULT):
            last = TS(ang[:, i], sm[1][:], float(mu), None, ALU.mult)
        L(last)
        L(TS(angn[:], ang[:], 1.0 / (2 * math.pi), ROUND, ALU.mult, ALU.add))
        L(TS(angn[:], angn[:], -ROUND, None, ALU.add))
        for c in TWO_PI_PARTS:
            L(STT(ang[:], angn[:], -c, ang[:], ALU.mult, ALU.add))
        ch.done(TS(ang[:], ang[:], 3.1415925, -3.1415925, ALU.min, ALU.max), ang_ready, 1)
        expf(mag[:].rearrange("p t g -> p (t g)"), magin[:].rearrange("p t g -> p (t g)"), 8 * G)
        dve.wait_ge(sin_ready, 2)
        L(TT(cs[:], cs[:], cs[:], ALU.mult))
        L(TS(cs[:], cs[:], -2.0, 1.0, ALU.mult, ALU.add))
        L(V.tensor_copy(S.rad8[:], mag[:, 7]))
        L(TT(lc[:], mag[:], cs[:, 0:8], ALU.mult))
        L(TT(ls[:], mag[:], sn[:, 0:8], ALU.mult))
        lre, lim = lam[:, 0], lam[:, 1]
        L(TT(sm[0][:], lre, lre, ALU.mult))
        L(TT(sm[1][:], lim, lim, ALU.mult))
        L(TT(sm[0][:], sm[0][:], sm[1][:], ALU.add))
        L(V.reciprocal(sm[1][:], sm[0][:]))
        L(TS(sm[2][:], lc[:, 0], -1.0, None, ALU.add))
        L(TT(sm[3][:], sm[2][:], lre, ALU.mult))
        L(TT(sm[4][:], ls[:, 0], lim, ALU.mult))
        L(TT(sm[3][:], sm[3][:], sm[4][:], ALU.add))
        L(TT(wre[:, 0], sm[3][:], sm[1][:], ALU.mult))
        L(TT(sm[3][:], ls[:, 0], lre, ALU.mult))
        L(TT(sm[4][:], sm[2][:], lim, ALU.mult))
        L(TT(sm[3][:], sm[3][:], sm[4][:], ALU.subtract))
        L(TT(wim[:, 0], sm[3][:], sm[1][:], ALU.mult))
        wr0 = wre[:, 0:1, :].to_broadcast([P, 7, G])
        wi0 = wim[:, 0:1, :].to_broadcast([P, 7, G])
        a, b = tw[0][:, 0:7], tw[1][:, 0:7]
        L(TT(a, lc[:, 0:7], wr0, ALU.mult))
        L(TT(b, ls[:, 0:7], wi0, ALU.mult))
        L(TT(wre[:, 1:8], a, b, ALU.subtract))
        L(TT(a, lc[:, 0:7], wi0, ALU.mult))
        L(TT(b, ls[:, 0:7], wr0, ALU.mult))
        L(TT(wim[:, 1:8], a, b, ALU.add))
        re, im = slice(0, NS), slice(NS, P)
        V.tensor_copy(x8[re], wre[re])
        V.tensor_copy(x8[im], wim[im])
        TS(y8[re], wim[re], -1.0, None, ALU.mult)
        V.tensor_copy(y8[im], wre[im]).then_inc(xy_ready, 1)
        V.tensor_copy(x9[re, 1:9], lc[re])
        TS(x9[im, 1:9], ls[im], -1.0, None, ALU.mult)
        TS(y9[re, 1:9], ls[re], -1.0, None, ALU.mult)
        TS(y9[im, 1:9], lc[im], -1.0, None, ALU.mult)
        V.memset(x9[re, 0], 1.0)
        V.memset(x9[im, 0], 0.0)
        V.memset(y9[re, 0], 0.0)
        L(V.memset(y9[im, 0], -1.0))
        dve.wait_ge(ct_copied, 2)
        for tau in range(9):
            L(TT(t5[0][:], c_t[:, 0], x9[:, tau, :].unsqueeze(2).to_broadcast([P, G, H]), ALU.mult))
            L(TT(t5[1][:], c_t[:, 1], y9[:, tau, :].unsqueeze(2).to_broadcast([P, G, H]), ALU.mult))
            ch.done(TT(cl[:, :, tau, :], t5[0][:], t5[1][:], ALU.add), cl_ready, tau + 1)

        for s in range(SP_TOK):
            k = CH - 1 - s
            L(TT(t5[0][:], b_in[0][:], x8[:, k, :].unsqueeze(2).to_broadcast([P, G, H]), ALU.mult))
            L(TT(t5[1][:], b_in[1][:], y8[:, k, :].unsqueeze(2).to_broadcast([P, G, H]), ALU.mult))
            ch.done(TT(it[:, :, s, :], t5[0][:], t5[1][:], ALU.add), it_ready_d, s + 1)

        dve.wait_ge(ld_g, 32)
        dve.wait_ge(col_mm, 1)
        V.tensor_copy(S.b1[:], ps[4][:, 0:KD])
        STT(S.a1[:], ps[4][:, KD:2 * KD], 1.0, gcol[:], ALU.add, ALU.mult)

        normalise(nc, S, dve, L, 0)

        dve.wait_ge(kr_copied, NQ)
        L(TT(ekern[:], S.ident[0:H, 0:H].unsqueeze(1).to_broadcast([H, G, H]),
             d_t[:].unsqueeze(2).to_broadcast([H, G, H]), ALU.mult))
        TT(kern[:, :, 0:H], kern[:, :, 0:H], ekern[:], ALU.add).then_inc(kr_done, 1)

    @block.tensor
    def _(pe):
        T = nc.tensor
        pe.wait_ge(id_ready, 3)
        pe.wait_ge(ld_small, 16 * 14)
        for i in range(2):
            T.transpose(ps[0][:, i * G:(i + 1) * G], lam_rows[:, i, :], S.ident[0:G, 0:G]).then_inc(lamt, 1)
        for i in range(2):
            for a in range(4):
                T.transpose(ps[1 + i][:, a * P:(a + 1) * P], c_rows[:, i, a, :], S.ident[:]).then_inc(ct_ready, 1)

        pe.wait_ge(c_ready, 1)
        pe.wait_ge(ld_b, 16)
        for i in range(4):
            T.matmul(ps[4 + i][0:1, :], S.ones[0:1, 0:1], brow[0:1, i * 512:(i + 1) * 512], start=True, stop=False)
        for k in range(KD):
            pe.wait_ge(ld_w[k % 2], 16 * (k // 2 + 1))
            for i in range(4):
                last = T.matmul(ps[4 + i][0:1, :], csl[:, k:k + 1], wt[k % 2][:, i * 512:(i + 1) * 512], start=False, stop=k == KD - 1)
            last.then_inc(w_used, 1)
        pe.wait_ge(row_out, 1)
        for k in range(2 * KD):
            last = T.matmul(ps[4][:, k:k + 1], arow[0:1, bass.ds(k // KD * D + k % KD, P, step=KD)], S.ones[0:1, 0:1], start=True, stop=True)
        last.then_inc(col_mm, 1)
        pe.wait_ge(ct_copied, 2)
        pe.wait_ge(it_ready, CH - SP_TOK)
        pe.wait_ge(it_ready_d, SP_TOK)
        for q in range(NQ):
            if q >= 2:
                pe.wait_ge(it_copied, q - 1)
            for g in range(4 * q, 4 * q + 4):
                T.transpose(ps[q % 2][:, (g % 4) * P:(g % 4 + 1) * P], it[:, g].rearrange("p s h -> p (s h)"),
                            S.ident[:]).then_inc(itt, 1)
        pe.wait_ge(cl_ready, 9)
        for q in range(NQ):
            if q >= 2:
                pe.wait_ge(kr_copied, q - 1)
            for g in range(4 * q, 4 * q + 4):
                T.matmul(ps[2 + q % 2][0:H, (g % 4) * P:(g % 4 + 1) * P], it[:, g, CH - 1, :],
                         cl[:, g, 0:8, :].rearrange("p t h -> p (t h)"), start=True, stop=True).then_inc(kr, 1)

    ctx.close()


def rstd_steps(nc, link, out, ss, tmp, half_root):
    V = nc.vector
    m, r = tmp
    link(V.tensor_scalar(m, ss, 1.0 / D, EPS, ALU.mult, ALU.add))
    link(V.reciprocal(r, m))
    half_root(out, r)
    link(V.tensor_tensor(r, out, out, ALU.mult))
    link(V.tensor_tensor(r, r, m, ALU.mult))
    link(V.tensor_scalar(r, r, -0.5, 1.5, ALU.mult, ALU.add))
    link(V.tensor_tensor(out, out, r, ALU.mult))


def squares(nc, S, act, b, junk):
    NJ = TA // P
    act.wait_ge(S.ld_x[b % 2], 16 * (b // 2 + 1))
    if b:
        act.wait_ge(S.xn, NJ * b)
    for j in range(NJ):
        nc.scalar.activation(junk[:], S.xb[b % 2][:, j], ACT.Square, accum_out=S.st[:, 0, j:j + 1]).then_inc(S.sq, 1)
        act.wait_ge(S.sq, NJ * b + j + 1)
    act.wait_ge(S.root_in, b + 1)
    nc.scalar.activation(S.st[:, 1], S.st[:, 3], ACT.Sqrt).then_inc(S.root, 1)


def normalise(nc, S, dve, link, b):
    NJ = TA // P
    dve.wait_ge(S.sq, NJ * (b + 1))

    def half_root(out, r):
        nc.vector.tensor_copy(S.st[:, 3], r).then_inc(S.root_in, 1)
        dve.wait_ge(S.root, b + 1)

    rstd_steps(nc, link, S.st[:, 1], S.st[:, 0], (S.st[:, 2], S.st[:, 4]), half_root)
    for j in range(NJ):
        nc.vector.tensor_scalar(S.xb[b % 2][:, j], S.xb[b % 2][:, j], S.st[:, 1, j:j + 1], None, ALU.mult).then_inc(S.xn, 1)


def project(nc, S, I):
    m, ps, sem = S.map, S.ps, S.sem
    ctx = ExitStack()
    NJ = TA // P
    NBA = SEQ // TA
    xb, ld_x, ld_w, xn = S.xb, S.ld_x, S.ld_w, S.xn
    NR = 6
    wraw = S.wraw + [m.at(f"a_wraw{2 + i}", o, [P, D]) for i, o in enumerate((67.25, 71.25, 199, 203))]
    hh = [m.at(f"a_hh{i}", 59.25 + 8 * i, [P, KD, TA], F32R) for i in range(2)]
    hl = [m.at(f"a_hl{i}", (75.25, 199)[i], [P, KD, TA], F32R) for i in range(2)]
    wl = m.at("a_wl", 87, [P, KD, D], F32R)
    wh = m.at("a_wh", 153, [P, KD, D], F32R)
    usb = [m.at(f"a_u{i}", 185 + 2 * i, [P, SSM_W]) for i in range(2)]
    full = [m.at(f"a_full{i}", 189 + 1 * i, [P, TA]) for i in range(2)]
    ET = 32
    et = m.at("e_tmp", 191, [P, G, ET])
    junk = m.at("a_junk", 195, [P, D], BF16)

    whi, wlo_u, wlo_p = sem("a_whi"), sem("a_wlou"), sem("a_wlop")
    ld_w = ld_w + [sem(f"a_ld_w{i}") for i in range(2, NR)]
    tr, hi, fu, lo, mm_u, mm_p, ev_u, ev_p = (sem("a_" + n) for n in ("tr", "hi", "full", "lo", "mmu", "mmp", "ev_u", "ev_p"))
    u_st = [sem("a_ust0"), sem("a_ust1")]
    dch, pch = sem("a_dch"), sem("a_pch")
    block = ctx.enter_context(nc.Block())

    @block.sync
    def _(sp):
        for k in range(2, KD):
            if k >= NR:
                sp.wait_ge(whi, k - NR + 1)
                sp.wait_ge(wlo_u, k - NR + 1)
                sp.wait_ge(wlo_p, k - NR + 1)
            sp.dma_start(wraw[k % NR][:], S.w_in[:, k, :]).then_inc(ld_w[k % NR], 16)
        for b in range(NBA):
            if b + 2 < NBA:
                sp.wait_ge(tr, KD * (b + 1))
                sp.dma_start(xb[b % 2][:], S.x_v[b + 2]).then_inc(ld_x[b % 2], 16)
            for j in range(NJ):
                n = NJ * b + j
                sp.wait_ge(ev_u, n + 1)
                sp.dma_start(S.u[n * P:(n + 1) * P, :], usb[n % 2][:]).then_inc(u_st[n % 2], 16)
        for i in range(2):
            sp.wait_ge(u_st[i], 16 * NBA * NJ // 2)

    @block.scalar
    def _(act):
        def weights(k):
            act.wait_ge(ld_w[k % NR], 16 * (k // NR + 1))
            nc.scalar.copy(wh[:, k], wraw[k % NR][:]).then_inc(whi, 1)

        def high(b, k):
            n = KD * b + k
            act.wait_ge(tr, n + 1)
            if n >= 2:
                act.wait_ge(lo, n - 1)
            nc.scalar.activation(full[k % 2][:], ps[k % 2][:, 0:TA], ACT.Identity, bias=S.b1[:, k:k + 1],
                                 scale=S.a1[:, k:k + 1]).then_inc(fu, 1)

        def evac(b):
            for j in range(NJ):
                n = NJ * b + j
                act.wait_ge(mm_u, n + 1)
                if n >= 2:
                    act.wait_ge(u_st[n % 2], 16 * (n // 2))
                nc.scalar.copy(usb[n % 2][:], ps[2 + j][:]).then_inc(ev_u, 1)

        for k in range(KD):
            weights(k)
            high(0, k)
        squares(nc, S, act, 1, junk)
        for b in range(NBA):
            if b + 1 < NBA:
                for k in range(KD):
                    high(b + 1, k)
            evac(b)
            if b + 2 < NBA:
                squares(nc, S, act, b + 2, junk)

    @block.gpsimd
    def _(pool):
        ch = Chain(pool, pch)
        L = ch.link
        Q = nc.gpsimd
        TT = Q.tensor_tensor
        for k in range(KD):
            pool.wait_ge(whi, k + 1)
            TT(wl[:, k, SSM_W:], wraw[k % NR][:, SSM_W:], wh[:, k, SSM_W:].bitcast(F32), ALU.subtract).then_inc(wlo_p, 1)
        ec, es, cs, sn = S.ec, S.es, S.cs, S.sn
        pool.wait_ge(S.mats_st, 32)
        L(Q.tensor_copy(ec[:, :, 0], cs[:, 7]))
        L(Q.tensor_copy(es[:, :, 0], sn[:, 7]))
        w = 1
        for lev in range(7):
            for a in range(0, w, ET):
                n = min(ET, w - a)
                src, dst, t = slice(a, a + n), slice(w + a, w + a + n), et[:, :, 0:n]
                cw = cs[:, 7 + lev, :].unsqueeze(2).to_broadcast([P, G, n])
                sw = sn[:, 7 + lev, :].unsqueeze(2).to_broadcast([P, G, n])
                L(TT(ec[:, :, dst], ec[:, :, src], cw, ALU.mult))
                L(TT(t, es[:, :, src], sw, ALU.mult))
                L(TT(ec[:, :, dst], ec[:, :, dst], t, ALU.subtract))
                L(TT(es[:, :, dst], es[:, :, src], cw, ALU.mult))
                L(TT(t, ec[:, :, src], sw, ALU.mult))
                L(TT(es[:, :, dst], es[:, :, dst], t, ALU.add))
            w *= 2

    @block.vector
    def _(dve):
        V = nc.vector
        ch = Chain(dve, dch)

        def low(b, k):
            n = KD * b + k
            dve.wait_ge(fu, n + 1)
            if b >= 2:
                dve.wait_ge(mm_p, 4 * (b - 1))
            V.tensor_copy(hh[b % 2][:, k], full[k % 2][:]).then_inc(hi, 1)
            dve.wait_ge(hi, n + 1)
            V.tensor_tensor(hl[b % 2][:, k], full[k % 2][:], hh[b % 2][:, k].bitcast(F32), ALU.subtract).then_inc(lo, 1)

        def wlow(k):
            dve.wait_ge(whi, k + 1)
            V.tensor_tensor(wl[:, k, 0:SSM_W], wraw[k % NR][:, 0:SSM_W], wh[:, k, 0:SSM_W].bitcast(F32), ALU.subtract).then_inc(wlo_u, 1)

        def evac(b):
            for j in range(4):
                dve.wait_ge(mm_p, 4 * b + j + 1)
                V.tensor_copy(S.pt[:, j, HALO + b * TA:HALO + (b + 1) * TA], ps[4 + j][:, 0:TA]).then_inc(ev_p, 1)

        for k in range(KD):
            wlow(k)
            low(0, k)
        normalise(nc, S, dve, ch.link, 1)
        dve.wait_ge(S.kpad_st, 32)
        V.memset(S.pt[:, :, 0:HALO], 0.0)
        dve.wait_ge(wlo_p, KD)
        for b in range(NBA):
            if b + 1 < NBA:
                for k in range(KD):
                    low(b + 1, k)
            if b + 2 < NBA:
                normalise(nc, S, dve, ch.link, b + 2)
            evac(b)

    @block.tensor
    def _(pe):
        T = nc.tensor

        def transposes(b):
            pe.wait_ge(xn, NJ * (b + 1))
            for k in range(KD):
                n = KD * b + k
                if n >= 2:
                    pe.wait_ge(fu, n - 1)
                for j in range(NJ):
                    last = T.transpose(ps[k % 2][:, j * P:(j + 1) * P], xb[b % 2][:, j, bass.ds(k, P, step=KD)], S.ident[:])
                last.then_inc(tr, 1)

        def output_u(b, j):
            if b:
                pe.wait_ge(ev_u, NJ * (b - 1) + j + 1)
            js = slice(j * P, (j + 1) * P)
            for k in range(KD):
                if j == 0:
                    pe.wait_ge(lo, KD * b + k + 1)
                    if b == 0:
                        pe.wait_ge(wlo_u, k + 1)
                last = three(nc, ps[2 + j][:], hh[b % 2][:, k, js], hl[b % 2][:, k, js], wh[:, k, 0:SSM_W],
                             wl[:, k, 0:SSM_W], k == 0, k == KD - 1)
            last.then_inc(mm_u, 1)

        def output_p(b, j):
            if b:
                pe.wait_ge(ev_p, 4 * (b - 1) + j + 1)
            elif j == 0:
                pe.wait_ge(wlo_p, KD)
            cs = slice(SSM_W + j * P, SSM_W + (j + 1) * P)
            for k in range(KD):
                last = three(nc, ps[4 + j][:, 0:TA], wh[:, k, cs], wl[:, k, cs], hh[b % 2][:, k, :], hl[b % 2][:, k, :],
                             k == 0, k == KD - 1)
            last.then_inc(mm_p, 1)

        transposes(0)
        for b in range(NBA):
            output_u(b, 0)
            if b + 1 < NBA:
                transposes(b + 1)
            output_u(b, 1)
            for j in range(4):
                output_p(b, j)

    ctx.close()


def scan(nc, S, I):
    m, ps, sem = S.map, S.ps, S.sem
    ctx = ExitStack()
    NQ2 = 2 * NQ
    W = QG * NCH
    tm = m.at("s_t", 71, [P, G, P])
    im = m.at("s_i", 87, [P, G, P])
    om = m.at("s_o", 103, [P, G, P])
    ec, es = S.ec, S.es
    us = m.at("s_u", 151, [P, CH, SSM_W])
    yh = [m.at(f"s_y{i}", 167 + 4 * i, [P, CH, P]) for i in range(2)]
    ut = [m.at(f"s_ut{i}", 175 + 2 * i, [P, W]) for i in range(4)]
    ss = m.at("s_s", 183, [P, W])
    bb = m.at("s_b", 185, [P, QG, NCH])
    zz = [m.at(f"s_z{i}", 187 + 2 * i, [P, QG, NCH]) for i in range(2)]
    xx = [m.at(f"s_x{i}", 191 + 2.0625 * i, [P, QG, NCH + 1]) for i in range(2)]
    uq = m.at("s_uq", 195.125, [P, QG, CH, H])
    pl = [m.at(f"s_pl{i}", 197.125 + 4.0625 * i, [P, HALO + HALF]) for i in range(2)]
    carry = m.at("s_carry", 205.25, [P, G])
    rc = m.at("s_rc", 205.5, [P, 4, HALO])
    ri = m.at("s_ri", 205.75, [P, HALO], I32)
    rt = m.at("s_rt", 205.875, [P, HALO])

    ld_m, ld_u, u_q, tr_u, ut_c, s_mm, s_c, s_j, m_used, z_ready, j2, x_ready, y_mm, y_act, y_tr, y_c = (
        sem("s_" + n) for n in ("ld_m", "ld_u", "u_q", "tr_u", "ut_c", "smm", "sc", "sj", "m_used", "z_ready", "j2",
                                "x_ready", "y_mm", "y_act", "y_tr", "y_c"))
    dch, pch, count, inv_count = sem("s_dch"), sem("s_pch"), sem("s_count"), sem("s_inv")
    u_v = S.u.rearrange("(h c t) n -> h c t n", h=2, t=CH)
    block = ctx.enter_context(nc.Block())

    @block.sync
    def _(sp):
        sp.dma_start(us[:], u_v[0]).then_inc(ld_u, 16)
        sp.wait_ge(S.mats_st, 32)
        sp.dma_start(im[:].rearrange("p g n -> p (g n)"), S.mats[:, 0, :]).then_inc(ld_m, 16)
        sp.dma_start(om[:].rearrange("p g n -> p (g n)"), S.mats[:, 1, :]).then_inc(ld_m, 16)
        sp.wait_ge(S.kpad_st, 32)
        for s in range(CH):
            o = (CH - 1 - s) * H
            sp.dma_start(tm[s * H:(s + 1) * H], S.kpad[:, :, o:o + P].rearrange("g h n -> h g n")).then_inc(ld_m, 16)
        sp.dma_start(S.col[:, 0:8], I["b_glu"][0].rearrange("(k p) -> p k", p=P), allow_slow_non_contiguous=True).then_inc(S.ld_col, 16)
        sp.dma_start(S.col[:, 8:12], I["b_pool"][0].rearrange("g d -> d g"), allow_slow_non_contiguous=True).then_inc(S.ld_col, 16)
        sp.dma_start(S.col[:, 12:16], I["pool_scale"][0].rearrange("(g d) -> d g", g=4), allow_slow_non_contiguous=True).then_inc(S.ld_col, 16)
        sp.wait_ge(tr_u, NQ)
        sp.dma_start(us[:], u_v[1]).then_inc(ld_u, 16)

    def turns(flip, swap, swap_back, enter, leave, back):
        def do(step, i):
            if 0 <= i < NQ2:
                step(i)
        for i in range(-2, NQ2 + 2):
            do(flip, i + 2)
            do(swap, i + 1)
            do(swap_back, i)
            do(enter, i + 2)
            do(leave, i - 1)
            do(back, i - 2)

    @block.tensor
    def _(pe):
        T = nc.tensor

        def flip(i):
            pe.wait_ge(u_q, i + 1)
            if i:
                pe.wait_ge(ut_c, i)
            for g in range(QG):
                last = T.transpose(ps[0][:, g * P:(g + 1) * P], uq[:, g].rearrange("p t h -> p (t h)"), S.ident[:])
            last.then_inc(tr_u, 1)

        def enter(i):
            pe.wait_ge(ut_c, i + 1)
            if i:
                pe.wait_ge(m_used, i)
            for g in range(QG):
                last = T.matmul(ps[1][:, g * P:(g + 1) * P], im[:, i % NQ * QG + g, :], ut[i % 4][:, g * P:(g + 1) * P],
                                start=True, stop=True)
            last.then_inc(s_mm, 1)

        def swap(i):
            pe.wait_ge(s_c, i + 1)
            if i:
                pe.wait_ge(m_used, i)
            T.matmul(ps[2][:], S.swap[:], ss[:], start=True, stop=True).then_inc(s_j, 1)

        def swap_back(i):
            pe.wait_ge(z_ready, i + 1)
            if i:
                pe.wait_ge(x_ready, i)
            T.matmul(ps[3][:], S.swap[:], zz[i % 2][:].rearrange("p g n -> p (g n)"), start=True, stop=True).then_inc(j2, 1)

        def leave(i):
            pe.wait_ge(x_ready, i + 1)
            if i >= 2:
                pe.wait_ge(y_act, i - 1)
            for g in range(QG):
                gg = i % NQ * QG + g
                o = ps[4 + i % 2][:, g * P:(g + 1) * P]
                T.matmul(o, ut[i % 4][:, g * P:(g + 1) * P], tm[:, gg, :], start=True, stop=False)
                last = T.matmul(o, xx[i % 2][:, g, 0:NCH], om[:, gg, :], start=False, stop=True)
            last.then_inc(y_mm, 1)

        def back(i):
            if i % 2 == 0:
                return
            pe.wait_ge(y_act, i + 1)
            for r in range(2):
                if i > 1:
                    pe.wait_ge(y_c, i - 1 + r - 1)
                for t in range(4):
                    last = T.transpose(ps[6 + r][:, t * P:(t + 1) * P], yh[(i // 2) % 2][:, 4 * r + t, :], S.ident[:])
                last.then_inc(y_tr, 1)

        pe.wait_ge(ld_m, 16 * 10)
        turns(flip, swap, swap_back, enter, leave, back)

    @block.scalar
    def _(act):
        def gather(i):
            half, q = divmod(i, NQ)
            if q == 0:
                act.wait_ge(ld_u, 16 * (half + 1))
            if i:
                act.wait_ge(tr_u, i)
            c = q * QG * H
            nc.scalar.copy(uq[:], us[:, :, c:c + QG * H].rearrange("p t (g h) -> p g t h", g=QG)).then_inc(u_q, 1)

        def flipped(i):
            act.wait_ge(tr_u, i + 1)
            if i >= 4:
                act.wait_ge(y_mm, i - 3)
            nc.scalar.copy(ut[i % 4][:], ps[0][:]).then_inc(ut_c, 1)
            if i + 1 < NQ2:
                gather(i + 1)

        def entered(i):
            act.wait_ge(s_mm, i + 1)
            if i:
                act.wait_ge(s_j, i)
            nc.scalar.copy(ss[:], ps[1][:]).then_inc(s_c, 1)

        def gelu(i):
            act.wait_ge(y_mm, i + 1)
            if i >= 4:
                act.wait_ge(y_tr, 2 * (i // 2 - 1))
            f = (i % 2) * QG * H
            for g in range(QG):
                last = nc.scalar.activation(yh[(i // 2) % 2][:, :, f + g * H:f + (g + 1) * H],
                                            ps[4 + i % 2][:, g * P:(g + 1) * P].rearrange("p (t h) -> p t h", t=CH),
                                            ACT.Gelu_apprx_tanh)
            last.then_inc(y_act, 1)

        def back(i):
            if i % 2 == 0:
                return
            half, q = divmod(i, NQ)
            for r in range(2):
                act.wait_ge(y_tr, i - 1 + r + 1)
                dst = S.yt[:, q // 2, half * HALF:(half + 1) * HALF].rearrange("p (c t) -> p t c", t=CH)
                nc.scalar.copy(dst[:, 4 * r:4 * r + 4, :], ps[6 + r][:].rearrange("p (t c) -> p t c", t=4)).then_inc(y_c, 1)

        gather(0)
        turns(flipped, lambda i: None, lambda i: None, entered, gelu, back)

    @block.vector
    def _(dve):
        V = nc.vector
        ch = Chain(dve, dch)
        L = ch.link
        TT = V.tensor_tensor
        f = "p g n -> p (g n)"

        def trig(i):
            gs = slice(i % NQ * QG, (i % NQ + 1) * QG)
            return gs, ec[:, gs, :].rearrange(f), es[:, gs, :].rearrange(f)

        def scan_item(i):
            gs, cosq, sinq = trig(i)
            zf, bf = zz[i % 2][:].rearrange(f), bb[:].rearrange(f)
            dve.wait_ge(s_c, i + 1)
            if i >= 2:
                dve.wait_ge(j2, i - 1)
            TT(zf, ps[1][:], cosq, ALU.mult)
            dve.wait_ge(s_j, i + 1)
            L(TT(bf, ps[2][:], sinq, ALU.mult))
            V.tensor_tensor(zf, zf, bf, ALU.add).then_inc(m_used, 1)
            dve.wait_ge(m_used, i + 1)
            for g in range(QG):
                gg = i % NQ * QG + g
                last = V.tensor_tensor_scan(zz[i % 2][:, g, :], S.rad8[:, gg:gg + 1].to_broadcast([P, NCH]),
                                            zz[i % 2][:, g, :], carry[:, gg:gg + 1], ALU.mult, ALU.add)
            last.then_inc(z_ready, 1)

        def turn_on(i):
            gs, cosq, sinq = trig(i)
            x = xx[i % 2]
            if i >= 2:
                dve.wait_ge(y_mm, i - 1)
            V.tensor_copy(x[:, :, 0:1], carry[:, gs].unsqueeze(2))
            dve.wait_ge(z_ready, i + 1)
            TT(x[:, :, 1:NCH + 1], zz[i % 2][:], ec[:, gs, :], ALU.mult)
            dve.wait_ge(j2, i + 1)
            L(TT(bb[:].rearrange(f), ps[3][:], sinq, ALU.mult))
            L(TT(x[:, :, 1:NCH + 1], x[:, :, 1:NCH + 1], bb[:], ALU.subtract))
            V.tensor_copy(carry[:, gs].unsqueeze(2), x[:, :, NCH:NCH + 1]).then_inc(x_ready, 1)
            if i + 1 == NQ:
                dve.wait_ge(x_ready, NQ)

        L(V.memset(carry[:], 0.0))
        dve.wait_ge(count, 4)
        V.reciprocal(rc[:], rc[:]).then_inc(inv_count, 1)
        dve.wait_ge(ld_m, 16 * 10)
        turns(lambda i: None, scan_item, turn_on, lambda i: None, lambda i: None, lambda i: None)

    @block.gpsimd
    def _(pool):
        ch = Chain(pool, pch)
        L = ch.link
        Q = nc.gpsimd
        L(Q.iota(ri[:], [[1, HALO]], base=1, channel_multiplier=0))
        L(Q.tensor_copy(rt[:], ri[:]))
        for w in range(4):
            Q.tensor_scalar(rc[:, w], rt[:], float(WINDOWS[w]), None, ALU.min).then_inc(count, 1)
        pool.wait_ge(inv_count, 1)
        for w, win in enumerate(WINDOWS):
            for half in (1, 0):
                o = half * HALF
                cur, sh, n = S.pt[:, w, o:o + HALO + HALF], 1, 0
                while sh < win:
                    nxt, lo = pl[n % 2], 2 * sh - 1
                    L(Q.tensor_tensor(nxt[:, lo:], cur[:, lo:], cur[:, lo - sh:HALO + HALF - sh], ALU.add))
                    cur, sh, n = nxt[:], sh * 2, n + 1
                if half == 0:
                    L(Q.tensor_tensor(rt[:], cur[:, HALO:2 * HALO], rc[:, w], ALU.mult))
                L(Q.tensor_scalar(cur[:, HALO:], cur[:, HALO:], 1.0 / win, None, ALU.mult))
                if half == 0:
                    L(Q.tensor_copy(cur[:, HALO:2 * HALO], rt[:]))
                L(Q.tensor_tensor(S.pt[:, w, o + HALO:o + HALO + HALF], cur[:, HALO:],
                                  S.pt[:, w, o + HALO:o + HALO + HALF], ALU.subtract))

    ctx.close()


def mix(nc, S, I):
    m, ps, sem = S.map, S.ps, S.sem
    KG = SSM_W // P
    KM = KD
    NBM = SEQ // TM
    S.oh = m.at("m_oh", 67.25, [P, KM, D], F32R)
    S.ol = m.at("m_ol", 99.25, [P, KM, D], F32R)
    gh = m.at("m_gh", 131.25, [P, KG, 2 * SSM_W], F32R)
    gl = m.at("m_gl", 147.25, [P, KG, 2 * SSM_W], F32R)
    yh = [m.at(f"m_yh{i}", 163.25 + 4 * i, [P, KG, TM], F32R) for i in range(2)]
    yl = [m.at(f"m_yl{i}", 171.25 + 4 * i, [P, KG, TM], F32R) for i in range(2)]
    raw = [m.at(f"m_raw{i}", 179.25 + 4 * i, [P, D]) for i in range(2)]
    sig = [m.at(f"m_sig{i}", 187.25 + i, [P, TM]) for i in range(2)]
    wp = m.at("m_wp", 189.25, [P, 4, P])
    col = S.col
    wt = [m.at(f"m_ada{i}", 191.25 + 4 * i, [P, D]) for i in range(2)]
    ada = m.at("m_ada_sum", 199.25, [P, D])
    VECS = (3, 4, 2, 5)
    NT = KD + 1
    SV = 4 * NBM // len(VECS)
    SU = SV - 2

    NW = KG + KM
    ld_g, ld_wp = [sem("m_ld0"), sem("m_ld1")], sem("m_ldwp")
    whi, wlo, wlo_d, yhi, ylo, mm, sg, ys, pmm, pev = (
        sem("m_" + n) for n in ("whi", "wlo", "wlod", "yhi", "ylo", "mm", "sg", "ys", "pmm", "pev"))
    ld_a = [sem("m_lda0"), sem("m_lda1")]
    a_used, a_sum, a_out, g_st = sem("m_aused"), sem("m_asum"), sem("m_aout"), sem("m_gst")
    ctx = ExitStack()
    block = ctx.enter_context(nc.Block())

    def weight_of(n):
        return (gh, gl, n) if n < KG else (S.oh, S.ol, n - KG)

    def tiles(slot):
        v, i = divmod(slot, SV)
        i -= 1
        if not 0 <= i < SU:
            return range(0)
        return range(v * NT + i * NT // SU, v * NT + (i + 1) * NT // SU)

    @block.sync
    def _(sp):
        wg = I["w_glu"][0].rearrange("(k p) n -> p k n", p=P)
        wo = I["w_out"][0].rearrange("(k p) n -> p k n", p=P)
        w_ada = I["w_ada"][0].rearrange("(p k) n -> p k n", k=KD)

        def load_w(n):
            if n >= 2:
                sp.wait_ge(whi, n - 1)
                sp.wait_ge(wlo, n - 1)
                sp.wait_ge(wlo_d, min(n - 1, KG))
            sp.dma_start(raw[n % 2][:], wg[:, n] if n < KG else wo[:, n - KG]).then_inc(ld_g[n % 2], 16)

        def load_a(n):
            v, k = divmod(n, NT)
            if n >= 2:
                sp.wait_ge(a_used, n - 1)
            c = slice(VECS[v] * D, (VECS[v] + 1) * D)
            if k < KD:
                sp.dma_start(wt[n % 2][:], w_ada[:, k, c]).then_inc(ld_a[n % 2], 16)
            else:
                sp.dma_start(wt[n % 2][0:1, :], I["b_ada"][0:1, c]).then_inc(ld_a[n % 2], 16)

        for n in range(KG):
            load_w(n)
        load_a(0)
        load_a(1)
        load_w(KG)
        load_w(KG + 1)
        for b in range(NBM):
            for t in range(4):
                slot = 4 * b + t
                for n in tiles(slot):
                    if n + 2 < len(VECS) * NT:
                        load_a(n + 2)
                if slot == 3 * SV:
                    sp.wait_ge(a_out, 3)
                    sp.dma_start(S.gates[0:1, :], ada[0:1, :]).then_inc(g_st, 16)
            if b + 2 < KM:
                load_w(KG + b + 2)
        sp.wait_ge(a_out, 4)
        sp.dma_start(S.gates[1:2, :], ada[0:1, :]).then_inc(g_st, 16)
        sp.wait_ge(g_st, 32)

    @block.scalar
    def _(act):
        act.dma_start(wp[:], I["w_pool"][0].rearrange("g c d -> c g d")).then_inc(ld_wp, 16)
        act.wait_ge(S.ld_col, 48)

        def weight(n):
            h, _, k = weight_of(n)
            act.wait_ge(ld_g[n % 2], 16 * (n // 2 + 1))
            nc.scalar.copy(h[:, k], raw[n % 2][:]).then_inc(whi, 1)

        def split(b):
            if b >= 2:
                act.wait_ge(mm, 8 * (b - 1))
            nc.scalar.copy(yh[b % 2][:], S.yt[:, :, b * TM:(b + 1) * TM]).then_inc(yhi, 1)

        split(0)
        for n in range(KG):
            weight(n)
        for b in range(NBM):
            if b + 1 < NBM:
                split(b + 1)
            for t in range(4):
                i = 4 * b + t
                act.wait_ge(mm, 2 * i + 2)
                if i >= 2:
                    act.wait_ge(ys, i - 1)
                nc.scalar.activation(sig[i % 2][:], ps[2 * (i % 2) + 1][:, 0:TM], ACT.Sigmoid, bias=col[:, 4 + t:5 + t]).then_inc(sg, 1)
            weight(KG + b)

    @block.gpsimd
    def _(pool):
        for n in range(NW):
            h, l, k = weight_of(n)
            c = slice(512 if n < KG else 0, D)
            pool.wait_ge(whi, n + 1)
            nc.gpsimd.tensor_tensor(l[:, k, c], raw[n % 2][:, c], h[:, k, c].bitcast(F32), ALU.subtract).then_inc(wlo, 1)

    @block.vector
    def _(dve):
        V = nc.vector
        dve.wait_ge(S.ld_col, 48)

        def split(b):
            if b >= 2:
                dve.wait_ge(mm, 8 * (b - 1))
            dve.wait_ge(yhi, b + 1)
            V.tensor_tensor(yl[b % 2][:], S.yt[:, :, b * TM:(b + 1) * TM], yh[b % 2][:].bitcast(F32), ALU.subtract).then_inc(ylo, 1)

        def ada_tile(n):
            v, k = divmod(n, NT)
            dve.wait_ge(ld_a[n % 2], 16 * (n // 2 + 1))
            if k == 0:
                if v == 3:
                    dve.wait_ge(g_st, 16)
                ins = V.tensor_scalar(ada[:], wt[n % 2][:], S.csl[:, 0:1], None, ALU.mult)
            elif k < KD:
                ins = V.scalar_tensor_tensor(ada[:], wt[n % 2][:], S.csl[:, k:k + 1], ada[:], ALU.mult, ALU.add)
            else:
                ins = V.tensor_tensor(ada[0:1, :], ada[0:1, :], wt[n % 2][0:1, :], ALU.add)
            ins.then_inc(a_used, 1)
            dve.wait_ge(a_used, n + 1)

        def ada_out(v):
            dve.wait_ge(a_sum, v + 1)
            if v == 0:
                last = V.tensor_copy(S.b2[:], ps[6][:, 0:KD])
            elif v == 1:
                last = V.scalar_tensor_tensor(S.a2[:], ps[6][:, 0:KD], 1.0, S.g_ffn[:], ALU.add, ALU.mult)
            else:
                V.tensor_copy(ada[0:1, 0:512], ps[6][0:1, :])
                last = V.tensor_copy(ada[0:1, 512:D], ps[7][0:1, :])
            last.then_inc(a_out, 1)

        split(0)
        for n in range(KG):
            dve.wait_ge(whi, n + 1)
            V.tensor_tensor(gl[:, n, 0:512], raw[n % 2][:, 0:512], gh[:, n, 0:512].bitcast(F32), ALU.subtract).then_inc(wlo_d, 1)
        for b in range(NBM):
            bs = slice(b * TM, (b + 1) * TM)
            if b + 1 < NBM:
                split(b + 1)
            for t in range(4):
                i = 4 * b + t
                dve.wait_ge(pmm, i + 1)
                V.tensor_scalar(S.pt[:, t, HALO + b * TM:HALO + (b + 1) * TM], ps[4 + i % 2][:, 0:TM], col[:, 8 + t:9 + t],
                                col[:, 12 + t:13 + t], ALU.add, ALU.mult).then_inc(pev, 1)
                dve.wait_ge(sg, i + 1)
                V.scalar_tensor_tensor(S.yt[:, t, bs], ps[2 * (i % 2)][:, 0:TM], col[:, t:t + 1], sig[i % 2][:], ALU.add,
                                       ALU.mult).then_inc(ys, 1)
                if i and i % SV == 0:
                    ada_out(i // SV - 1)
                for n in tiles(i):
                    ada_tile(n)
        ada_out(3)

    @block.tensor
    def _(pe):
        T = nc.tensor

        def ada_sum(v):
            pe.wait_ge(a_used, NT * (v + 1))
            if v:
                pe.wait_ge(a_out, v)
            if v < 2:
                for k in range(KD):
                    last = T.matmul(ps[6][:, k:k + 1], ada[:, bass.ds(k, P, step=KD)], S.ones[:, 0:1], start=True, stop=True)
            else:
                for r in range(2):
                    last = T.matmul(ps[6 + r][0:1, :], S.ones[:, 0:1], ada[:, r * 512:(r + 1) * 512], start=True, stop=True)
            last.then_inc(a_sum, 1)

        def pooling(i):
            b, w = divmod(i, 4)
            if i >= 2:
                pe.wait_ge(pev, i - 1)
            T.matmul(ps[4 + i % 2][:, 0:TM], wp[:, w], S.pt[:, w, HALO + b * TM:HALO + (b + 1) * TM], start=True,
                     stop=True).then_inc(pmm, 1)

        pe.wait_ge(ld_wp, 16)
        for i in range(4 * NBM):
            b, t = divmod(i, 4)
            pooling(i)
            if i == 0:
                pe.wait_ge(wlo, KG)
                pe.wait_ge(wlo_d, KG)
            if i and i % SV == 0:
                ada_sum(i // SV - 1)
            if t == 0:
                pe.wait_ge(ylo, b + 1)
            if i >= 2:
                pe.wait_ge(ys, i - 1)
            for part in range(2):
                c = slice(part * SSM_W + t * P, part * SSM_W + (t + 1) * P)
                for k in range(KG):
                    last = three(nc, ps[2 * (i % 2) + part][:, 0:TM], gh[:, k, c], gl[:, k, c], yh[b % 2][:, k], yl[b % 2][:, k],
                                 k == 0, k == KG - 1)
                last.then_inc(mm, 1)
        ada_sum(3)

    ctx.close()


def ffn(nc, S, I):
    m, ps, sem = S.map, S.ps, S.sem
    ctx = ExitStack()
    NT = TF // P
    NO = 2 * NT
    NM = SEQ // P
    KM = KD
    h2h = m.at("f_h2h", 3, [P, KD, TF], F32R)
    h2l = m.at("f_h2l", 35, [P, KD, TF], F32R)
    acc = m.at("f_acc", 67.25, [P, NT, D])
    ah = [m.at(f"f_ah{i}", 99.25 + 8 * i, [P, TF], F32R) for i in range(2)]
    al = [m.at(f"f_al{i}", 103.25 + 8 * i, [P, TF], F32R) for i in range(2)]
    uh = [m.at(f"f_uh{i}", (143.25, 115.25)[i], [P, 2, KD, P], F32R) for i in range(2)]
    ul = [m.at(f"f_ul{i}", (151.25, 123.25)[i], [P, 2, KD, P], F32R) for i in range(2)]
    slot = [m.at(f"f_slot{i}", 131.25 + 4 * i, [P, D]) for i in range(3)]
    mh = [m.at(f"o_mh{i}", 159.25 + 8 * i, [P, KM, P], F32R) for i in range(2)]
    ml = [m.at(f"o_ml{i}", 163.25 + 8 * i, [P, KM, P], F32R) for i in range(2)]
    xt = [m.at(f"o_x{i}", 175.25 + 4 * i, [P, D]) for i in range(2)]
    xg = m.at("o_xg", 183.25, [P, D])
    gb = m.at("o_gate", 187.25, [P, D])
    xn = m.at("o_xn", 191.25, [P, D])
    ht = m.at("o_ht", 195.25, [P, KD, P])
    junk = m.at("o_junk", 199.25, [P, D], BF16)
    dh = [m.at(f"f_dh{i}", 159.25 + 8 * i, [P, D], F32R) for i in range(2)]
    dl = [m.at(f"f_dl{i}", 163.25 + 8 * i, [P, D], F32R) for i in range(2)]
    gs = m.at("f_gs", 175.25, [P, 2 + TF])
    cv = [m.at(f"f_cv{i}", 179.375 + 2 * i, [P, 512]) for i in range(2)]
    full = [m.at(f"f_full{i}", 183.375 + 2 * i, [P, 512]) for i in range(2)]
    gt = m.at("f_gt", 187.375, [P, D])
    gf = m.at("f_gf", 191.375, [P, D])
    xr = [m.at(f"f_xr{i}", 195.375 + 4 * i, [P, D]) for i in range(2)]
    halo = m.at("f_halo", 203.5, [P, NF, 2])
    cw = m.at("f_cw", 203.75, [P, 4, NF])
    cj = [m.at(f"f_cj{i}", 204.125 + 0.0625 * i, [P, 4]) for i in range(2)]
    st = m.at("f_stat", 204.25, [P, 8, NM])
    crow = m.at("f_crow", 204.75, [4 * NF, P])

    ld_b, ld_x, x_st, h_st = sem("o_ldb"), [sem("o_ldx0"), sem("o_ldx1")], [sem("o_xst0"), sem("o_xst1")], sem("o_hst")
    mhi, mlo, om, xg_r, x1r, sq, root_in, root, xnr, tr, hta, htb = (
        sem("o_" + n) for n in ("mhi", "mlo", "mm", "xg", "x1", "sq", "ri", "ro", "xn", "tr", "hta", "htb"))
    ld_cw, cwt, cw_ok, dch = sem("f_ldcw"), sem("f_cwt"), sem("f_cwok"), sem("f_dch")
    ld_s = [sem(f"f_ld{i}") for i in range(3)]
    h2hi, h2lo, uhi, ulo, dhi, dlo, upg, upv, gev, chn, cvd, hal, sil, prod, vhi, vlo, dmm, dad = (
        sem("f_" + n) for n in ("h2hi", "h2lo", "uhi", "ulo", "dhi", "dlo", "upg", "upv", "gev", "chn", "cvd", "hal",
                                "sil", "prod", "vhi", "vlo", "dmm", "dad"))
    ld_g, ld_r, gated, t1, sq2, root_in2, root2, oo_r, o_st = (
        sem("z_" + n) for n in ("ldg", "ldr", "gated", "t1", "sq", "ri", "ro", "oo", "ost"))

    w_up = I["w_up"][0].rearrange("(p k) n -> p k n", k=KD)
    w_dn = I["w_down"][0]
    V, A, T, Q = nc.vector, nc.scalar, nc.tensor, nc.gpsimd
    HU = [sum(1 for k in range(KD) if k % 3 == i) for i in range(3)]

    def landed(i, pas, j):
        return 16 * (pas * (HU[i] + NF) + HU[i] + j + 1)

    block = ctx.enter_context(nc.Block())

    def tail_dmas(sp, pas):
        def load_r(t):
            n = pas * NT + t
            if n:
                sp.wait_ge(ld_r, 16 * n)
            if n >= 2:
                sp.wait_ge(t1, n - 1)
            sp.dma_start(xr[t % 2][:], S.x1[n * P:(n + 1) * P, :]).then_inc(ld_r, 16)

        def store_o(t):
            n = pas * NT + t
            sp.wait_ge(oo_r, n + 1)
            sp.dma_start(I["out"][0, n * P:(n + 1) * P, :], acc[:, t]).then_inc(o_st, 16)

        for g in range(2):
            for t in range(4 * g, 4 * g + 4):
                load_r(t)
            for t in range(4 * g, 4 * g + 4):
                store_o(t)

    @block.sync
    def _(sp):
        for i in range(3):
            sp.dma_start(crow[i * NF:(i + 1) * NF, :], I["w_conv"][0, i].rearrange("(j p) -> j p", p=P)).then_inc(ld_cw, 16)
        sp.dma_start(crow[3 * NF:4 * NF, :], I["b_conv"][0].rearrange("(j p) -> j p", p=P)).then_inc(ld_cw, 16)
        sp.dma_start(gb[:], S.gates[0:1, :].to_broadcast([P, D])).then_inc(ld_b, 16)

        def load_x(n):
            if n >= 2:
                sp.wait_ge(xnr, n - 1)
                sp.wait_ge(x_st[n % 2], 16 * (n // 2))
            sp.dma_start(xt[n % 2][:], I["x"][0, n * P:(n + 1) * P, :]).then_inc(ld_x[n % 2], 16)

        def store_h(n):
            sp.wait_ge(hta, n + 1)
            sp.wait_ge(htb, n + 1)
            sp.dma_start(S.h2[:, :, n * P:(n + 1) * P], ht[:]).then_inc(h_st, 16)

        load_x(0)
        load_x(1)
        for n in range(NM):
            sp.wait_ge(x1r, 2 * (n + 1))
            sp.dma_start(S.x1[n * P:(n + 1) * P, :], xt[n % 2][:]).then_inc(x_st[n % 2], 16)
            if n + 2 < NM:
                load_x(n + 2)
            if n >= 1:
                store_h(n - 1)

        def unit(i, src):
            sp.dma_start(slot[i][:] if len(src.shape) == 2 else slot[i][:].rearrange("p (k n) -> p k n", k=KD), src).then_inc(ld_s[i], 16)

        def load_u(pas, j, freed, between=None):
            for part in (1, 0):
                i = 1 - part
                sp.wait_ge(uhi, freed(part)[0])
                sp.wait_ge(ulo, freed(part)[0])
                unit(i, w_up[:, :, bass.ds((j + NF if part else j) * P, P)])
            if between:
                between()
            sp.wait_ge(dhi, freed(0)[1])
            sp.wait_ge(dlo, freed(0)[1])
            unit(2, w_dn[bass.ds(j * P, P), :])

        for pas in range(NP):
            t0 = pas * TF
            if pas == 0:
                sp.wait_ge(h_st, 16 * (NM - 1))
            for k in range(KD):
                i = k % 3
                if k >= 3:
                    sp.wait_ge(h2hi, pas * KD + k - 2)
                    sp.wait_ge(h2lo, pas * KD + k - 2)
                elif pas:
                    if i < 2:
                        sp.wait_ge(uhi, 2 * pas * NF - 1 + i)
                        sp.wait_ge(ulo, 2 * pas * NF - 1 + i)
                    else:
                        sp.wait_ge(dhi, pas * NF)
                        sp.wait_ge(dlo, pas * NF)
                unit(i, S.h2[:, k, t0:t0 + TF])
                if pas == 0 and k == 2:
                    store_h(NM - 1)
            for i in range(2):
                last = max(k for k in range(KD) if k % 3 == i)
                sp.wait_ge(h2hi, pas * KD + last + 1)
                sp.wait_ge(h2lo, pas * KD + last + 1)
                unit(i, w_up[:, :, (1 - i) * D_FF:(1 - i) * D_FF + P])
            last = max(k for k in range(KD) if k % 3 == 2)
            sp.wait_ge(h2hi, pas * KD + last + 1)
            sp.wait_ge(h2lo, pas * KD + last + 1)
            unit(2, w_dn[0:P, :])

            def freed_of(pas, j):
                return lambda part: (2 * (pas * NF + j - 1) + (1 if part else 2), pas * NF + j)

            load_u(pas, 1, freed_of(pas, 1), (lambda: tail_dmas(sp, pas - 1)) if pas else None)
            if pas == 0:
                sp.wait_ge(xnr, NM)
                sp.wait_ge(hta, NM)
                sp.wait_ge(x_st[0], 16 * NM // 2)
                sp.wait_ge(x_st[1], 16 * NM // 2)
                sp.wait_ge(h_st, 16 * NM)
                sp.dma_start(gt[:], S.gates[1:2, :].to_broadcast([P, D])).then_inc(ld_g, 16)
                sp.dma_start(gf[:], I["g_norm_final"].rearrange("(a d) -> a d", a=1).to_broadcast([P, D])).then_inc(ld_g, 16)
            with sp.Fori(0, NF // 2 - 1) as it:
                load_u(pas, 2 * it + 2, freed_of(pas, 2 * it + 2))
                load_u(pas, 2 * it + 3, freed_of(pas, 2 * it + 3))
        tail_dmas(sp, NP - 1)
        sp.wait_ge(o_st, 16 * NT * NP)

    @block.scalar
    def _(act):
        def split(n):
            if n >= 2:
                act.wait_ge(om, 2 * (n - 1))
            A.copy(mh[n % 2][:, 0:4], S.yt[:, :, n * P:(n + 1) * P]).then_inc(mhi, 1)
            A.copy(mh[n % 2][:, 4:8], S.pt[:, :, HALO + n * P:HALO + (n + 1) * P]).then_inc(mhi, 1)

        def stats(n):
            act.wait_ge(x1r, 2 * (n + 1))
            A.activation(junk[:], xt[n % 2][:], ACT.Square, accum_out=st[:, 0, n:n + 1]).then_inc(sq, 1)
            act.wait_ge(root_in, n + 1)
            A.activation(st[:, 1, n:n + 1], st[:, 3, n:n + 1], ACT.Sqrt).then_inc(root, 1)

        def transposed(n):
            act.wait_ge(tr, n + 1)
            if n:
                act.wait_ge(h_st, 16 * n)
            for k in range(4):
                last = A.activation(ht[:, k], ps[6][:, k * P:(k + 1) * P], ACT.Identity, bias=S.b2[:, k:k + 1], scale=S.a2[:, k:k + 1])
            last.then_inc(hta, 1)

        split(0)
        for n in range(NM):
            if n + 1 < NM:
                split(n + 1)
            stats(n)
            if n:
                transposed(n - 1)
        transposed(NM - 1)

        def up_high(pas, j, b, guard):
            for part in (1, 0):
                i = 1 - part
                act.wait_ge(ld_s[i], landed(i, pas, j))
                if guard and part:
                    act.wait_ge(upv, 2 * (pas * NF + j - 1))
                A.copy(uh[b][:, part].rearrange("p k n -> p (k n)"), slot[i][:]).then_inc(uhi, 1)

        def down_high(pas, j, b, guard):
            act.wait_ge(ld_s[2], landed(2, pas, j))
            if guard:
                act.wait_ge(dmm, NO * (pas * NF + j))
            A.copy(dh[b][:], slot[2][:]).then_inc(dhi, 1)

        def hidden(pas, j, b, guard):
            J = pas * NF + j
            for t in range(2):
                act.wait_ge(upg, 2 * J + t + 1)
                if t == 0 and guard:
                    act.wait_ge(cvd, 2 * J)
                    act.wait_ge(hal, J)
                A.copy(gs[:, 2 + t * 512:2 + (t + 1) * 512], ps[t][:]).then_inc(gev, 1)
            for t in range(2):
                act.wait_ge(cvd, 2 * J + t + 1)
                A.activation(cv[t][:], cv[t][:], ACT.Silu, bias=cj[b][:, 3:4]).then_inc(sil, 1)
            for t in range(2):
                act.wait_ge(prod, 2 * J + t + 1)
                A.copy(ah[b][:, t * 512:(t + 1) * 512], full[t][:]).then_inc(vhi, 1)

        def tail(pas, g):
            for t in range(4 * g, 4 * g + 4):
                n = pas * NT + t
                act.wait_ge(t1, n + 1)
                if n:
                    act.wait_ge(sq2, n)
                A.activation(gs[:, 0:D], acc[:, t], ACT.Square, accum_out=st[:, 0, t:t + 1]).then_inc(sq2, 1)
            act.wait_ge(root_in2, 2 * pas + g + 1)
            A.activation(st[:, 1, 4 * g:4 * g + 4], st[:, 3, 4 * g:4 * g + 4], ACT.Sqrt).then_inc(root2, 1)

        for pas in range(NP):
            if pas == 0:
                act.wait_ge(mlo, 2 * NM)
            for k in range(KD):
                i, n = k % 3, k // 3
                act.wait_ge(ld_s[i], 16 * (pas * (HU[i] + NF) + n + 1))
                if pas and k == 0:
                    act.wait_ge(upv, 2 * pas * NF)
                A.copy(h2h[:, k], slot[i][:]).then_inc(h2hi, 1)
            up_high(pas, 0, 0, False)
            if pas:
                tail(pas - 1, 0)
            if pas == 0:
                act.wait_ge(om, 2 * NM)
            up_high(pas, 1, 1, False)
            hidden(pas, 0, 0, pas > 0)
            if pas:
                tail(pas - 1, 1)
            down_high(pas, 0, 0, pas > 0)
            with act.Fori(1, NF // 2) as it:
                up_high(pas, 2 * it, 0, True)
                hidden(pas, 2 * it - 1, 1, True)
                down_high(pas, 2 * it - 1, 1, True)
                up_high(pas, 2 * it + 1, 1, True)
                hidden(pas, 2 * it, 0, True)
                down_high(pas, 2 * it, 0, True)
            hidden(pas, NF - 1, 1, True)
            down_high(pas, NF - 1, 1, True)
        tail(NP - 1, 0)
        tail(NP - 1, 1)

    @block.gpsimd
    def _(pool):
        for n in range(NM):
            for part, src in ((0, S.yt[:, :, n * P:(n + 1) * P]), (1, S.pt[:, :, HALO + n * P:HALO + (n + 1) * P])):
                c = slice(4 * part, 4 * part + 4)
                pool.wait_ge(mhi, 2 * n + part + 1)
                Q.tensor_tensor(ml[n % 2][:, c], src, mh[n % 2][:, c].bitcast(F32), ALU.subtract).then_inc(mlo, 1)

        def up_low(pas, j, b):
            for part in (1, 0):
                pool.wait_ge(uhi, 2 * (pas * NF + j) + (1 if part else 2))
                Q.tensor_tensor(ul[b][:, part].rearrange("p k n -> p (k n)"), slot[1 - part][:],
                                uh[b][:, part].rearrange("p k n -> p (k n)").bitcast(F32), ALU.subtract).then_inc(ulo, 1)

        def down_low(pas, j, b):
            pool.wait_ge(dhi, pas * NF + j + 1)
            Q.tensor_tensor(dl[b][:], slot[2][:], dh[b][:].bitcast(F32), ALU.subtract).then_inc(dlo, 1)

        for pas in range(NP):
            for k in range(KD):
                pool.wait_ge(h2hi, pas * KD + k + 1)
                Q.tensor_tensor(h2l[:, k], slot[k % 3][:], h2h[:, k].bitcast(F32), ALU.subtract).then_inc(h2lo, 1)
            up_low(pas, 0, 0)
            up_low(pas, 1, 1)
            down_low(pas, 0, 0)
            with pool.Fori(1, NF // 2) as it:
                up_low(pas, 2 * it, 0)
                down_low(pas, 2 * it - 1, 1)
                up_low(pas, 2 * it + 1, 1)
                down_low(pas, 2 * it, 0)
            down_low(pas, NF - 1, 1)

    @block.vector
    def _(dve):
        ch = Chain(dve, dch)
        dve.wait_ge(cwt, 1)
        V.tensor_copy(cw[:].rearrange("p i j -> p (i j)"), ps[6][:, 0:4 * NF]).then_inc(cw_ok, 1)
        V.memset(halo[:], 0.0)
        dve.wait_ge(ld_b, 16)

        def residual(n):
            dve.wait_ge(ld_x[n % 2], 16 * (n // 2 + 1))
            for r in range(2):
                i = 2 * n + r
                rs = slice(r * 512, (r + 1) * 512)
                dve.wait_ge(om, i + 1)
                V.tensor_tensor(xg[:, rs], ps[i % 4][:], gb[:, rs], ALU.mult).then_inc(xg_r, 1)
                dve.wait_ge(xg_r, i + 1)
                V.tensor_tensor(xt[n % 2][:, rs], xg[:, rs], xt[n % 2][:, rs], ALU.add).then_inc(x1r, 1)

        def normalise(n):
            dve.wait_ge(sq, n + 1)

            def root_step(out, r):
                V.tensor_copy(st[:, 3, n:n + 1], r).then_inc(root_in, 1)
                dve.wait_ge(root, n + 1)

            c = [st[:, i, n:n + 1] for i in range(5)]
            rstd_steps(nc, ch.link, c[1], c[0], (c[2], c[4]), root_step)
            if n:
                dve.wait_ge(tr, n)
            V.tensor_scalar(xn[:], xt[n % 2][:], c[1], None, ALU.mult).then_inc(xnr, 1)

        def transposed(n):
            dve.wait_ge(tr, n + 1)
            if n:
                dve.wait_ge(h_st, 16 * n)
            for k in range(4, KD):
                last = V.tensor_scalar(ht[:, k], ps[7][:, (k - 4) * P:(k - 3) * P], S.a2[:, k:k + 1], S.b2[:, k:k + 1], ALU.mult, ALU.add)
            last.then_inc(htb, 1)

        for n in range(NM):
            residual(n)
            if n:
                transposed(n - 1)
            normalise(n)
        transposed(NM - 1)

        def adds(pas, j, first=False):
            for i in range(NO):
                t, r = divmod(i, 2)
                dve.wait_ge(dmm, NO * (pas * NF + j) + i + 1)
                c = acc[:, t, r * 512:(r + 1) * 512]
                if first:
                    V.tensor_copy(c, ps[4 + i % 4][:]).then_inc(dad, 1)
                else:
                    V.tensor_tensor(c, ps[4 + i % 4][:], c, ALU.add).then_inc(dad, 1)

        def hidden(pas, j, b):
            J = pas * NF + j
            V.tensor_copy(cj[b][:].unsqueeze(2), cw[:, :, bass.ds(j, 1)])
            V.tensor_copy(gs[:, 0:2], halo[:, bass.ds(j, 1), :]).then_inc(chn, 1)
            dve.wait_ge(chn, 5 * J + 1)
            for t in range(2):
                o = t * 512
                dve.wait_ge(gev, 2 * J + t + 1)
                V.tensor_scalar(cv[t][:], gs[:, o:o + 512], cj[b][:, 0:1], None, ALU.mult).then_inc(chn, 1)
                dve.wait_ge(chn, 5 * J + 2 + 2 * t)
                V.scalar_tensor_tensor(cv[t][:], gs[:, o + 1:o + 513], cj[b][:, 1:2], cv[t][:], ALU.mult, ALU.add).then_inc(chn, 1)
                dve.wait_ge(chn, 5 * J + 3 + 2 * t)
                V.scalar_tensor_tensor(cv[t][:], gs[:, o + 2:o + 514], cj[b][:, 2:3], cv[t][:], ALU.mult, ALU.add).then_inc(cvd, 1)
            V.tensor_copy(halo[:, bass.ds(j, 1), :], gs[:, TF:TF + 2]).then_inc(hal, 1)
            for t in range(2):
                dve.wait_ge(sil, 2 * J + t + 1)
                dve.wait_ge(upv, 2 * J + t + 1)
                V.tensor_tensor(full[t][:], ps[2 + t][:], cv[t][:], ALU.mult).then_inc(prod, 1)
            for t in range(2):
                ts = slice(t * 512, (t + 1) * 512)
                dve.wait_ge(vhi, 2 * J + t + 1)
                V.tensor_tensor(al[b][:, ts], full[t][:], ah[b][:, ts].bitcast(F32), ALU.subtract).then_inc(vlo, 1)

        def tail(pas, g):
            for t in range(4 * g, 4 * g + 4):
                n = pas * NT + t
                if t == 0 and pas == 0:
                    dve.wait_ge(ld_g, 32)
                V.tensor_tensor(acc[:, t], acc[:, t], gt[:], ALU.mult).then_inc(gated, 1)
                dve.wait_ge(gated, n + 1)
                dve.wait_ge(ld_r, 16 * (n + 1))
                V.tensor_tensor(acc[:, t], acc[:, t], xr[t % 2][:], ALU.add).then_inc(t1, 1)
            dve.wait_ge(sq2, pas * NT + 4 * g + 4)

            def root_step(out, r):
                V.tensor_copy(st[:, 3, 4 * g:4 * g + 4], r).then_inc(root_in2, 1)
                dve.wait_ge(root2, 2 * pas + g + 1)

            c = [st[:, i, 4 * g:4 * g + 4] for i in range(5)]
            rstd_steps(nc, ch.link, c[1], c[0], (c[2], c[4]), root_step)
            for t in range(4 * g, 4 * g + 4):
                V.scalar_tensor_tensor(acc[:, t], acc[:, t], st[:, 1, t:t + 1], gf[:], ALU.mult, ALU.mult).then_inc(oo_r, 1)

        for pas in range(NP):
            if pas:
                tail(pas - 1, 0)
            hidden(pas, 0, 0)
            if pas:
                tail(pas - 1, 1)
                dve.wait_ge(o_st, 16 * NT * pas)
            adds(pas, 0, True)
            hidden(pas, 1, 1)
            with dve.Fori(1, NF // 2) as it:
                adds(pas, 2 * it - 1)
                hidden(pas, 2 * it, 0)
                adds(pas, 2 * it)
                hidden(pas, 2 * it + 1, 1)
            adds(pas, NF - 1)
        tail(NP - 1, 0)
        tail(NP - 1, 1)

    @block.tensor
    def _(pe):
        pe.wait_ge(ld_cw, 64)
        T.transpose(ps[6][:, 0:4 * NF], crow[:], S.ident[0:4 * NF, 0:4 * NF]).then_inc(cwt, 1)
        pe.wait_ge(cw_ok, 1)

        def project_out(n):
            pe.wait_ge(mlo, 2 * (n + 1))
            for r in range(2):
                i = 2 * n + r
                if i >= 4:
                    pe.wait_ge(xg_r, i - 3)
                rs = slice(r * 512, (r + 1) * 512)
                for k in range(KM):
                    last = three(nc, ps[i % 4][:], mh[n % 2][:, k], ml[n % 2][:, k], S.oh[:, k, rs], S.ol[:, k, rs], k == 0, k == KM - 1)
                last.then_inc(om, 1)

        def flip(n):
            pe.wait_ge(xnr, n + 1)
            if n:
                pe.wait_ge(hta, n)
                pe.wait_ge(htb, n)
            for k in range(KD):
                last = T.transpose(ps[6 + k // 4][:, k % 4 * P:(k % 4 + 1) * P], xn[:, bass.ds(k, P, step=KD)], S.ident[:])
            last.then_inc(tr, 1)

        for n in range(NM):
            project_out(n)
            if n:
                flip(n - 1)
        flip(NM - 1)
        pe.wait_ge(xg_r, 2 * NM)

        def up(pas, j, b, first):
            J = pas * NF + j
            for part, out, done, free in ((1, 0, upg, gev), (0, 2, upv, prod)):
                pe.wait_ge(ulo, 2 * J + (1 if part else 2))
                for t in range(2):
                    if not first:
                        pe.wait_ge(free, 2 * J - 1 + t)
                    ts = slice(t * 512, (t + 1) * 512)
                    for k in range(KD):
                        if isinstance(j, int) and j == 0 and part == 1 and t == 0:
                            pe.wait_ge(h2lo, pas * KD + k + 1)
                        last = three(nc, ps[out + t][:], uh[b][:, part, k, :], ul[b][:, part, k, :],
                                     h2h[:, k, ts], h2l[:, k, ts], k == 0, k == KD - 1)
                    last.then_inc(done, 1)

        def down(pas, j, b, first):
            J = pas * NF + j
            pe.wait_ge(vlo, 2 * J + 2)
            pe.wait_ge(dlo, J + 1)
            for i in range(NO):
                t, r = divmod(i, 2)
                if not (first and i < 4):
                    pe.wait_ge(dad, NO * J + i - 3)
                ts, rs = slice(t * P, (t + 1) * P), slice(r * 512, (r + 1) * 512)
                three(nc, ps[4 + i % 4][:], ah[b][:, ts], al[b][:, ts], dh[b][:, rs], dl[b][:, rs], True, True).then_inc(dmm, 1)

        for pas in range(NP):
            up(pas, 0, 0, pas == 0)
            up(pas, 1, 1, False)
            if pas == 0:
                pe.wait_ge(hta, NM)
                pe.wait_ge(htb, NM)
            down(pas, 0, 0, pas == 0)
            with pe.Fori(1, NF // 2) as it:
                up(pas, 2 * it, 0, False)
                down(pas, 2 * it - 1, 1, False)
                up(pas, 2 * it + 1, 1, False)
                down(pas, 2 * it, 0, False)
            down(pas, NF - 1, 1, False)

    ctx.close()


class Shared:
    pass


def build(nc, I, debug=None):
    S = Shared()
    base = (nc.sbuf_base + 63) // 64 * 64
    slab = nc.alloc_sbuf_tensor("slab", [P, (SBUF_BYTES + 64) // 4], F32)
    S.map = Place(nc, base)
    ctx = ExitStack()
    S.sem = lambda name: ctx.enter_context(nc.semaphore(name))
    S.ps = [nc.alloc_psum_tensor(f"bank{i}", [P, 512], F32) for i in range(8)]
    at = S.map.at
    S.ident = at("ident", 0, [P, P])
    S.swap = at("swap", 0.5, [P, P])
    S.ones = at("ones", 1, [P, P])
    S.a1, S.b1, S.a2, S.b2 = (at(n, 1.5 + 0.0625 * i, [P, KD]) for i, n in enumerate(("a1", "b1", "a2", "b2")))
    S.rad8 = at("rad8", 2, [P, G])
    S.csl, S.g_ffn = at("c_silu", 2.25, [P, KD]), at("g_ffn", 2.3125, [P, KD])
    S.pt = at("pt", 3, [P, 4, HALO + SEQ])
    S.yt = at("yt", 35.25, [P, 4, SEQ])
    kind = "ExternalOutput" if debug else None

    def dram(name, shape):
        if debug is not None and name in debug:
            return debug[name]
        return nc.dram_tensor(name, list(shape), F32).ap()

    S.u = dram("u_scratch", (SEQ, SSM_W))
    S.x1 = dram("x1_scratch", (SEQ, D))
    S.kpad = dram("kpad", (G, H, 240))
    S.mats = dram("mats", (P, 2, G * P))
    S.gates = dram("gates", (2, D))
    S.h2 = dram("h2_scratch", (P, KD, SEQ))
    S.col, S.ld_col = at("m_col", 206.5, [P, 16]), S.sem("ld_col")
    S.sn, S.cs = (at(n, 83.25 + 1.75 * i, [P, NM, G]) for i, n in enumerate(("sn", "cs")))
    S.ec, S.es = (at(n, 119 + 16 * i, [P, G, NCH]) for i, n in enumerate(("s_cos", "s_sin")))
    S.xb = [at(f"a_x{i}", 35.25 + 8 * i, [P, TA // P, D]) for i in range(2)]
    S.wraw = [at(f"a_wraw{i}", 51.25 + 4 * i, [P, D]) for i in range(2)]
    S.st = at("a_stat", 86.75, [P, 5, TA // P])
    S.sq, S.root_in, S.root, S.xn = (S.sem("a_" + n) for n in ("sq", "root_in", "root", "xn"))
    S.ld_x, S.ld_w = [S.sem("a_ld_x0"), S.sem("a_ld_x1")], [S.sem("a_ld_w0"), S.sem("a_ld_w1")]
    S.mats_st, S.kpad_st = S.sem("mats_stored"), S.sem("kpad_stored")
    S.w_in = I["w_in"][0].rearrange("(p k) n -> p k n", k=KD)
    S.x_v = I["x"][0].rearrange("(b j p) d -> b p j d", p=P, j=TA // P)
    prepare(nc, S, I)
    project(nc, S, I)
    scan(nc, S, I)
    mix(nc, S, I)
    ffn(nc, S, I)
    ctx.close()


_INS = ["x", "c", "w_ada", "b_ada", "g_norm_mix", "w_in", "ssm_lam_re", "ssm_lam_im", "ssm_log_dt", "ssm_b_re",
        "ssm_b_im", "ssm_c_re", "ssm_c_im", "ssm_d", "w_glu", "b_glu", "w_pool", "b_pool", "pool_scale", "w_out",
        "g_norm_ffn", "w_up", "w_conv", "b_conv", "w_down", "g_norm_final"]


def kernel(**inputs):
    import numpy as _np
    import concourse.bacc as _bacc
    from concourse import mybir as _mybir
    from concourse.bass_utils import run_bass_kernel_spmd as _run

    nc = _bacc.Bacc("TRN2", target_bir_lowering=False, num_devices=1)
    arrays, handles = {}, {}
    for name in _INS:
        a = _np.ascontiguousarray(inputs[name])
        arrays[f"in_{name}"] = a
        handles[name] = nc.dram_tensor(f"in_{name}", a.shape, _mybir.dt.from_np(a.dtype), kind="ExternalInput").ap()
    handles["out"] = nc.dram_tensor("out_0", (1, SEQ, D), _mybir.dt.float32, kind="ExternalOutput").ap()
    build(nc, handles)
    r = _run(nc, [arrays], core_ids=[0])
    return r.results[0]["out_0"]
```

```python
import math
from contextlib import ExitStack

import numpy as np

import concourse.bass as bass
from concourse import mybir

F32 = mybir.dt.float32
F32R = mybir.dt.float32r
BF16 = mybir.dt.bfloat16
I32 = mybir.dt.int32
ALU = mybir.AluOpType
ACT = mybir.ActivationFunctionType

P = 128
D = 1024
SEQ = 2048
KD = D // P
SSM_W = 512
G, H, NS = 32, 16, 64
CH = 8
HALF = SEQ // 2
NCH = HALF // CH
QG = 4
NQ = G // QG
WINDOWS = (2, 4, 8, 16)
HALO = 16
D_FF = 2816
NF = D_FF // P
TM = 256
TA = 256
TF = 1024
NP = SEQ // TF
EPS = 1e-6
MULT = [1, 2, 3, 4, 5, 6, 7, 8, 16, 32, 64, 128, 256, 512]
NM = len(MULT)

TWO_PI_PARTS = (6.28125, 0.0019350051879882812, 3.0198272e-07)
LN2_PARTS = (0.693359375, -2.12194440e-4)
ROUND = 12582912.0


class Chain:

    def __init__(self, sem):
        self.eng, self.sem, self.n = None, sem, 0

    def on(self, eng):
        self.eng = eng
        return self

    def link(self, ins):
        self.n += 1
        ins.then_inc(self.sem, 1)
        self.eng.wait_ge(self.sem, self.n)

    def done(self, ins, sem, n):
        ins.then_inc(sem, 1)
        self.eng.wait_ge(sem, n)


class Place:

    def __init__(self, nc, base):
        self.nc, self.base = nc, base

    def at(self, name, kib, shape, dtype=F32):
        size = int(np.prod(shape[1:])) * (2 if dtype == BF16 else 4)
        assert kib * 1024 + size <= SBUF_BYTES, name
        return self.nc.alloc_sbuf_tensor_at(name, list(shape), dtype, offset=self.base + int(kib * 1024))


SBUF_BYTES = 212000


def three(nc, out, wh, wl, xh, xl, first, last):
    nc.tensor.matmul(out, wh, xh, start=first, stop=False)
    nc.tensor.matmul(out, wh, xl, start=False, stop=False)
    return nc.tensor.matmul(out, wl, xh, start=False, stop=last)


def prepare(nc, S, I):
    m = S.map
    ps = S.ps
    sem = S.sem
    ctx = ExitStack()
    kern = m.at("kern", 3, [H, G, P])
    zpad = m.at("zpad", 19, [H, G, 112])
    b_in = [m.at(f"b_in{i}", 59.25 + 2 * i, [P, G, H]) for i in range(2)]
    c_rows = m.at("c_rows", 63.25, [P, 2, 4, 2 * NS])
    c_t = m.at("c_t", 67.25, [P, 2, G, H])
    t5 = [m.at(f"t5_{i}", 71.25 + 2 * i, [P, G, H]) for i in range(2)]
    lam_rows = m.at("lam_rows", 75.25, [G, 2, 2 * NS])
    x9 = m.at("x9", 77.25, [P, 9, G])
    y9 = m.at("y9", 78.5, [P, 9, G])
    x8 = m.at("x8", 79.75, [P, 8, G])
    y8 = m.at("y8", 80.75, [P, 8, G])
    gcol = m.at("norm_g", 81.75, [P, KD])
    csb = m.at("c_in", 82, [P, KD])
    d_t = m.at("d_t", 82.75, [H, G])
    sn, cs = S.sn, S.cs
    lam = m.at("lam", 87, [P, 2, G])
    dt = m.at("dt", 87.5, [P, G])
    ex = [m.at(f"exp_t{i}", 88 + 1.0 * i, [P, 8 * G]) for i in range(4)]
    exi = m.at("exp_i", 92, [P, 8 * G], I32)
    mag = m.at("mag", 93, [P, 8, G])
    magin = m.at("magin", 94, [P, 8, G])
    ang = m.at("ang", 95, [P, NM, G])
    angn = m.at("angn", 97, [P, NM, G])
    lc = m.at("lc", 99, [P, 8, G])
    ls = m.at("ls", 100, [P, 8, G])
    wre = m.at("wre", 101, [P, 8, G])
    wim = m.at("wim", 102, [P, 8, G])
    sm = [m.at(f"sm{i}", 103 + 0.25 * i, [P, G]) for i in range(8)]
    tw = [m.at(f"tw{i}", 105 + 1.0 * i, [P, 8, G]) for i in range(2)]
    ekern = m.at("ekern", 107, [H, G, H])
    t5p = [m.at(f"t5p_{i}", 109 + 2 * i, [P, G, H]) for i in range(2)]
    isb = m.at("isb", 119, [P, G, P])
    cl = m.at("cl", 135, [P, G, 9, H])
    wt = [m.at(f"ada_w{i}", 153 + 4 * i, [P, D]) for i in range(4)]
    brow = m.at("ada_brow", 169, [1, 2048])
    arow = m.at("ada_row", 177, [1, 2048])
    it = m.at("it", 185, [P, G, CH, H])
    csl = S.csl

    ld_c, ld_small, ld_w, ld_g = sem("p_ld_c"), sem("p_ld_small"), [sem(f"p_ld_w{i}") for i in range(4)], sem("p_ld_g")
    c_ready, w_used = sem("p_c_ready"), sem("p_w_used")
    id_ready, lamt, ct_ready, ang_ready, sin_ready = sem("p_id"), sem("p_lamt"), sem("p_ct"), sem("p_ang"), sem("p_sin")
    ct_copied, it_ready, itt, it_copied = sem("p_ctc"), sem("p_it"), sem("p_itt"), sem("p_itc")
    kr, kr_copied, kr_done, cl_ready = sem("p_kr"), sem("p_krc"), sem("p_krd"), sem("p_cl")
    row_out, col_mm, zp_ready, xy_ready = (sem("p_" + n) for n in ("row", "colmm", "zp", "xy"))
    ld_b, ld_lam, copied_d = sem("p_ldb"), sem("p_ldlam"), sem("p_copied_d")

    it_ready_d = sem("p_itd")
    w_ada = I["w_ada"][0].rearrange("(p k) n -> p k n", k=KD)
    SP_TOK = 1
    junk = m.at("p_junk", 113, [P, D], BF16)

    block = ctx.enter_context(nc.Block())

    @block.sync
    def _(sp):
        sp.dma_start(csb[:], I["c"][0].rearrange("(p k) -> p k", k=KD)).then_inc(ld_c, 16)
        sp.dma_start(brow[:], I["b_ada"][0:1, 0:2048]).then_inc(ld_b, 16)
        for n in range(2 * KD):
            k, v = divmod(n, 2)
            if n >= 4:
                sp.wait_ge(w_used, n - 3)
            sp.dma_start(wt[n % 4][:], w_ada[:, k, v * D:(v + 1) * D]).then_inc(ld_w[n % 4], 16)
        for b in range(2):
            sp.dma_start(S.xb[b][:], S.x_v[b]).then_inc(S.ld_x[b], 16)
        for k in range(4):
            if k == 2:
                sp.wait_ge(cl_ready, 9)
                sp.wait_ge(it_ready_d, SP_TOK)
            sp.dma_start(S.wraw[k][:], S.w_in[:, k, :]).then_inc(S.ld_w[k], 16)

    @block.scalar
    def _(act):
        d = act.dma_start
        for i, name in enumerate(("ssm_lam_re", "ssm_lam_im")):
            for dup in range(2):
                d(lam_rows[:, i, dup * NS:(dup + 1) * NS], I[name][0]).then_inc(ld_lam, 16)
        d(dt[:], I["ssm_log_dt"][0:1, :].to_broadcast([P, G])).then_inc(ld_lam, 16)
        d(gcol[:], I["g_norm_mix"][0].rearrange("(p k) -> p k", k=KD)).then_inc(ld_g, 16)
        d(S.g_ffn[:], I["g_norm_ffn"][0].rearrange("(p k) -> p k", k=KD)).then_inc(ld_g, 16)
        act.wait_ge(ld_c, 16)
        nc.scalar.activation(csl[:], csb[:], ACT.Silu).then_inc(c_ready, 1)
        for i, name in enumerate(("ssm_b_re", "ssm_b_im")):
            for dup in range(2):
                d(b_in[i][dup * NS:(dup + 1) * NS], I[name][0].rearrange("g p h -> p g h")).then_inc(ld_small, 16)
        for i, name in enumerate(("ssm_c_re", "ssm_c_im")):
            for dup in range(2):
                d(c_rows[:, i, :, dup * NS:(dup + 1) * NS],
                  I[name][0].rearrange("(a g) h p -> (g h) a p", a=4)).then_inc(ld_small, 16)
        d(d_t[:], I["ssm_d"][0].rearrange("(g h) -> h g", h=H), allow_slow_non_contiguous=True).then_inc(ld_small, 16)
        act.wait_ge(ang_ready, 1)
        nc.scalar.activation(sn[:], ang[:], ACT.Sin).then_inc(sin_ready, 1)
        nc.scalar.activation(cs[:], ang[:], ACT.Sin, scale=0.5).then_inc(sin_ready, 1)
        for i in range(2):
            act.wait_ge(ct_ready, 4 * (i + 1))
            nc.scalar.copy(c_t[:, i].rearrange("p g h -> p (g h)"), ps[1 + i][:]).then_inc(ct_copied, 1)
        act.wait_ge(zp_ready, 1)
        d(S.kpad[:, :, 0:112].rearrange("g h n -> h g n"), zpad[:]).then_inc(S.kpad_st, 16)

        act.wait_ge(w_used, 2 * KD)
        for i in range(4):
            last = nc.scalar.copy(arow[0:1, i * 512:(i + 1) * 512], ps[4 + i][0:1, :])
        last.then_inc(row_out, 1)
        squares(nc, S, act, 0, junk)
        for q in range(0, NQ, 2):
            act.wait_ge(itt, 4 * (q + 1))
            nc.scalar.copy(isb[:, 4 * q:4 * q + 4, :].rearrange("p g n -> p (g n)"), ps[q % 2][:]).then_inc(it_copied, 1)
        act.wait_ge(it_copied, NQ // 2)
        act.wait_ge(copied_d, NQ // 2)
        d(S.mats[:, 0, :], isb[:].rearrange("p g n -> p (g n)")).then_inc(S.mats_st, 16)
        act.wait_ge(cl_ready, 9)
        d(S.mats[:, 1, :].rearrange("p (g n) -> p g n", g=G), cl[:, :, 1:9, :].rearrange("p g t h -> p g (t h)")).then_inc(S.mats_st, 16)
        for q in range(0, NQ, 2):
            act.wait_ge(kr, 4 * (q + 1))
            nc.scalar.copy(kern[:, 4 * q:4 * q + 4, :].rearrange("p g n -> p (g n)"), ps[2 + q % 2][0:H, :]).then_inc(kr_copied, 1)
        act.wait_ge(kr_done, 1)
        d(S.kpad[:, :, 112:240].rearrange("g h n -> h g n"), kern[:]).then_inc(S.kpad_st, 16)

    @block.gpsimd
    def _(pool):
        ch = S.chain_g.on(pool)
        nc.gpsimd.memset(S.ones[:], 1.0).then_inc(id_ready, 1)
        nc.gpsimd.memset(zpad[:], 0.0).then_inc(zp_ready, 1)
        ch.link(nc.gpsimd.memset(S.ident[:], 0.0))
        ch.link(nc.gpsimd.memset(S.swap[:], 0.0))
        nc.gpsimd.affine_select(out=S.ident[:], in_=S.ident[:], compare_op=ALU.not_equal, fill=1.0, base=0,
                                pattern=[[-1, P]], channel_multiplier=1).then_inc(id_ready, 1)
        ch.link(nc.gpsimd.affine_select(out=S.swap[:], in_=S.swap[:], compare_op=ALU.not_equal, fill=1.0, base=-NS,
                                        pattern=[[-1, P]], channel_multiplier=1))
        nc.gpsimd.affine_select(out=S.swap[:], in_=S.swap[:], compare_op=ALU.not_equal, fill=-1.0, base=NS,
                                pattern=[[-1, P]], channel_multiplier=1).then_inc(id_ready, 1)
        TT = nc.gpsimd.tensor_tensor
        pool.wait_ge(ld_small, 16 * 9)
        pool.wait_ge(xy_ready, 1)
        for s in range(SP_TOK, CH):
            k = CH - 1 - s
            ch.link(TT(t5p[0][:], b_in[0][:], x8[:, k, :].unsqueeze(2).to_broadcast([P, G, H]), ALU.mult))
            ch.link(TT(t5p[1][:], b_in[1][:], y8[:, k, :].unsqueeze(2).to_broadcast([P, G, H]), ALU.mult))
            ch.done(TT(it[:, :, s, :], t5p[0][:], t5p[1][:], ALU.add), it_ready, s - SP_TOK + 1)

    @block.vector
    def _(dve):
        ch = S.chain_v.on(dve)
        L = ch.link
        V = nc.vector
        TT, TS, STT = V.tensor_tensor, V.tensor_scalar, V.scalar_tensor_tensor

        def expf(out, x, n):
            t, k, r, p = (e[:, 0:n] for e in ex)
            L(TS(x, x, 88.0, -87.0, ALU.min, ALU.max))
            L(TS(t, x, 1.0 / math.log(2.0), ROUND, ALU.mult, ALU.add))
            L(TS(k, t, -ROUND, None, ALU.add))
            L(STT(r, k, -LN2_PARTS[0], x, ALU.mult, ALU.add))
            L(STT(r, k, -LN2_PARTS[1], r, ALU.mult, ALU.add))
            L(TS(p, r, 1.0 / 5040, None, ALU.mult))
            for c in (720, 120, 24, 6, 2, 1):
                L(STT(p, p, 1.0 / c, r, ALU.add, ALU.mult))
            L(TS(t, k, 127.0, 8388608.0, ALU.add, ALU.mult))
            L(V.tensor_copy(exi[:, 0:n], t))
            L(STT(out, p, 1.0, exi[:, 0:n].bitcast(F32), ALU.add, ALU.mult))

        dve.wait_ge(ld_lam, 16 * 5)
        dve.wait_ge(lamt, 2)
        L(V.tensor_copy(lam[:].rearrange("p i g -> p (i g)"), ps[0][:, 0:2 * G]))
        L(V.tensor_copy(sm[7][:], dt[:]))
        expf(dt[:], sm[7][:], G)
        L(TT(sm[0][:], lam[:, 0], dt[:], ALU.mult))
        L(TT(sm[1][:], lam[:, 1], dt[:], ALU.mult))
        for tau in range(8):
            TS(magin[:, tau], sm[0][:], float(tau + 1), None, ALU.mult)
        for i, mu in enumerate(MULT):
            last = TS(ang[:, i], sm[1][:], float(mu), None, ALU.mult)
        L(last)
        L(TS(angn[:], ang[:], 1.0 / (2 * math.pi), ROUND, ALU.mult, ALU.add))
        L(TS(angn[:], angn[:], -ROUND, None, ALU.add))
        for c in TWO_PI_PARTS:
            L(STT(ang[:], angn[:], -c, ang[:], ALU.mult, ALU.add))
        ch.done(TS(ang[:], ang[:], 3.1415925, -3.1415925, ALU.min, ALU.max), ang_ready, 1)
        expf(mag[:].rearrange("p t g -> p (t g)"), magin[:].rearrange("p t g -> p (t g)"), 8 * G)
        dve.wait_ge(sin_ready, 2)
        L(TT(cs[:], cs[:], cs[:], ALU.mult))
        L(TS(cs[:], cs[:], -2.0, 1.0, ALU.mult, ALU.add))
        L(V.tensor_copy(S.rad8[:], mag[:, 7]))
        L(TT(lc[:], mag[:], cs[:, 0:8], ALU.mult))
        L(TT(ls[:], mag[:], sn[:, 0:8], ALU.mult))
        lre, lim = lam[:, 0], lam[:, 1]
        L(TT(sm[0][:], lre, lre, ALU.mult))
        L(TT(sm[1][:], lim, lim, ALU.mult))
        L(TT(sm[0][:], sm[0][:], sm[1][:], ALU.add))
        L(V.reciprocal(sm[1][:], sm[0][:]))
        L(TS(sm[2][:], lc[:, 0], -1.0, None, ALU.add))
        L(TT(sm[3][:], sm[2][:], lre, ALU.mult))
        L(TT(sm[4][:], ls[:, 0], lim, ALU.mult))
        L(TT(sm[3][:], sm[3][:], sm[4][:], ALU.add))
        L(TT(wre[:, 0], sm[3][:], sm[1][:], ALU.mult))
        L(TT(sm[3][:], ls[:, 0], lre, ALU.mult))
        L(TT(sm[4][:], sm[2][:], lim, ALU.mult))
        L(TT(sm[3][:], sm[3][:], sm[4][:], ALU.subtract))
        L(TT(wim[:, 0], sm[3][:], sm[1][:], ALU.mult))
        wr0 = wre[:, 0:1, :].to_broadcast([P, 7, G])
        wi0 = wim[:, 0:1, :].to_broadcast([P, 7, G])
        a, b = tw[0][:, 0:7], tw[1][:, 0:7]
        L(TT(a, lc[:, 0:7], wr0, ALU.mult))
        L(TT(b, ls[:, 0:7], wi0, ALU.mult))
        L(TT(wre[:, 1:8], a, b, ALU.subtract))
        L(TT(a, lc[:, 0:7], wi0, ALU.mult))
        L(TT(b, ls[:, 0:7], wr0, ALU.mult))
        L(TT(wim[:, 1:8], a, b, ALU.add))
        re, im = slice(0, NS), slice(NS, P)
        V.tensor_copy(x8[re], wre[re])
        V.tensor_copy(x8[im], wim[im])
        TS(y8[re], wim[re], -1.0, None, ALU.mult)
        V.tensor_copy(y8[im], wre[im]).then_inc(xy_ready, 1)
        V.tensor_copy(x9[re, 1:9], lc[re])
        TS(x9[im, 1:9], ls[im], -1.0, None, ALU.mult)
        TS(y9[re, 1:9], ls[re], -1.0, None, ALU.mult)
        TS(y9[im, 1:9], lc[im], -1.0, None, ALU.mult)
        V.memset(x9[re, 0], 1.0)
        V.memset(x9[im, 0], 0.0)
        V.memset(y9[re, 0], 0.0)
        L(V.memset(y9[im, 0], -1.0))
        dve.wait_ge(ld_small, 16 * 9)
        dve.wait_ge(ct_copied, 2)
        for tau in range(9):
            L(TT(t5[0][:], c_t[:, 0], x9[:, tau, :].unsqueeze(2).to_broadcast([P, G, H]), ALU.mult))
            L(TT(t5[1][:], c_t[:, 1], y9[:, tau, :].unsqueeze(2).to_broadcast([P, G, H]), ALU.mult))
            ch.done(TT(cl[:, :, tau, :], t5[0][:], t5[1][:], ALU.add), cl_ready, tau + 1)

        for s in range(SP_TOK):
            k = CH - 1 - s
            L(TT(t5[0][:], b_in[0][:], x8[:, k, :].unsqueeze(2).to_broadcast([P, G, H]), ALU.mult))
            L(TT(t5[1][:], b_in[1][:], y8[:, k, :].unsqueeze(2).to_broadcast([P, G, H]), ALU.mult))
            ch.done(TT(it[:, :, s, :], t5[0][:], t5[1][:], ALU.add), it_ready_d, s + 1)

        dve.wait_ge(ld_g, 32)
        dve.wait_ge(col_mm, 1)
        V.tensor_copy(S.b1[:], ps[4][:, 0:KD])
        STT(S.a1[:], ps[4][:, KD:2 * KD], 1.0, gcol[:], ALU.add, ALU.mult)

        normalise(nc, S, dve, L, 0)

        for q in range(1, NQ, 2):
            dve.wait_ge(itt, 4 * (q + 1))
            V.tensor_copy(isb[:, 4 * q:4 * q + 4, :].rearrange("p g n -> p (g n)"), ps[q % 2][:]).then_inc(copied_d, 1)
        for q in range(1, NQ, 2):
            dve.wait_ge(kr, 4 * (q + 1))
            V.tensor_copy(kern[:, 4 * q:4 * q + 4, :].rearrange("p g n -> p (g n)"), ps[2 + q % 2][0:H, :]).then_inc(copied_d, 1)

        dve.wait_ge(kr_copied, NQ // 2)
        dve.wait_ge(copied_d, NQ)
        L(TT(ekern[:], S.ident[0:H, 0:H].unsqueeze(1).to_broadcast([H, G, H]),
             d_t[:].unsqueeze(2).to_broadcast([H, G, H]), ALU.mult))
        TT(kern[:, :, 0:H], kern[:, :, 0:H], ekern[:], ALU.add).then_inc(kr_done, 1)

    @block.tensor
    def _(pe):
        T = nc.tensor
        pe.wait_ge(id_ready, 3)
        pe.wait_ge(ld_lam, 16 * 5)
        for i in range(2):
            T.transpose(ps[0][:, i * G:(i + 1) * G], lam_rows[:, i, :], S.ident[0:G, 0:G]).then_inc(lamt, 1)
        pe.wait_ge(c_ready, 1)
        pe.wait_ge(ld_b, 16)
        for i in range(4):
            T.matmul(ps[4 + i][0:1, :], S.ones[0:1, 0:1], brow[0:1, i * 512:(i + 1) * 512], start=True, stop=False)
        for n in range(2 * KD):
            k, v = divmod(n, 2)
            pe.wait_ge(ld_w[n % 4], 16 * (n // 4 + 1))
            for r in range(2):
                last = T.matmul(ps[4 + 2 * v + r][0:1, :], csl[:, k:k + 1], wt[n % 4][:, r * 512:(r + 1) * 512], start=False, stop=k == KD - 1)
            last.then_inc(w_used, 1)
            if n == KD:
                pe.wait_ge(ld_small, 16 * 9)
                for i in range(2):
                    for a in range(4):
                        T.transpose(ps[1 + i][:, a * P:(a + 1) * P], c_rows[:, i, a, :], S.ident[:]).then_inc(ct_ready, 1)
        pe.wait_ge(row_out, 1)
        for k in range(2 * KD):
            last = T.matmul(ps[4][:, k:k + 1], arow[0:1, bass.ds(k // KD * D + k % KD, P, step=KD)], S.ones[0:1, 0:1], start=True, stop=True)
        last.then_inc(col_mm, 1)
        pe.wait_ge(ct_copied, 2)
        pe.wait_ge(it_ready, CH - SP_TOK)
        pe.wait_ge(it_ready_d, SP_TOK)
        for q in range(NQ):
            if q >= 2:
                pe.wait_ge(copied_d if q % 2 else it_copied, q // 2)
            for g in range(4 * q, 4 * q + 4):
                T.transpose(ps[q % 2][:, (g % 4) * P:(g % 4 + 1) * P], it[:, g].rearrange("p s h -> p (s h)"),
                            S.ident[:]).then_inc(itt, 1)
        pe.wait_ge(cl_ready, 9)
        for q in range(NQ):
            if q >= 2:
                pe.wait_ge(copied_d if q % 2 else kr_copied, q // 2 + (NQ // 2 if q % 2 else 0))
            for g in range(4 * q, 4 * q + 4):
                T.matmul(ps[2 + q % 2][0:H, (g % 4) * P:(g % 4 + 1) * P], it[:, g, CH - 1, :],
                         cl[:, g, 0:8, :].rearrange("p t h -> p (t h)"), start=True, stop=True).then_inc(kr, 1)

    ctx.close()


def rstd_steps(nc, link, out, ss, tmp, half_root):
    V = nc.vector
    m, r = tmp
    link(V.tensor_scalar(m, ss, 1.0 / D, EPS, ALU.mult, ALU.add))
    link(V.reciprocal(r, m))
    half_root(out, r)
    link(V.tensor_tensor(r, out, out, ALU.mult))
    link(V.tensor_tensor(r, r, m, ALU.mult))
    link(V.tensor_scalar(r, r, -0.5, 1.5, ALU.mult, ALU.add))
    link(V.tensor_tensor(out, out, r, ALU.mult))


def squares(nc, S, act, b, junk):
    NJ = TA // P
    act.wait_ge(S.ld_x[b % 2], 16 * (b // 2 + 1))
    if b:
        act.wait_ge(S.xn, NJ * b)
    for j in range(NJ):
        nc.scalar.activation(junk[:], S.xb[b % 2][:, j], ACT.Square, accum_out=S.st[:, 0, j:j + 1]).then_inc(S.sq, 1)
        act.wait_ge(S.sq, NJ * b + j + 1)
    act.wait_ge(S.root_in, b + 1)
    nc.scalar.activation(S.st[:, 1], S.st[:, 3], ACT.Sqrt).then_inc(S.root, 1)


def normalise(nc, S, dve, link, b):
    NJ = TA // P
    dve.wait_ge(S.sq, NJ * (b + 1))

    def half_root(out, r):
        nc.vector.tensor_copy(S.st[:, 3], r).then_inc(S.root_in, 1)
        dve.wait_ge(S.root, b + 1)

    rstd_steps(nc, link, S.st[:, 1], S.st[:, 0], (S.st[:, 2], S.st[:, 4]), half_root)
    for j in range(NJ):
        nc.vector.tensor_scalar(S.xb[b % 2][:, j], S.xb[b % 2][:, j], S.st[:, 1, j:j + 1], None, ALU.mult).then_inc(S.xn, 1)


def project(nc, S, I):
    m, ps, sem = S.map, S.ps, S.sem
    ctx = ExitStack()
    NJ = TA // P
    NBA = SEQ // TA
    xb, ld_x, ld_w, xn = S.xb, S.ld_x, S.ld_w, S.xn
    NR = 6
    wraw = S.wraw + [m.at(f"a_wraw{4 + i}", 199 + 4 * i, [P, D]) for i in range(2)]
    hh = [m.at(f"a_hh{i}", 59.25 + 8 * i, [P, KD, TA], F32R) for i in range(2)]
    hl = [m.at(f"a_hl{i}", (75.25, 199)[i], [P, KD, TA], F32R) for i in range(2)]
    wl = m.at("a_wl", 87, [P, KD, D], F32R)
    wh = m.at("a_wh", 153, [P, KD, D], F32R)
    usb = [m.at(f"a_u{i}", 185 + 2 * i, [P, SSM_W]) for i in range(2)]
    full = [m.at(f"a_full{i}", 189 + 1 * i, [P, TA]) for i in range(2)]
    ET = 32
    et = m.at("e_tmp", 191, [P, G, ET])
    junk = m.at("a_junk", 195, [P, D], BF16)

    whi, wlo_u, wlo_p = sem("a_whi"), sem("a_wlou"), sem("a_wlop")
    ld_w = ld_w + [sem(f"a_ld_w{i}") for i in range(4, NR)]
    tr, fu, lo, mm_u, mm_p, ev_u, ev_p = (sem("a_" + n) for n in ("tr", "full", "lo", "mmu", "mmp", "ev_u", "ev_p"))
    u_st = [sem("a_ust0"), sem("a_ust1")]
    block = ctx.enter_context(nc.Block())

    @block.sync
    def _(sp):
        for k in range(4, KD):
            if k >= NR:
                sp.wait_ge(whi, k - NR + 1)
                sp.wait_ge(wlo_u, k - NR + 1)
                sp.wait_ge(wlo_p, k - NR + 1)
            sp.dma_start(wraw[k % NR][:], S.w_in[:, k, :]).then_inc(ld_w[k % NR], 16)
        for b in range(NBA):
            if b + 2 < NBA:
                sp.wait_ge(tr, KD * (b + 1))
                sp.dma_start(xb[b % 2][:], S.x_v[b + 2]).then_inc(ld_x[b % 2], 16)
            for j in range(NJ):
                n = NJ * b + j
                sp.wait_ge(ev_u, n + 1)
                sp.dma_start(S.u[n * P:(n + 1) * P, :], usb[n % 2][:]).then_inc(u_st[n % 2], 16)
        for i in range(2):
            sp.wait_ge(u_st[i], 16 * NBA * NJ // 2)

    @block.scalar
    def _(act):
        def weights(k):
            act.wait_ge(ld_w[k % NR], 16 * (k // NR + 1))
            nc.scalar.copy(wh[:, k], wraw[k % NR][:]).then_inc(whi, 1)

        def high(b, k):
            n = KD * b + k
            act.wait_ge(tr, n + 1)
            if n >= 2:
                act.wait_ge(lo, n - 1)
            nc.scalar.activation(full[k % 2][:], ps[k % 2][:, 0:TA], ACT.Identity, bias=S.b1[:, k:k + 1],
                                 scale=S.a1[:, k:k + 1]).then_inc(fu, 1)

        def evac(b):
            for j in range(NJ):
                n = NJ * b + j
                act.wait_ge(mm_u, n + 1)
                if n >= 2:
                    act.wait_ge(u_st[n % 2], 16 * (n // 2))
                nc.scalar.copy(usb[n % 2][:], ps[2 + j][:]).then_inc(ev_u, 1)

        for k in range(KD):
            weights(k)
            high(0, k)
        squares(nc, S, act, 1, junk)
        for b in range(NBA):
            if b + 1 < NBA:
                for k in range(KD):
                    high(b + 1, k)
            evac(b)
            if b + 2 < NBA:
                squares(nc, S, act, b + 2, junk)

    @block.gpsimd
    def _(pool):
        ch = S.chain_g.on(pool)
        L = ch.link
        Q = nc.gpsimd
        TT = Q.tensor_tensor
        for k in range(KD):
            pool.wait_ge(whi, k + 1)
            TT(wl[:, k, SSM_W:], wraw[k % NR][:, SSM_W:], wh[:, k, SSM_W:].bitcast(F32), ALU.subtract).then_inc(wlo_p, 1)
        ec, es, cs, sn = S.ec, S.es, S.cs, S.sn
        pool.wait_ge(S.mats_st, 32)
        L(Q.tensor_copy(ec[:, :, 0], cs[:, 7]))
        L(Q.tensor_copy(es[:, :, 0], sn[:, 7]))
        w = 1
        for lev in range(7):
            for a in range(0, w, ET):
                n = min(ET, w - a)
                src, dst, t = slice(a, a + n), slice(w + a, w + a + n), et[:, :, 0:n]
                cw = cs[:, 7 + lev, :].unsqueeze(2).to_broadcast([P, G, n])
                sw = sn[:, 7 + lev, :].unsqueeze(2).to_broadcast([P, G, n])
                L(TT(ec[:, :, dst], ec[:, :, src], cw, ALU.mult))
                L(TT(t, es[:, :, src], sw, ALU.mult))
                L(TT(ec[:, :, dst], ec[:, :, dst], t, ALU.subtract))
                L(TT(es[:, :, dst], es[:, :, src], cw, ALU.mult))
                L(TT(t, ec[:, :, src], sw, ALU.mult))
                L(TT(es[:, :, dst], es[:, :, dst], t, ALU.add))
            w *= 2

    @block.vector
    def _(dve):
        V = nc.vector
        ch = S.chain_v.on(dve)

        def low(b, k):
            n = KD * b + k
            dve.wait_ge(fu, n + 1)
            if b >= 2:
                dve.wait_ge(mm_p, 4 * (b - 1))
            ch.link(V.tensor_copy(hh[b % 2][:, k], full[k % 2][:]))
            V.tensor_tensor(hl[b % 2][:, k], full[k % 2][:], hh[b % 2][:, k].bitcast(F32), ALU.subtract).then_inc(lo, 1)

        def wlow(k):
            dve.wait_ge(whi, k + 1)
            V.tensor_tensor(wl[:, k, 0:SSM_W], wraw[k % NR][:, 0:SSM_W], wh[:, k, 0:SSM_W].bitcast(F32), ALU.subtract).then_inc(wlo_u, 1)

        def evac(b):
            for j in range(4):
                dve.wait_ge(mm_p, 4 * b + j + 1)
                V.tensor_copy(S.pt[:, j, HALO + b * TA:HALO + (b + 1) * TA], ps[4 + j][:, 0:TA]).then_inc(ev_p, 1)

        for k in range(KD):
            wlow(k)
            low(0, k)
        normalise(nc, S, dve, ch.link, 1)
        dve.wait_ge(S.kpad_st, 32)
        V.memset(S.pt[:, :, 0:HALO], 0.0)
        dve.wait_ge(wlo_p, KD)
        for b in range(NBA):
            if b + 1 < NBA:
                for k in range(KD):
                    low(b + 1, k)
            if b + 2 < NBA:
                normalise(nc, S, dve, ch.link, b + 2)
            evac(b)

    @block.tensor
    def _(pe):
        T = nc.tensor

        def transpose(b, k):
            n = KD * b + k
            if k == 0:
                pe.wait_ge(xn, NJ * (b + 1))
            if n >= 2:
                pe.wait_ge(fu, n - 1)
            for j in range(NJ):
                last = T.transpose(ps[k % 2][:, j * P:(j + 1) * P], xb[b % 2][:, j, bass.ds(k, P, step=KD)], S.ident[:])
            last.then_inc(tr, 1)

        def output_u(b, j):
            if b:
                pe.wait_ge(ev_u, NJ * (b - 1) + j + 1)
            js = slice(j * P, (j + 1) * P)
            for k in range(KD):
                if j == NJ - 1 and b + 1 < NBA:
                    transpose(b + 1, k)
                if j == 0:
                    pe.wait_ge(lo, KD * b + k + 1)
                    if b == 0:
                        pe.wait_ge(wlo_u, k + 1)
                last = three(nc, ps[2 + j][:], hh[b % 2][:, k, js], hl[b % 2][:, k, js], wh[:, k, 0:SSM_W],
                             wl[:, k, 0:SSM_W], k == 0, k == KD - 1)
            last.then_inc(mm_u, 1)

        def output_p(b, j):
            if b:
                pe.wait_ge(ev_p, 4 * (b - 1) + j + 1)
            elif j == 0:
                pe.wait_ge(wlo_p, KD)
            cs = slice(SSM_W + j * P, SSM_W + (j + 1) * P)
            for k in range(KD):
                last = three(nc, ps[4 + j][:, 0:TA], wh[:, k, cs], wl[:, k, cs], hh[b % 2][:, k, :], hl[b % 2][:, k, :],
                             k == 0, k == KD - 1)
            last.then_inc(mm_p, 1)

        for k in range(KD):
            transpose(0, k)
        for b in range(NBA):
            for j in range(NJ):
                output_u(b, j)
            for j in range(4):
                output_p(b, j)

    ctx.close()


def scan(nc, S, I):
    m, ps, sem = S.map, S.ps, S.sem
    ctx = ExitStack()
    NQ2 = 2 * NQ
    W = QG * NCH
    tm = m.at("s_t", 71, [P, G, P])
    im = m.at("s_i", 87, [P, G, P])
    om = m.at("s_o", 103, [P, G, P])
    ec, es = S.ec, S.es
    us = m.at("s_u", 151, [P, CH, SSM_W])
    yh = [m.at(f"s_y{i}", 167 + 4 * i, [P, CH, P]) for i in range(2)]
    ut = [m.at(f"s_ut{i}", 175 + 2 * i, [P, W]) for i in range(4)]
    ss = m.at("s_s", 183, [P, W])
    bb = m.at("s_b", 185, [P, QG, NCH])
    zz = [m.at(f"s_z{i}", 187 + 2 * i, [P, QG, NCH]) for i in range(2)]
    xx = [m.at(f"s_x{i}", 191 + 2.0625 * i, [P, QG, NCH + 1]) for i in range(2)]
    uq = m.at("s_uq", 195.125, [P, QG, CH, H])
    pl = [m.at(f"s_pl{i}", 197.125 + 4.0625 * i, [P, HALO + HALF]) for i in range(2)]
    carry = m.at("s_carry", 205.25, [P, G])
    rc = m.at("s_rc", 205.5, [P, 4, HALO])
    ri = m.at("s_ri", 205.75, [P, HALO], I32)
    rt = m.at("s_rt", 205.875, [P, HALO])

    UH = SSM_W // 2
    ld_u, ld_i, ld_m = ([sem(f"s_{n}{c}") for c in range(2)] for n in ("ld_u", "ld_i", "ld_m"))
    u_q, tr_u, ut_c, s_mm, s_c, s_j, m_used, z_ready, j2, x_ready, y_mm, y_act, y_tr, y_c = (
        sem("s_" + n) for n in ("u_q", "tr_u", "ut_c", "smm", "sc", "sj", "m_used", "z_ready", "j2",
                                "x_ready", "y_mm", "y_act", "y_tr", "y_c"))
    count, inv_count = sem("s_count"), sem("s_inv")
    u_v = S.u.rearrange("(h c t) n -> h c t n", h=2, t=CH)
    block = ctx.enter_context(nc.Block())

    @block.sync
    def _(sp):
        def load_u(half, c):
            sp.dma_start(us[:, :, c * UH:(c + 1) * UH], u_v[half][:, :, c * UH:(c + 1) * UH]).then_inc(ld_u[c], 16)

        for c in range(2):
            gs = slice(c * G // 2, (c + 1) * G // 2)
            load_u(0, c)
            if c == 0:
                sp.wait_ge(S.mats_st, 32)
            sp.dma_start(im[:, gs], S.mats[:, 0, :].rearrange("p (g n) -> p g n", g=G)[:, gs]).then_inc(ld_i[c], 16)
            sp.dma_start(om[:, gs], S.mats[:, 1, :].rearrange("p (g n) -> p g n", g=G)[:, gs]).then_inc(ld_m[c], 16)
            if c == 0:
                sp.wait_ge(S.kpad_st, 32)
            for s in range(CH):
                o = (CH - 1 - s) * H
                sp.dma_start(tm[s * H:(s + 1) * H, gs], S.kpad[gs, :, o:o + P].rearrange("g h n -> h g n")).then_inc(ld_m[c], 16)
        sp.dma_start(S.col[:, 0:8], I["b_glu"][0].rearrange("(k p) -> p k", p=P), allow_slow_non_contiguous=True).then_inc(S.ld_col, 16)
        sp.dma_start(S.col[:, 8:12], I["b_pool"][0].rearrange("g d -> d g"), allow_slow_non_contiguous=True).then_inc(S.ld_col, 16)
        sp.dma_start(S.col[:, 12:16], I["pool_scale"][0].rearrange("(g d) -> d g", g=4), allow_slow_non_contiguous=True).then_inc(S.ld_col, 16)
        for c in range(2):
            sp.wait_ge(u_q, (c + 1) * NQ // 2)
            load_u(1, c)
        wg = I["w_glu"][0].rearrange("(k p) n -> p k n", p=P)
        sp.wait_ge(s_mm, NQ + NQ // 2)
        for k in range(2):
            sp.dma_start(S.raw_glu[k][:], wg[:, k]).then_inc(S.ld_glu[k], 16)
        sp.wait_ge(y_mm, NQ + NQ // 2)
        for k in range(2, 4):
            sp.dma_start(S.raw_glu[k][:], wg[:, k]).then_inc(S.ld_glu[k], 16)

    def turns(flip, swap, swap_back, enter, leave, back):
        def do(step, i):
            if 0 <= i < NQ2:
                step(i)
        for i in range(-2, NQ2 + 2):
            do(flip, i + 2)
            do(swap, i + 1)
            do(swap_back, i)
            do(leave, i - 1)
            do(enter, i + 2)
            do(back, i - 2)

    @block.tensor
    def _(pe):
        T = nc.tensor

        def flip(i):
            pe.wait_ge(u_q, i + 1)
            if i:
                pe.wait_ge(ut_c, i)
            for g in range(QG):
                last = T.transpose(ps[0][:, g * P:(g + 1) * P], uq[:, g].rearrange("p t h -> p (t h)"), S.ident[:])
            last.then_inc(tr_u, 1)

        def enter(i):
            if i in (0, NQ // 2):
                pe.wait_ge(ld_i[i // (NQ // 2)], 16)
            pe.wait_ge(ut_c, i + 1)
            if i:
                pe.wait_ge(m_used, i)
            for g in range(QG):
                last = T.matmul(ps[1][:, g * P:(g + 1) * P], im[:, i % NQ * QG + g, :], ut[i % 4][:, g * P:(g + 1) * P],
                                start=True, stop=True)
            last.then_inc(s_mm, 1)

        def swap(i):
            pe.wait_ge(s_c, i + 1)
            if i:
                pe.wait_ge(m_used, i)
            T.matmul(ps[2][:], S.swap[:], ss[:], start=True, stop=True).then_inc(s_j, 1)

        def swap_back(i):
            pe.wait_ge(z_ready, i + 1)
            if i:
                pe.wait_ge(x_ready, i)
            T.matmul(ps[3][:], S.swap[:], zz[i % 2][:].rearrange("p g n -> p (g n)"), start=True, stop=True).then_inc(j2, 1)

        def leave(i):
            if i in (0, NQ // 2):
                pe.wait_ge(ld_m[i // (NQ // 2)], 16 * (CH + 1))
            pe.wait_ge(x_ready, i + 1)
            if i >= 2:
                pe.wait_ge(y_act, i - 1)
            for g in range(QG):
                gg = i % NQ * QG + g
                o = ps[4 + i % 2][:, g * P:(g + 1) * P]
                T.matmul(o, ut[i % 4][:, g * P:(g + 1) * P], tm[:, gg, :], start=True, stop=False)
                last = T.matmul(o, xx[i % 2][:, g, 0:NCH], om[:, gg, :], start=False, stop=True)
            last.then_inc(y_mm, 1)

        def back(i):
            if i % 2 == 0:
                return
            pe.wait_ge(y_act, i + 1)
            for r in range(2):
                if i > 1:
                    pe.wait_ge(y_c, i - 1 + r - 1)
                for t in range(4):
                    last = T.transpose(ps[6 + r][:, t * P:(t + 1) * P], yh[(i // 2) % 2][:, 4 * r + t, :], S.ident[:])
                last.then_inc(y_tr, 1)

        turns(flip, swap, swap_back, enter, leave, back)

    @block.scalar
    def _(act):
        def gather(i):
            half, q = divmod(i, NQ)
            if q % (NQ // 2) == 0:
                act.wait_ge(ld_u[q // (NQ // 2)], 16 * (half + 1))
            if i:
                act.wait_ge(tr_u, i)
            c = q * QG * H
            nc.scalar.copy(uq[:], us[:, :, c:c + QG * H].rearrange("p t (g h) -> p g t h", g=QG)).then_inc(u_q, 1)

        def flipped(i):
            act.wait_ge(tr_u, i + 1)
            if i >= 4:
                act.wait_ge(y_mm, i - 3)
            nc.scalar.copy(ut[i % 4][:], ps[0][:]).then_inc(ut_c, 1)
            if i + 1 < NQ2:
                gather(i + 1)

        def entered(i):
            act.wait_ge(s_mm, i + 1)
            if i:
                act.wait_ge(s_j, i)
            nc.scalar.copy(ss[:], ps[1][:]).then_inc(s_c, 1)

        def gelu(i):
            act.wait_ge(y_mm, i + 1)
            if i >= 4:
                act.wait_ge(y_tr, 2 * (i // 2 - 1))
            f = (i % 2) * QG * H
            for g in range(QG):
                last = nc.scalar.activation(yh[(i // 2) % 2][:, :, f + g * H:f + (g + 1) * H],
                                            ps[4 + i % 2][:, g * P:(g + 1) * P].rearrange("p (t h) -> p t h", t=CH),
                                            ACT.Gelu_apprx_tanh)
            last.then_inc(y_act, 1)

        def back(i):
            if i % 2 == 0:
                return
            half, q = divmod(i, NQ)
            for r in range(2):
                act.wait_ge(y_tr, i - 1 + r + 1)
                dst = S.yt[:, q // 2, half * HALF:(half + 1) * HALF].rearrange("p (c t) -> p t c", t=CH)
                nc.scalar.copy(dst[:, 4 * r:4 * r + 4, :], ps[6 + r][:].rearrange("p (t c) -> p t c", t=4)).then_inc(y_c, 1)

        gather(0)
        turns(flipped, lambda i: None, lambda i: None, entered, gelu, back)

    @block.vector
    def _(dve):
        V = nc.vector
        ch = S.chain_v.on(dve)
        L = ch.link
        TT = V.tensor_tensor
        f = "p g n -> p (g n)"

        def trig(i):
            gs = slice(i % NQ * QG, (i % NQ + 1) * QG)
            return gs, ec[:, gs, :].rearrange(f), es[:, gs, :].rearrange(f)

        def scan_item(i):
            gs, cosq, sinq = trig(i)
            zf, bf = zz[i % 2][:].rearrange(f), bb[:].rearrange(f)
            dve.wait_ge(s_c, i + 1)
            if i >= 2:
                dve.wait_ge(j2, i - 1)
            TT(zf, ps[1][:], cosq, ALU.mult)
            dve.wait_ge(s_j, i + 1)
            L(TT(bf, ps[2][:], sinq, ALU.mult))
            V.tensor_tensor(zf, zf, bf, ALU.add).then_inc(m_used, 1)
            dve.wait_ge(m_used, i + 1)
            for g in range(QG):
                gg = i % NQ * QG + g
                last = V.tensor_tensor_scan(zz[i % 2][:, g, :], S.rad8[:, gg:gg + 1].to_broadcast([P, NCH]),
                                            zz[i % 2][:, g, :], carry[:, gg:gg + 1], ALU.mult, ALU.add)
            last.then_inc(z_ready, 1)

        def turn_on(i):
            gs, cosq, sinq = trig(i)
            x = xx[i % 2]
            if i >= 2:
                dve.wait_ge(y_mm, i - 1)
            V.tensor_copy(x[:, :, 0:1], carry[:, gs].unsqueeze(2))
            dve.wait_ge(z_ready, i + 1)
            TT(x[:, :, 1:NCH + 1], zz[i % 2][:], ec[:, gs, :], ALU.mult)
            dve.wait_ge(j2, i + 1)
            L(TT(bb[:].rearrange(f), ps[3][:], sinq, ALU.mult))
            L(TT(x[:, :, 1:NCH + 1], x[:, :, 1:NCH + 1], bb[:], ALU.subtract))
            V.tensor_copy(carry[:, gs].unsqueeze(2), x[:, :, NCH:NCH + 1]).then_inc(x_ready, 1)
            if i + 1 == NQ:
                dve.wait_ge(x_ready, NQ)

        L(V.memset(carry[:], 0.0))
        dve.wait_ge(count, 4)
        V.reciprocal(rc[:], rc[:]).then_inc(inv_count, 1)
        turns(lambda i: None, scan_item, turn_on, lambda i: None, lambda i: None, lambda i: None)

    @block.gpsimd
    def _(pool):
        ch = S.chain_g.on(pool)
        L = ch.link
        Q = nc.gpsimd
        L(Q.iota(ri[:], [[1, HALO]], base=1, channel_multiplier=0))
        L(Q.tensor_copy(rt[:], ri[:]))
        for w in range(4):
            Q.tensor_scalar(rc[:, w], rt[:], float(WINDOWS[w]), None, ALU.min).then_inc(count, 1)
        pool.wait_ge(inv_count, 1)
        for w, win in enumerate(WINDOWS):
            for half in (1, 0):
                o = half * HALF
                cur, sh, n = S.pt[:, w, o:o + HALO + HALF], 1, 0
                while sh < win:
                    nxt, lo = pl[n % 2], 2 * sh - 1
                    L(Q.tensor_tensor(nxt[:, lo:], cur[:, lo:], cur[:, lo - sh:HALO + HALF - sh], ALU.add))
                    cur, sh, n = nxt[:], sh * 2, n + 1
                if half == 0:
                    L(Q.tensor_tensor(rt[:], cur[:, HALO:2 * HALO], rc[:, w], ALU.mult))
                L(Q.tensor_scalar(cur[:, HALO:], cur[:, HALO:], 1.0 / win, None, ALU.mult))
                if half == 0:
                    L(Q.tensor_copy(cur[:, HALO:2 * HALO], rt[:]))
                L(Q.tensor_tensor(S.pt[:, w, o + HALO:o + HALO + HALF], cur[:, HALO:],
                                  S.pt[:, w, o + HALO:o + HALO + HALF], ALU.subtract))

    ctx.close()


def mix(nc, S, I):
    m, ps, sem = S.map, S.ps, S.sem
    KG = SSM_W // P
    KM = KD
    NBM = SEQ // TM
    S.oh = m.at("m_oh", 67.25, [P, KM, D], F32R)
    S.ol = m.at("m_ol", 99.25, [P, KM, D], F32R)
    gh = m.at("m_gh", 131.25, [P, KG, 2 * SSM_W], F32R)
    gl = m.at("m_gl", 147.25, [P, KG, 2 * SSM_W], F32R)
    yh = [m.at(f"m_yh{i}", 163.25 + 4 * i, [P, KG, TM], F32R) for i in range(2)]
    yl = [m.at(f"m_yl{i}", 171.25 + 4 * i, [P, KG, TM], F32R) for i in range(2)]
    raw = [m.at(f"m_raw{i}", 179.25 + 4 * i, [P, D]) for i in range(2)]
    sig = [m.at(f"m_sig{i}", 187.25 + i, [P, TM]) for i in range(2)]
    wp = m.at("m_wp", 189.25, [P, 4, P])
    col = S.col
    wt = [m.at(f"m_ada{i}", 191.25 + 4 * i, [P, D]) for i in range(2)]
    ada = m.at("m_ada_sum", 199.25, [P, D])
    VECS = (3, 4, 2, 5)
    NT = KD + 1
    SV = 4 * NBM // len(VECS)
    SU = SV - 3

    NW = KG + KM
    ld_g, ld_wp = [sem(f"m_ld{i}") for i in range(2)], sem("m_ldwp")
    whi, wlo, wlo_d, yhi, ylo, mm, sg, ys, pmm, pev = (
        sem("m_" + n) for n in ("whi", "wlo", "wlod", "yhi", "ylo", "mm", "sg", "ys", "pmm", "pev"))
    ld_a = [sem("m_lda0"), sem("m_lda1")]
    a_used, a_sum, a_out, g_st = sem("m_aused"), sem("m_asum"), sem("m_aout"), sem("m_gst")
    ctx = ExitStack()
    block = ctx.enter_context(nc.Block())

    def raw_of(n):
        return S.raw_glu[n] if n < KG else raw[(n - KG) % 2]

    def raw_landed(n):
        return (S.ld_glu[n], 16) if n < KG else (ld_g[(n - KG) % 2], 16 * ((n - KG) // 2 + 1))

    def weight_of(n):
        return (gh, gl, n) if n < KG else (S.oh, S.ol, n - KG)

    def tiles(slot):
        v, i = divmod(slot, SV)
        i -= 1
        if not 0 <= i < SU:
            return range(0)
        return range(v * NT + i * NT // SU, v * NT + (i + 1) * NT // SU)

    @block.sync
    def _(sp):
        wo = I["w_out"][0].rearrange("(k p) n -> p k n", p=P)
        w_ada = I["w_ada"][0].rearrange("(p k) n -> p k n", k=KD)

        def load_w(n):
            if n >= KG + 2:
                sp.wait_ge(whi, n - 1)
                sp.wait_ge(wlo, n - 1)
            sp.dma_start(raw[(n - KG) % 2][:], wo[:, n - KG]).then_inc(ld_g[(n - KG) % 2], 16)

        def load_a(n):
            v, k = divmod(n, NT)
            if n >= 2:
                sp.wait_ge(a_used, n - 1)
            c = slice(VECS[v] * D, (VECS[v] + 1) * D)
            if k < KD:
                sp.dma_start(wt[n % 2][:], w_ada[:, k, c]).then_inc(ld_a[n % 2], 16)
            else:
                sp.dma_start(wt[n % 2][0:1, :], I["b_ada"][0:1, c]).then_inc(ld_a[n % 2], 16)

        load_a(0)
        load_a(1)
        load_w(KG)
        load_w(KG + 1)
        for b in range(NBM):
            for t in range(4):
                slot = 4 * b + t
                for n in tiles(slot):
                    if n + 2 < len(VECS) * NT:
                        load_a(n + 2)
                if slot == 3 * SV:
                    sp.wait_ge(a_out, 3)
                    sp.dma_start(S.gates[0:1, :], ada[0:1, :]).then_inc(g_st, 16)
            if b + 2 < KM:
                load_w(KG + b + 2)
        sp.wait_ge(a_out, 4)
        sp.dma_start(S.gates[1:2, :], ada[0:1, :]).then_inc(g_st, 16)
        sp.wait_ge(g_st, 32)

    @block.scalar
    def _(act):
        act.dma_start(wp[:], I["w_pool"][0].rearrange("g c d -> c g d")).then_inc(ld_wp, 16)
        act.wait_ge(S.ld_col, 48)

        def weight(n):
            h, k = weight_of(n)[0], weight_of(n)[2]
            if n == KG:
                act.wait_ge(wlo, KG)
                act.wait_ge(wlo_d, KG)
            act.wait_ge(*raw_landed(n))
            nc.scalar.copy(h[:, k], raw_of(n)[:]).then_inc(whi, 1)

        def split(b):
            if b >= 2:
                act.wait_ge(mm, 8 * (b - 1))
            nc.scalar.copy(yh[b % 2][:], S.yt[:, :, b * TM:(b + 1) * TM]).then_inc(yhi, 1)

        split(0)
        for n in range(KG):
            weight(n)
        for b in range(NBM):
            if b + 1 < NBM:
                split(b + 1)
            for t in range(4):
                i = 4 * b + t
                act.wait_ge(mm, 2 * i + 2)
                if i >= 2:
                    act.wait_ge(ys, i - 1)
                nc.scalar.activation(sig[i % 2][:], ps[2 * (i % 2) + 1][:, 0:TM], ACT.Sigmoid, bias=col[:, 4 + t:5 + t]).then_inc(sg, 1)
            weight(KG + b)

    @block.gpsimd
    def _(pool):
        for n in range(NW):
            h, l, k = weight_of(n)
            c = slice(512 if n < KG else 0, D)
            if n == KG:
                pool.wait_ge(wlo_d, KG)
            pool.wait_ge(whi, n + 1)
            nc.gpsimd.tensor_tensor(l[:, k, c], raw_of(n)[:, c], h[:, k, c].bitcast(F32), ALU.subtract).then_inc(wlo, 1)

    @block.vector
    def _(dve):
        V = nc.vector
        dve.wait_ge(S.ld_col, 48)

        def split(b):
            if b >= 2:
                dve.wait_ge(mm, 8 * (b - 1))
            dve.wait_ge(yhi, b + 1)
            V.tensor_tensor(yl[b % 2][:], S.yt[:, :, b * TM:(b + 1) * TM], yh[b % 2][:].bitcast(F32), ALU.subtract).then_inc(ylo, 1)

        def ada_tile(n):
            v, k = divmod(n, NT)
            dve.wait_ge(ld_a[n % 2], 16 * (n // 2 + 1))
            if k == 0:
                if v == 3:
                    dve.wait_ge(g_st, 16)
                ins = V.tensor_scalar(ada[:], wt[n % 2][:], S.csl[:, 0:1], None, ALU.mult)
            elif k < KD:
                ins = V.scalar_tensor_tensor(ada[:], wt[n % 2][:], S.csl[:, k:k + 1], ada[:], ALU.mult, ALU.add)
            else:
                ins = V.tensor_tensor(ada[0:1, :], ada[0:1, :], wt[n % 2][0:1, :], ALU.add)
            ins.then_inc(a_used, 1)
            dve.wait_ge(a_used, n + 1)

        def ada_out(v):
            dve.wait_ge(a_sum, v + 1)
            if v == 0:
                last = V.tensor_copy(S.b2[:], ps[6][:, 0:KD])
            elif v == 1:
                last = V.scalar_tensor_tensor(S.a2[:], ps[6][:, 0:KD], 1.0, S.g_ffn[:], ALU.add, ALU.mult)
            else:
                V.tensor_copy(ada[0:1, 0:512], ps[6][0:1, :])
                last = V.tensor_copy(ada[0:1, 512:D], ps[7][0:1, :])
            last.then_inc(a_out, 1)

        split(0)
        for n in range(KG):
            dve.wait_ge(whi, n + 1)
            V.tensor_tensor(gl[:, n, 0:512], raw_of(n)[:, 0:512], gh[:, n, 0:512].bitcast(F32), ALU.subtract).then_inc(wlo_d, 1)
        for b in range(NBM):
            bs = slice(b * TM, (b + 1) * TM)
            if b + 1 < NBM:
                split(b + 1)
            for t in range(4):
                i = 4 * b + t
                dve.wait_ge(pmm, i + 1)
                V.tensor_scalar(S.pt[:, t, HALO + b * TM:HALO + (b + 1) * TM], ps[4 + i % 2][:, 0:TM], col[:, 8 + t:9 + t],
                                col[:, 12 + t:13 + t], ALU.add, ALU.mult).then_inc(pev, 1)
                dve.wait_ge(sg, i + 1)
                V.scalar_tensor_tensor(S.yt[:, t, bs], ps[2 * (i % 2)][:, 0:TM], col[:, t:t + 1], sig[i % 2][:], ALU.add,
                                       ALU.mult).then_inc(ys, 1)
                if i and i % SV == 0:
                    ada_out(i // SV - 1)
                for n in tiles(i):
                    ada_tile(n)
        ada_out(3)

    @block.tensor
    def _(pe):
        T = nc.tensor

        def ada_sum(v):
            pe.wait_ge(a_used, NT * (v + 1))
            if v:
                pe.wait_ge(a_out, v)
            if v < 2:
                for k in range(KD):
                    last = T.matmul(ps[6][:, k:k + 1], ada[:, bass.ds(k, P, step=KD)], S.ones[:, 0:1], start=True, stop=True)
            else:
                for r in range(2):
                    last = T.matmul(ps[6 + r][0:1, :], S.ones[:, 0:1], ada[:, r * 512:(r + 1) * 512], start=True, stop=True)
            last.then_inc(a_sum, 1)

        def pooling(i):
            b, w = divmod(i, 4)
            if i >= 2:
                pe.wait_ge(pev, i - 1)
            T.matmul(ps[4 + i % 2][:, 0:TM], wp[:, w], S.pt[:, w, HALO + b * TM:HALO + (b + 1) * TM], start=True,
                     stop=True).then_inc(pmm, 1)

        pe.wait_ge(ld_wp, 16)
        for i in range(4 * NBM):
            b, t = divmod(i, 4)
            pooling(i)
            if i == 0:
                pe.wait_ge(wlo, KG)
                pe.wait_ge(wlo_d, KG)
            if i and i % SV == 0:
                ada_sum(i // SV - 1)
            if t == 0:
                pe.wait_ge(ylo, b + 1)
            if i >= 2:
                pe.wait_ge(ys, i - 1)
            for part in range(2):
                c = slice(part * SSM_W + t * P, part * SSM_W + (t + 1) * P)
                for k in range(KG):
                    last = three(nc, ps[2 * (i % 2) + part][:, 0:TM], gh[:, k, c], gl[:, k, c], yh[b % 2][:, k], yl[b % 2][:, k],
                                 k == 0, k == KG - 1)
                last.then_inc(mm, 1)
        ada_sum(3)

    ctx.close()


def ffn(nc, S, I):
    m, ps, sem = S.map, S.ps, S.sem
    ctx = ExitStack()
    NT = TF // P
    NO = 2 * NT
    NM = SEQ // P
    KM = KD
    h2h = m.at("f_h2h", 3, [P, KD, TF], F32R)
    h2l = m.at("f_h2l", 35, [P, KD, TF], F32R)
    acc = m.at("f_acc", 67.25, [P, NT, D])
    ah = [m.at(f"f_ah{i}", 99.25 + 8 * i, [P, TF], F32R) for i in range(2)]
    al = [m.at(f"f_al{i}", 103.25 + 8 * i, [P, TF], F32R) for i in range(2)]
    uh = [m.at(f"f_uh{i}", (143.25, 115.25)[i], [P, 2, KD, P], F32R) for i in range(2)]
    ul = [m.at(f"f_ul{i}", (151.25, 123.25)[i], [P, 2, KD, P], F32R) for i in range(2)]
    slot = [m.at(f"f_slot{i}", 131.25 + 4 * i, [P, D]) for i in range(3)]
    mh = [m.at(f"o_mh{i}", 159.25 + 8 * i, [P, KM, P], F32R) for i in range(2)]
    ml = [m.at(f"o_ml{i}", 163.25 + 8 * i, [P, KM, P], F32R) for i in range(2)]
    xt = [m.at(f"o_x{i}", 175.25 + 4 * i, [P, D]) for i in range(2)]
    xg = m.at("o_xg", 183.25, [P, D])
    gb = m.at("o_gate", 187.25, [P, D])
    xn = m.at("o_xn", 191.25, [P, D])
    ht = m.at("o_ht", 195.25, [P, KD, P])
    junk = m.at("o_junk", 199.25, [P, D], BF16)
    dh = [m.at(f"f_dh{i}", 159.25 + 8 * i, [P, D], F32R) for i in range(2)]
    dl = [m.at(f"f_dl{i}", 163.25 + 8 * i, [P, D], F32R) for i in range(2)]
    gs = m.at("f_gs", 175.25, [P, 2 + TF])
    cv = [m.at(f"f_cv{i}", 179.375 + 2 * i, [P, 512]) for i in range(2)]
    full = [m.at(f"f_full{i}", 183.375 + 2 * i, [P, 512]) for i in range(2)]
    gt = m.at("f_gt", 187.375, [P, D])
    gf = m.at("f_gf", 191.375, [P, D])
    xr = [m.at(f"f_xr{i}", 195.375 + 4 * i, [P, D]) for i in range(2)]
    xl = m.at("f_xl", 3, [P, NT, D])
    halo = m.at("f_halo", 203.5, [P, NF, 2])
    cw = m.at("f_cw", 203.75, [P, 4, NF])
    cj = [m.at(f"f_cj{i}", 204.125 + 0.0625 * i, [P, 4]) for i in range(2)]
    st = m.at("f_stat", 204.25, [P, 8, NM])
    crow = m.at("f_crow", 204.75, [4 * NF, P])

    ld_b, ld_x, x_st, h_st = sem("o_ldb"), [sem("o_ldx0"), sem("o_ldx1")], [sem("o_xst0"), sem("o_xst1")], sem("o_hst")
    mhi, mlo, om, xg_r, x1r, sq, xnr, tr, hta, htb = (
        sem("o_" + n) for n in ("mhi", "mlo", "mm", "xg", "x1", "sq", "xn", "tr", "hta", "htb"))
    root_in, root = S.root_in, S.root
    R1, R2 = SEQ // TA, SEQ // TA + NM
    ld_cw, cwt, cw_ok = sem("f_ldcw"), sem("f_cwt"), sem("f_cwok")
    ld_s = [sem(f"f_ld{i}") for i in range(3)]
    ld_h = [sem(f"f_ldh{i}") for i in range(KD // 2)]
    h2hi, h2lo, h2lo_d, uhi, ulo, dhi, dlo, upg, upv, gev, chn, cvd, hal, sil, prod, vhi, vlo, dmm, dad = (
        sem("f_" + n) for n in ("h2hi", "h2lo", "h2lod", "uhi", "ulo", "dhi", "dlo", "upg", "upv", "gev", "chn", "cvd", "hal",
                                "sil", "prod", "vhi", "vlo", "dmm", "dad"))
    ld_g, sq2, oo_r, o_st = (
        sem("z_" + n) for n in ("ldg", "sq", "oo", "ost"))
    ld_r, t1 = ([sem(f"z_{n}{i}") for i in range(2)] for n in ("ldr", "t1_"))

    w_up = I["w_up"][0].rearrange("(p k) n -> p k n", k=KD)
    w_dn = I["w_down"][0]
    V, A, T, Q = nc.vector, nc.scalar, nc.tensor, nc.gpsimd
    KP = (4, 6)
    assert NP == len(KP)

    def landed(pas, j):
        return 16 * (pas * NF + j + 1)

    block = ctx.enter_context(nc.Block())

    def residual_of(eng, pas, t):
        if pas == NP - 1:
            eng.wait_ge(ld_h[t // 4], 16 * (NP + 1))
            return xl[:, t]
        eng.wait_ge(ld_r[t % 2], 16 * ((pas * NT + t) // 2 + 1))
        return xr[t % 2][:]

    def tail_dmas(sp, pas):
        def load_r(t):
            n = pas * NT + t
            if n >= 2:
                sp.wait_ge(t1[t % 2], n // 2)
            sp.dma_start(xr[t % 2][:], S.x1[n * P:(n + 1) * P, :]).then_inc(ld_r[t % 2], 16)

        def store_o(t):
            n = pas * NT + t
            sp.wait_ge(oo_r, n + 1)
            sp.dma_start(I["out"][0, n * P:(n + 1) * P, :], acc[:, t]).then_inc(o_st, 16)

        if pas == NP - 1:
            sp.wait_ge(upv, 2 * NP * NF)
            for g in range(2):
                n = pas * NT + 4 * g
                sp.dma_start(xl[:, 4 * g:4 * g + 4], S.x1[n * P:(n + 4) * P, :].rearrange("(t p) d -> p t d", p=P)).then_inc(ld_h[g], 16)
            for t in range(NT):
                store_o(t)
            return
        for t in range(6):
            load_r(t)
        for t in range(4):
            store_o(t)
        for t in range(6, NT):
            load_r(t)
        for t in range(4, NT):
            store_o(t)

    @block.sync
    def _(sp):
        for i in range(3):
            sp.dma_start(crow[i * NF:(i + 1) * NF, :], I["w_conv"][0, i].rearrange("(j p) -> j p", p=P)).then_inc(ld_cw, 16)
        sp.dma_start(crow[3 * NF:4 * NF, :], I["b_conv"][0].rearrange("(j p) -> j p", p=P)).then_inc(ld_cw, 16)
        sp.dma_start(gb[:], S.gates[0:1, :].to_broadcast([P, D])).then_inc(ld_b, 16)

        def load_x(n):
            if n >= 2:
                sp.wait_ge(xnr, n - 1)
                sp.wait_ge(x_st[n % 2], 16 * (n // 2))
            sp.dma_start(xt[n % 2][:], I["x"][0, n * P:(n + 1) * P, :]).then_inc(ld_x[n % 2], 16)

        def store_h(n):
            sp.wait_ge(hta, n + 1)
            sp.wait_ge(htb, n + 1)
            sp.dma_start(S.h2[:, :, n * P:(n + 1) * P], ht[:]).then_inc(h_st, 16)

        def unit(i, src):
            sp.dma_start(slot[i][:] if len(src.shape) == 2 else slot[i][:].rearrange("p (k n) -> p k n", k=KD), src).then_inc(ld_s[i], 16)

        def load_u(pas, j, freed, between=None):
            for part in (1, 0):
                i = 1 - part
                sp.wait_ge(uhi, freed(part)[0])
                sp.wait_ge(ulo, freed(part)[0])
                unit(i, w_up[:, :, bass.ds((j + NF if part else j) * P, P)])
            if between:
                between()
            sp.wait_ge(dhi, freed(0)[1])
            sp.wait_ge(dlo, freed(0)[1])
            unit(2, w_dn[bass.ds(j * P, P), :])

        def load_h(pas):
            for i in range(KD // 2):
                ks = slice(2 * i, 2 * i + 2)
                sp.dma_start(h2l[:, ks].bitcast(F32), S.h2[:, ks, pas * TF:(pas + 1) * TF]).then_inc(ld_h[i], 16)

        load_x(0)
        load_x(1)
        for n in range(NM):
            if n == NM - 1:
                sp.wait_ge(h_st, 16 * NT)
                sp.wait_ge(mlo, 2 * NM)
                load_h(0)
            sp.wait_ge(x1r, 2 * (n + 1))
            sp.dma_start(S.x1[n * P:(n + 1) * P, :], xt[n % 2][:]).then_inc(x_st[n % 2], 16)
            if n + 2 < NM:
                load_x(n + 2)
            if n >= 1:
                store_h(n - 1)
            if n == 2:
                unit(0, w_up[:, :, D_FF:D_FF + P])
                unit(1, w_up[:, :, 0:P])
                unit(2, w_dn[0:P, :])
        for pas in range(NP):
            if pas:
                for i in range(2):
                    sp.wait_ge(uhi, 2 * pas * NF - 1 + i)
                    sp.wait_ge(ulo, 2 * pas * NF - 1 + i)
                    unit(i, w_up[:, :, (1 - i) * D_FF:(1 - i) * D_FF + P])
                if pas == 1:
                    sp.wait_ge(h_st, 16 * NM)
                sp.wait_ge(upv, 2 * pas * NF)
                load_h(pas)
                sp.wait_ge(dhi, pas * NF)
                sp.wait_ge(dlo, pas * NF)
                unit(2, w_dn[0:P, :])

            def freed_of(pas, j):
                return lambda part: (2 * (pas * NF + j - 1) + (1 if part else 2), pas * NF + j)

            load_u(pas, 1, freed_of(pas, 1), (lambda: tail_dmas(sp, pas - 1)) if pas else (lambda: store_h(NM - 1)))
            if pas == 0:
                sp.wait_ge(xnr, NM)
                sp.wait_ge(hta, NM)
                sp.wait_ge(x_st[0], 16 * NM // 2)
                sp.wait_ge(x_st[1], 16 * NM // 2)
                sp.wait_ge(h_st, 16 * NM)
                sp.dma_start(gt[:], S.gates[1:2, :].to_broadcast([P, D])).then_inc(ld_g, 16)
                sp.dma_start(gf[:], I["g_norm_final"].rearrange("(a d) -> a d", a=1).to_broadcast([P, D])).then_inc(ld_g, 16)
            with sp.Fori(0, NF // 2 - 1) as it:
                load_u(pas, 2 * it + 2, freed_of(pas, 2 * it + 2))
                load_u(pas, 2 * it + 3, freed_of(pas, 2 * it + 3))
        tail_dmas(sp, NP - 1)
        sp.wait_ge(o_st, 16 * NT * NP)

    @block.scalar
    def _(act):
        def split(n):
            if n >= 2:
                act.wait_ge(om, 2 * (n - 1))
            A.copy(mh[n % 2][:, 0:4], S.yt[:, :, n * P:(n + 1) * P]).then_inc(mhi, 1)
            A.copy(mh[n % 2][:, 4:8], S.pt[:, :, HALO + n * P:HALO + (n + 1) * P]).then_inc(mhi, 1)

        def stats(n):
            act.wait_ge(x1r, 2 * (n + 1))
            A.activation(junk[:], xt[n % 2][:], ACT.Square, accum_out=st[:, 0, n:n + 1]).then_inc(sq, 1)
            act.wait_ge(root_in, R1 + n + 1)
            A.activation(st[:, 1, n:n + 1], st[:, 3, n:n + 1], ACT.Sqrt).then_inc(root, 1)

        def transposed(n):
            act.wait_ge(tr, n + 1)
            if n:
                act.wait_ge(h_st, 16 * n)
            for k in range(4):
                last = A.activation(ht[:, k], ps[6][:, k * P:(k + 1) * P], ACT.Identity, bias=S.b2[:, k:k + 1], scale=S.a2[:, k:k + 1])
            last.then_inc(hta, 1)

        def up_high(pas, j, b, guard):
            for part in (1, 0):
                i = 1 - part
                act.wait_ge(ld_s[i], landed(pas, j))
                if guard and part:
                    act.wait_ge(upv, 2 * (pas * NF + j - 1))
                A.copy(uh[b][:, part].rearrange("p k n -> p (k n)"), slot[i][:]).then_inc(uhi, 1)

        def down_high(pas, j, b, guard):
            act.wait_ge(ld_s[2], landed(pas, j))
            if guard:
                act.wait_ge(dmm, NO * (pas * NF + j))
            A.copy(dh[b][:], slot[2][:]).then_inc(dhi, 1)

        def hidden(pas, j, b, guard):
            J = pas * NF + j
            for t in range(2):
                act.wait_ge(upg, 2 * J + t + 1)
                if t == 0 and guard:
                    act.wait_ge(cvd, 2 * J)
                    act.wait_ge(hal, J)
                A.copy(gs[:, 2 + t * 512:2 + (t + 1) * 512], ps[t][:]).then_inc(gev, 1)
            for t in range(2):
                act.wait_ge(cvd, 2 * J + t + 1)
                A.activation(cv[t][:], cv[t][:], ACT.Silu, bias=cj[b][:, 3:4]).then_inc(sil, 1)
            for t in range(2):
                act.wait_ge(prod, 2 * J + t + 1)
                A.copy(ah[b][:, t * 512:(t + 1) * 512], full[t][:]).then_inc(vhi, 1)

        def tail_squares(pas, g):
            for t in range(4 * g, 4 * g + 4):
                n = pas * NT + t
                act.wait_ge(t1[t % 2], n // 2 + 1)
                if n:
                    act.wait_ge(sq2, n)
                A.activation(gs[:, 0:D], acc[:, t], ACT.Square, accum_out=st[:, 0, t:t + 1]).then_inc(sq2, 1)

        def tail_root(pas, g):
            act.wait_ge(root_in, R2 + 2 * pas + g + 1)
            A.activation(st[:, 1, 4 * g:4 * g + 4], st[:, 3, 4 * g:4 * g + 4], ACT.Sqrt).then_inc(root, 1)

        def tail(pas, g):
            tail_squares(pas, g)
            tail_root(pas, g)

        def h_high(pas, ks):
            for k in ks:
                act.wait_ge(ld_h[k // 2], 16 * (pas + 1))
                A.copy(h2h[:, k], h2l[:, k].bitcast(F32)).then_inc(h2hi, 1)

        split(0)
        for n in range(NM):
            if n + 1 < NM:
                split(n + 1)
            else:
                act.wait_ge(mlo, 2 * NM)
                h_high(0, range(KD))
            stats(n)
            if n:
                transposed(n - 1)
            if n == NM // 2:
                up_high(0, 0, 0, False)
        for pas in range(NP):
            if pas:
                up_high(pas, 0, 0, True)
                h_high(pas, range(KD))
                tail(pas - 1, 0)
            else:
                act.wait_ge(om, 2 * NM)
                for i in range(2):
                    act.wait_ge(x_st[i], 16 * NM // 2)
            up_high(pas, 1, 1, pas > 0)
            hidden(pas, 0, 0, pas > 0)
            if pas == 0:
                transposed(NM - 1)
            if pas:
                tail(pas - 1, 1)
            down_high(pas, 0, 0, pas > 0)
            with act.Fori(1, NF // 2) as it:
                up_high(pas, 2 * it, 0, True)
                hidden(pas, 2 * it - 1, 1, True)
                down_high(pas, 2 * it - 1, 1, True)
                up_high(pas, 2 * it + 1, 1, True)
                hidden(pas, 2 * it, 0, True)
                down_high(pas, 2 * it, 0, True)
            hidden(pas, NF - 1, 1, True)
            down_high(pas, NF - 1, 1, True)
        for step in (tail_squares, tail_root):
            step(NP - 1, 0)
            step(NP - 1, 1)

    @block.gpsimd
    def _(pool):
        ch = S.chain_g.on(pool)
        for n in range(NM):
            for part, src in ((0, S.yt[:, :, n * P:(n + 1) * P]), (1, S.pt[:, :, HALO + n * P:HALO + (n + 1) * P])):
                c = slice(4 * part, 4 * part + 4)
                pool.wait_ge(mhi, 2 * n + part + 1)
                Q.tensor_tensor(ml[n % 2][:, c], src, mh[n % 2][:, c].bitcast(F32), ALU.subtract).then_inc(mlo, 1)

        def up_low(pas, j, b):
            for part in (1, 0):
                pool.wait_ge(uhi, 2 * (pas * NF + j) + (1 if part else 2))
                Q.tensor_tensor(ul[b][:, part].rearrange("p k n -> p (k n)"), slot[1 - part][:],
                                uh[b][:, part].rearrange("p k n -> p (k n)").bitcast(F32), ALU.subtract).then_inc(ulo, 1)

        def down_low(pas, j, b):
            pool.wait_ge(dhi, pas * NF + j + 1)
            Q.tensor_tensor(dl[b][:], slot[2][:], dh[b][:].bitcast(F32), ALU.subtract).then_inc(dlo, 1)

        def tail(pas, g):
            for t in range(4 * g + 1, 4 * g + 4, 2):
                pool.wait_ge(dad, NO * (pas + 1) * NF - NO + 2 * t + 2)
                ch.link(Q.tensor_tensor(acc[:, t], acc[:, t], gt[:], ALU.mult))
                Q.tensor_tensor(acc[:, t], acc[:, t], residual_of(pool, pas, t), ALU.add).then_inc(t1[1], 1)

        for pas in range(NP):
            up_low(pas, 0, 0)
            for k in range(KP[pas]):
                pool.wait_ge(h2hi, pas * KD + k + 1)
                Q.tensor_tensor(h2l[:, k], h2l[:, k].bitcast(F32), h2h[:, k].bitcast(F32), ALU.subtract).then_inc(h2lo, 1)
            if pas == 1:
                pool.wait_ge(ld_g, 32)
            if pas:
                tail(pas - 1, 0)
            up_low(pas, 1, 1)
            if pas:
                tail(pas - 1, 1)
            down_low(pas, 0, 0)
            with pool.Fori(1, NF // 2) as it:
                up_low(pas, 2 * it, 0)
                down_low(pas, 2 * it - 1, 1)
                up_low(pas, 2 * it + 1, 1)
                down_low(pas, 2 * it, 0)
            down_low(pas, NF - 1, 1)
        tail(NP - 1, 0)
        tail(NP - 1, 1)

    @block.vector
    def _(dve):
        ch = S.chain_v.on(dve)
        dve.wait_ge(cwt, 1)
        V.tensor_copy(cw[:].rearrange("p i j -> p (i j)"), ps[6][:, 0:4 * NF]).then_inc(cw_ok, 1)
        V.memset(halo[:], 0.0)
        dve.wait_ge(ld_b, 16)

        def residual(n):
            dve.wait_ge(ld_x[n % 2], 16 * (n // 2 + 1))
            for r in range(2):
                i = 2 * n + r
                rs = slice(r * 512, (r + 1) * 512)
                dve.wait_ge(om, i + 1)
                V.tensor_tensor(xg[:, rs], ps[i % 4][:], gb[:, rs], ALU.mult).then_inc(xg_r, 1)
                dve.wait_ge(xg_r, i + 1)
                V.tensor_tensor(xt[n % 2][:, rs], xg[:, rs], xt[n % 2][:, rs], ALU.add).then_inc(x1r, 1)

        def normalise(n):
            dve.wait_ge(sq, n + 1)

            def root_step(out, r):
                V.tensor_copy(st[:, 3, n:n + 1], r).then_inc(root_in, 1)
                dve.wait_ge(root, R1 + n + 1)

            c = [st[:, i, n:n + 1] for i in range(5)]
            rstd_steps(nc, ch.link, c[1], c[0], (c[2], c[4]), root_step)
            if n:
                dve.wait_ge(tr, n)
            V.tensor_scalar(xn[:], xt[n % 2][:], c[1], None, ALU.mult).then_inc(xnr, 1)

        def transposed(n):
            dve.wait_ge(tr, n + 1)
            if n:
                dve.wait_ge(h_st, 16 * n)
            for k in range(4, KD):
                last = V.tensor_scalar(ht[:, k], ps[7][:, (k - 4) * P:(k - 3) * P], S.a2[:, k:k + 1], S.b2[:, k:k + 1], ALU.mult, ALU.add)
            last.then_inc(htb, 1)

        def h_low(pas):
            for k in range(KP[pas], KD):
                dve.wait_ge(h2hi, pas * KD + k + 1)
                V.tensor_tensor(h2l[:, k], h2l[:, k].bitcast(F32), h2h[:, k].bitcast(F32), ALU.subtract).then_inc(h2lo_d, 1)

        for n in range(NM):
            residual(n)
            if n:
                transposed(n - 1)
            normalise(n)

        def adds(pas, j, first=False):
            for i in range(NO):
                t, r = divmod(i, 2)
                dve.wait_ge(dmm, NO * (pas * NF + j) + i + 1)
                c = acc[:, t, r * 512:(r + 1) * 512]
                if first:
                    V.tensor_copy(c, ps[4 + i % 4][:]).then_inc(dad, 1)
                else:
                    V.tensor_tensor(c, ps[4 + i % 4][:], c, ALU.add).then_inc(dad, 1)

        def conv(pas, j, b):
            J = pas * NF + j
            V.tensor_copy(cj[b][:].unsqueeze(2), cw[:, :, bass.ds(j, 1)])
            V.tensor_copy(gs[:, 0:2], halo[:, bass.ds(j, 1), :]).then_inc(chn, 1)
            dve.wait_ge(chn, 5 * J + 1)
            for t in range(2):
                o = t * 512
                dve.wait_ge(gev, 2 * J + t + 1)
                V.tensor_scalar(cv[t][:], gs[:, o:o + 512], cj[b][:, 0:1], None, ALU.mult).then_inc(chn, 1)
                dve.wait_ge(chn, 5 * J + 2 + 2 * t)
                V.scalar_tensor_tensor(cv[t][:], gs[:, o + 1:o + 513], cj[b][:, 1:2], cv[t][:], ALU.mult, ALU.add).then_inc(chn, 1)
                dve.wait_ge(chn, 5 * J + 3 + 2 * t)
                V.scalar_tensor_tensor(cv[t][:], gs[:, o + 2:o + 514], cj[b][:, 2:3], cv[t][:], ALU.mult, ALU.add).then_inc(cvd, 1)
            V.tensor_copy(halo[:, bass.ds(j, 1), :], gs[:, TF:TF + 2]).then_inc(hal, 1)

        def gate(pas, j, b):
            J = pas * NF + j
            for t in range(2):
                dve.wait_ge(sil, 2 * J + t + 1)
                dve.wait_ge(upv, 2 * J + t + 1)
                V.tensor_tensor(full[t][:], ps[2 + t][:], cv[t][:], ALU.mult).then_inc(prod, 1)
            for t in range(2):
                ts = slice(t * 512, (t + 1) * 512)
                dve.wait_ge(vhi, 2 * J + t + 1)
                V.tensor_tensor(al[b][:, ts], full[t][:], ah[b][:, ts].bitcast(F32), ALU.subtract).then_inc(vlo, 1)

        def hidden(pas, j, b):
            conv(pas, j, b)
            gate(pas, j, b)

        def tail_residual(pas, g):
            for t in range(4 * g, 4 * g + 4, 2):
                if t == 0 and pas == 0:
                    dve.wait_ge(ld_g, 32)
                ch.link(V.tensor_tensor(acc[:, t], acc[:, t], gt[:], ALU.mult))
                V.tensor_tensor(acc[:, t], acc[:, t], residual_of(dve, pas, t), ALU.add).then_inc(t1[0], 1)

        def tail_norm(pas, g):
            dve.wait_ge(sq2, pas * NT + 4 * g + 4)

            def root_step(out, r):
                V.tensor_copy(st[:, 3, 4 * g:4 * g + 4], r).then_inc(root_in, 1)
                dve.wait_ge(root, R2 + 2 * pas + g + 1)

            c = [st[:, i, 4 * g:4 * g + 4] for i in range(5)]
            rstd_steps(nc, ch.link, c[1], c[0], (c[2], c[4]), root_step)
            for t in range(4 * g, 4 * g + 4):
                V.scalar_tensor_tensor(acc[:, t], acc[:, t], st[:, 1, t:t + 1], gf[:], ALU.mult, ALU.mult).then_inc(oo_r, 1)

        def tail(pas, g):
            tail_residual(pas, g)
            tail_norm(pas, g)

        for pas in range(NP):
            h_low(pas)
            if pas:
                tail(pas - 1, 0)
            else:
                dve.wait_ge(x_st[0], 16 * NM // 2)
                dve.wait_ge(x_st[1], 16 * NM // 2)
            hidden(pas, 0, 0)
            if pas == 0:
                transposed(NM - 1)
            if pas:
                tail(pas - 1, 1)
                dve.wait_ge(o_st, 16 * NT * pas)
            adds(pas, 0, True)
            hidden(pas, 1, 1)
            with dve.Fori(1, NF // 2 - 1) as it:
                adds(pas, 2 * it - 1)
                hidden(pas, 2 * it, 0)
                adds(pas, 2 * it)
                hidden(pas, 2 * it + 1, 1)
            adds(pas, NF - 3)
            hidden(pas, NF - 2, 0)
            hidden(pas, NF - 1, 1)
            adds(pas, NF - 2)
            adds(pas, NF - 1)
        for step in (tail_residual, tail_norm):
            step(NP - 1, 0)
            step(NP - 1, 1)

    @block.tensor
    def _(pe):
        def project_out(n):
            pe.wait_ge(mlo, 2 * (n + 1))
            for r in range(2):
                i = 2 * n + r
                if i >= 4:
                    pe.wait_ge(xg_r, i - 3)
                rs = slice(r * 512, (r + 1) * 512)
                for k in range(KM):
                    last = three(nc, ps[i % 4][:], mh[n % 2][:, k], ml[n % 2][:, k], S.oh[:, k, rs], S.ol[:, k, rs], k == 0, k == KM - 1)
                last.then_inc(om, 1)

        def flip(n):
            pe.wait_ge(xnr, n + 1)
            if n:
                pe.wait_ge(hta, n)
                pe.wait_ge(htb, n)
            for k in range(KD):
                last = T.transpose(ps[6 + k // 4][:, k % 4 * P:(k % 4 + 1) * P], xn[:, bass.ds(k, P, step=KD)], S.ident[:])
            last.then_inc(tr, 1)

        for n in range(NM):
            project_out(n)
            if n == 0:
                pe.wait_ge(ld_cw, 64)
                T.transpose(ps[6][:, 0:4 * NF], crow[:], S.ident[0:4 * NF, 0:4 * NF]).then_inc(cwt, 1)
                pe.wait_ge(cw_ok, 1)
            if n:
                flip(n - 1)

        def up(pas, j, b, first):
            J = pas * NF + j
            for part, out, done, free in ((1, 0, upg, gev), (0, 2, upv, prod)):
                pe.wait_ge(ulo, 2 * J + (1 if part else 2))
                for t in range(2):
                    if not first:
                        pe.wait_ge(free, 2 * J - 1 + t)
                    elif t == 0:
                        pe.wait_ge(xg_r, 2 * NM - (2 if part else 0))
                    ts = slice(t * 512, (t + 1) * 512)
                    for k in range(KD):
                        if isinstance(j, int) and j == 0 and part == 1 and t == 0:
                            if k < KP[pas]:
                                pe.wait_ge(h2lo, sum(KP[:pas]) + k + 1)
                            else:
                                pe.wait_ge(h2lo_d, pas * KD - sum(KP[:pas + 1]) + k + 1)
                        last = three(nc, ps[out + t][:], uh[b][:, part, k, :], ul[b][:, part, k, :],
                                     h2h[:, k, ts], h2l[:, k, ts], k == 0, k == KD - 1)
                    last.then_inc(done, 1)

        def down(pas, j, b, first):
            J = pas * NF + j
            pe.wait_ge(vlo, 2 * J + 2)
            pe.wait_ge(dlo, J + 1)
            for i in range(NO):
                t, r = divmod(i, 2)
                if not (first and i < 4):
                    pe.wait_ge(dad, NO * J + i - 3)
                ts, rs = slice(t * P, (t + 1) * P), slice(r * 512, (r + 1) * 512)
                three(nc, ps[4 + i % 4][:], ah[b][:, ts], al[b][:, ts], dh[b][:, rs], dl[b][:, rs], True, True).then_inc(dmm, 1)

        for pas in range(NP):
            up(pas, 0, 0, pas == 0)
            if pas == 0:
                flip(NM - 1)
            up(pas, 1, 1, False)
            if pas == 0:
                pe.wait_ge(hta, NM)
                pe.wait_ge(htb, NM)
            down(pas, 0, 0, pas == 0)
            with pe.Fori(1, NF // 2) as it:
                up(pas, 2 * it, 0, False)
                down(pas, 2 * it - 1, 1, False)
                up(pas, 2 * it + 1, 1, False)
                down(pas, 2 * it, 0, False)
            down(pas, NF - 1, 1, False)

    ctx.close()


class Shared:
    pass


def build(nc, I):
    S = Shared()
    base = (nc.sbuf_base + 63) // 64 * 64
    nc.alloc_sbuf_tensor("slab", [P, (SBUF_BYTES + 64) // 4], F32)
    S.map = Place(nc, base)
    ctx = ExitStack()
    S.sem = lambda name: ctx.enter_context(nc.semaphore(name))
    S.ps = [nc.alloc_psum_tensor(f"bank{i}", [P, 512], F32) for i in range(8)]
    at = S.map.at
    S.ident = at("ident", 0, [P, P])
    S.swap = at("swap", 0.5, [P, P])
    S.ones = at("ones", 1, [P, P])
    S.a1, S.b1, S.a2, S.b2 = (at(n, 1.5 + 0.0625 * i, [P, KD]) for i, n in enumerate(("a1", "b1", "a2", "b2")))
    S.rad8 = at("rad8", 2, [P, G])
    S.csl, S.g_ffn = at("c_silu", 2.25, [P, KD]), at("g_ffn", 2.3125, [P, KD])
    S.pt = at("pt", 3, [P, 4, HALO + SEQ])
    S.yt = at("yt", 35.25, [P, 4, SEQ])
    def dram(name, shape):
        return nc.dram_tensor(name, list(shape), F32).ap()

    S.u = dram("u_scratch", (SEQ, SSM_W))
    S.x1 = dram("x1_scratch", (SEQ, D))
    S.kpad = dram("kpad", (G, H, 240))
    S.mats = dram("mats", (P, 2, G * P))
    S.gates = dram("gates", (2, D))
    S.h2 = dram("h2_scratch", (P, KD, SEQ))
    S.raw_glu = [at(f"raw_glu{i}", o, [P, D]) for i, o in enumerate((87, 91, 103, 107))]
    S.ld_glu = [S.sem(f"ld_glu{i}") for i in range(4)]
    assert SSM_W == 4 * P
    S.col, S.ld_col = at("m_col", 206.5, [P, 16]), S.sem("ld_col")
    S.chain_v, S.chain_g = Chain(S.sem("chain_v")), Chain(S.sem("chain_g"))
    S.sn, S.cs = (at(n, 83.25 + 1.75 * i, [P, NM, G]) for i, n in enumerate(("sn", "cs")))
    S.ec, S.es = (at(n, 119 + 16 * i, [P, G, NCH]) for i, n in enumerate(("s_cos", "s_sin")))
    S.xb = [at(f"a_x{i}", 35.25 + 8 * i, [P, TA // P, D]) for i in range(2)]
    S.wraw = [at(f"a_wraw{i}", o, [P, D]) for i, o in enumerate((51.25, 55.25, 67.25, 71.25))]
    S.st = at("a_stat", 86.75, [P, 5, TA // P])
    S.sq, S.root_in, S.root, S.xn = (S.sem("a_" + n) for n in ("sq", "root_in", "root", "xn"))
    S.ld_x, S.ld_w = [S.sem("a_ld_x0"), S.sem("a_ld_x1")], [S.sem(f"a_ld_w{i}") for i in range(4)]
    S.mats_st, S.kpad_st = S.sem("mats_stored"), S.sem("kpad_stored")
    S.w_in = I["w_in"][0].rearrange("(p k) n -> p k n", k=KD)
    S.x_v = I["x"][0].rearrange("(b j p) d -> b p j d", p=P, j=TA // P)
    prepare(nc, S, I)
    project(nc, S, I)
    scan(nc, S, I)
    mix(nc, S, I)
    ffn(nc, S, I)
    ctx.close()


_INS = ["x", "c", "w_ada", "b_ada", "g_norm_mix", "w_in", "ssm_lam_re", "ssm_lam_im", "ssm_log_dt", "ssm_b_re",
        "ssm_b_im", "ssm_c_re", "ssm_c_im", "ssm_d", "w_glu", "b_glu", "w_pool", "b_pool", "pool_scale", "w_out",
        "g_norm_ffn", "w_up", "w_conv", "b_conv", "w_down", "g_norm_final"]


def kernel(**inputs):
    import numpy as _np
    import concourse.bacc as _bacc
    from concourse import mybir as _mybir
    from concourse.bass_utils import run_bass_kernel_spmd as _run

    nc = _bacc.Bacc("TRN2", target_bir_lowering=False, num_devices=1)
    arrays, handles = {}, {}
    for name in _INS:
        a = _np.ascontiguousarray(inputs[name])
        arrays[f"in_{name}"] = a
        handles[name] = nc.dram_tensor(f"in_{name}", a.shape, _mybir.dt.from_np(a.dtype), kind="ExternalInput").ap()
    handles["out"] = nc.dram_tensor("out_0", (1, SEQ, D), _mybir.dt.float32, kind="ExternalOutput").ap()
    build(nc, handles)
    r = _run(nc, [arrays], core_ids=[0])
    return r.results[0]["out_0"]
```
